# Optimizing a Trainium2 kernel written in Bass

```python
import jax, jax.numpy as jnp
from jax import lax
import numpy as np

D_MODEL = 1024
BATCH = 1
SEQ = 512
DEPTH = 1

N_META = 16
HEAD_DIM = 64
FOX_HEADS = 8
FOX_WIDTH = FOX_HEADS * HEAD_DIM
RWKV_HEADS = 8
RWKV_WIDTH = RWKV_HEADS * HEAD_DIM
DECAY_LORA = 64
AAA_LORA = 64
GATE_LORA = 160
ATTN_BLOCK = 128
PEER_HEADS = 8
PEER_QDIM = 256
N_KEYS = 128
N_EXPERTS = N_KEYS * N_KEYS
PEER_TOPK = 16
PEER_CHUNK = 128
NORM_EPS = 1e-6
RWKV_GN_EPS = 64e-5
MASK_VALUE = -1e30

FOX_COLS = 3 * FOX_WIDTH + FOX_HEADS
RWKV_COLS = 3 * RWKV_WIDTH + DECAY_LORA + AAA_LORA + GATE_LORA
GATE_COLS = 2 * D_MODEL
IN_COLS = FOX_COLS + RWKV_COLS + GATE_COLS

kernel_name = 'fox_rwkv7_peer_hybrid_block'

def _split(z, sizes):
    idx = np.cumsum(sizes)[:-1].tolist()
    return jnp.split(z, idx, axis=-1)

def rmsnorm(x, g):
    xf = x.astype(jnp.float32)
    y = xf * lax.rsqrt(jnp.mean(xf * xf, axis=-1, keepdims=True) + NORM_EPS)
    return (y * g.astype(jnp.float32)).astype(x.dtype)

def fox_attention(q, k, v, log_f):
    B, T, H, Dh = q.shape
    pad = (-T) % ATTN_BLOCK
    L = T + pad
    nb = L // ATTN_BLOCK
    pad4 = ((0, 0), (pad, 0), (0, 0), (0, 0))
    qp = jnp.pad(q, pad4)
    k32 = jnp.pad(k, pad4).astype(jnp.float32)
    vp = jnp.pad(v, pad4)
    c = jnp.cumsum(jnp.pad(log_f, ((0, 0), (pad, 0), (0, 0))), axis=1)
    c_k = jnp.transpose(c, (0, 2, 1))
    kpos = jnp.arange(L)
    k_valid = kpos >= pad
    q_blocks = jnp.moveaxis(qp.reshape(B, nb, ATTN_BLOCK, H, Dh), 1, 0)
    c_blocks = jnp.moveaxis(c.reshape(B, nb, ATTN_BLOCK, H), 1, 0)
    scale = Dh ** -0.5

    def one_block(args):
        i, q_i, c_i = args
        s = jnp.einsum('bqhd,bkhd->bhqk', q_i.astype(jnp.float32), k32) * scale
        s = s + jnp.transpose(c_i, (0, 2, 1))[..., :, None] - c_k[:, :, None, :]
        qpos = i * ATTN_BLOCK + jnp.arange(ATTN_BLOCK)
        mask = (kpos[None, :] <= qpos[:, None]) & k_valid[None, :]
        p = jax.nn.softmax(jnp.where(mask, s, MASK_VALUE), axis=-1)
        return jnp.einsum('bhqk,bkhd->bqhd', p.astype(vp.dtype), vp)

    o = lax.map(one_block, (jnp.arange(nb), q_blocks, c_blocks))
    o = jnp.moveaxis(o, 0, 1).reshape(B, L, H, Dh)
    return o[:, pad:]

def rwkv7_time_mix(z, mu, w0, w_up, a0, a_up, g_up, k_k, k_a, r_k, ln_g, ln_b):
    B, T, _ = z.shape
    f32 = jnp.float32
    z_prev = jnp.pad(z, ((0, 0), (1, 0), (0, 0)))[:, :-1]
    z = z + mu * (z_prev - z)
    r, k, v, wd, ad, gd = _split(z, [RWKV_WIDTH] * 3 + [DECAY_LORA, AAA_LORA, GATE_LORA])
    w = -jax.nn.softplus(-(w0 + jnp.tanh(wd) @ w_up)) - 0.5
    decay = jnp.exp(-jnp.exp(w.astype(f32)))
    a = jax.nn.sigmoid(a0 + ad @ a_up)
    g = jax.nn.sigmoid(gd) @ g_up
    kk = k * k_k
    k = k * (1.0 + (a - 1.0) * k_a)

    def heads(t):
        return t.reshape(B, T, RWKV_HEADS, HEAD_DIM).astype(f32)

    r, k, v, decay, a, kk = (heads(t) for t in (r, k, v, decay, a, kk))
    kk = kk / jnp.maximum(jnp.sqrt(jnp.sum(kk * kk, axis=-1, keepdims=True)), 1e-12)

    def step(S, inp):
        r_t, w_t, k_t, v_t, kk_t, a_t = inp
        sa = jnp.einsum('bhvk,bhk->bhv', S, -kk_t)
        S = (S * w_t[:, :, None, :] + sa[..., None] * (kk_t * a_t)[:, :, None, :]
             + v_t[..., None] * k_t[:, :, None, :])
        return S, jnp.einsum('bhvk,bhk->bhv', S, r_t)

    xs = tuple(jnp.moveaxis(t, 1, 0) for t in (r, decay, k, v, kk, a))
    S0 = jnp.zeros((B, RWKV_HEADS, HEAD_DIM, HEAD_DIM), f32)
    _, y = lax.scan(step, S0, xs)
    y = jnp.moveaxis(y, 0, 1)
    mean = jnp.mean(y, axis=-1, keepdims=True)
    var = jnp.mean(jnp.square(y - mean), axis=-1, keepdims=True)
    y = (y - mean) * lax.rsqrt(var + RWKV_GN_EPS)
    y = y.reshape(B, T, RWKV_WIDTH) * ln_g + ln_b
    bonus = (jnp.sum(r * k * r_k, axis=-1, keepdims=True) * v).reshape(B, T, RWKV_WIDTH)
    return ((y + bonus) * g).astype(z.dtype)

def peer_ffn(xn, w_q, sub_k1, sub_k2, u, v):
    B, T, D = xn.shape
    xc = xn.reshape(-1, PEER_CHUNK, D)
    half = PEER_QDIM // 2

    def one_chunk(x_c):
        q = (x_c @ w_q).reshape(PEER_CHUNK, PEER_HEADS, PEER_QDIM)
        s1 = jnp.einsum('chd,nd->chn', q[..., :half], sub_k1).astype(jnp.float32)
        s2 = jnp.einsum('chd,nd->chn', q[..., half:], sub_k2).astype(jnp.float32)
        t1, i1 = lax.top_k(s1, PEER_TOPK)
        t2, i2 = lax.top_k(s2, PEER_TOPK)
        cand_s = (t1[..., :, None] + t2[..., None, :]).reshape(PEER_CHUNK, PEER_HEADS, PEER_TOPK ** 2)
        cand_i = (i1[..., :, None] * N_KEYS + i2[..., None, :]).reshape(PEER_CHUNK, PEER_HEADS, PEER_TOPK ** 2)
        top_s, pos = lax.top_k(cand_s, PEER_TOPK)
        ids = jnp.take_along_axis(cand_i, pos, axis=-1)
        gate = jax.nn.softmax(top_s, axis=-1)
        hid = jax.nn.gelu(jnp.einsum('chkd,cd->chk', u[ids], x_c).astype(jnp.float32), approximate=False)
        return jnp.einsum('chk,chkd->cd', (gate * hid).astype(v.dtype), v[ids])

    return lax.map(one_chunk, xc).reshape(B, T, D)

def setup_inputs(seed: int = 0) -> dict:
    key = jax.random.key(seed)
    ks = iter(jax.random.split(key, 32))
    L = DEPTH

    def nrm(shape, scale):
        return scale * jax.random.normal(next(ks), shape, jnp.float32)

    def uni(shape, lo, hi):
        return jax.random.uniform(next(ks), shape, jnp.float32, lo, hi)

    return {
        'x': nrm((BATCH, SEQ, D_MODEL), 1.0),
        'meta_tokens': nrm((N_META, D_MODEL), 1.0),
        'norm1_g': 1.0 + nrm((L, D_MODEL), 0.02),
        'w_in': nrm((L, D_MODEL, IN_COLS), D_MODEL ** -0.5),
        'fox_q_norm': 1.0 + nrm((L, FOX_HEADS, HEAD_DIM), 0.02),
        'fox_k_norm': 1.0 + nrm((L, FOX_HEADS, HEAD_DIM), 0.02),
        'fox_f_bias': 4.0 + nrm((L, FOX_HEADS), 0.5),
        'rwkv_mu': uni((L, RWKV_COLS), 0.0, 1.0),
        'rwkv_w0': uni((L, RWKV_WIDTH), -6.0, -1.0),
        'rwkv_w_up': nrm((L, DECAY_LORA, RWKV_WIDTH), 0.1),
        'rwkv_a0': nrm((L, RWKV_WIDTH), 0.1),
        'rwkv_a_up': nrm((L, AAA_LORA, RWKV_WIDTH), 0.5 * AAA_LORA ** -0.5),
        'rwkv_g_up': nrm((L, GATE_LORA, RWKV_WIDTH), GATE_LORA ** -0.5),
        'rwkv_k_k': 0.85 + nrm((L, RWKV_WIDTH), 0.05),
        'rwkv_k_a': 1.0 + nrm((L, RWKV_WIDTH), 0.05),
        'rwkv_r_k': nrm((L, RWKV_HEADS, HEAD_DIM), 0.1),
        'rwkv_ln_g': 1.0 + nrm((L, RWKV_WIDTH), 0.02),
        'rwkv_ln_b': nrm((L, RWKV_WIDTH), 0.02),
        'w_branch_fox': nrm((L, FOX_WIDTH, D_MODEL), FOX_WIDTH ** -0.5),
        'w_branch_rwkv': nrm((L, RWKV_WIDTH, D_MODEL), RWKV_WIDTH ** -0.5),
        'w_out': nrm((L, D_MODEL, D_MODEL), D_MODEL ** -0.5),
        'norm2_g': 1.0 + nrm((L, D_MODEL), 0.02),
        'peer_w_q': nrm((L, D_MODEL, PEER_HEADS * PEER_QDIM), D_MODEL ** -0.5),
        'peer_sub_k1': nrm((L, N_KEYS, PEER_QDIM // 2), (PEER_QDIM // 2) ** -0.5),
        'peer_sub_k2': nrm((L, N_KEYS, PEER_QDIM // 2), (PEER_QDIM // 2) ** -0.5),
        'peer_u': nrm((L, N_EXPERTS, D_MODEL), D_MODEL ** -0.5),
        'peer_v': nrm((L, N_EXPERTS, D_MODEL), 0.5),
    }

def reference(x, meta_tokens, norm1_g, w_in, fox_q_norm, fox_k_norm, fox_f_bias,
              rwkv_mu, rwkv_w0, rwkv_w_up, rwkv_a0, rwkv_a_up, rwkv_g_up, rwkv_k_k,
              rwkv_k_a, rwkv_r_k, rwkv_ln_g, rwkv_ln_b, w_branch_fox, w_branch_rwkv,
              w_out, norm2_g, peer_w_q, peer_sub_k1, peer_sub_k2, peer_u, peer_v):
    B = x.shape[0]
    meta = jnp.broadcast_to(meta_tokens[None].astype(x.dtype), (B, N_META, D_MODEL))
    h = jnp.concatenate([meta, x], axis=1)
    for l in range(DEPTH):
        T = h.shape[1]
        xn = rmsnorm(h, norm1_g[l])
        z = xn @ w_in[l]
        z_fox, z_rwkv, z_gate = _split(z, [FOX_COLS, RWKV_COLS, GATE_COLS])
        fq, fk, fv, f_logit = _split(z_fox, [FOX_WIDTH] * 3 + [FOX_HEADS])
        fq = rmsnorm(fq.reshape(B, T, FOX_HEADS, HEAD_DIM), fox_q_norm[l])
        fk = rmsnorm(fk.reshape(B, T, FOX_HEADS, HEAD_DIM), fox_k_norm[l])
        fv = fv.reshape(B, T, FOX_HEADS, HEAD_DIM)
        log_f = jax.nn.log_sigmoid((f_logit + fox_f_bias[l]).astype(jnp.float32))
        y_fox = fox_attention(fq, fk, fv, log_f).reshape(B, T, FOX_WIDTH)
        y_rwkv = rwkv7_time_mix(z_rwkv, rwkv_mu[l], rwkv_w0[l], rwkv_w_up[l], rwkv_a0[l],
                                rwkv_a_up[l], rwkv_g_up[l], rwkv_k_k[l], rwkv_k_a[l],
                                rwkv_r_k[l], rwkv_ln_g[l], rwkv_ln_b[l])
        gate_fox, gate_rwkv = jnp.split(jax.nn.sigmoid(z_gate), 2, axis=-1)
        mixed = gate_fox * (y_fox @ w_branch_fox[l]) + gate_rwkv * (y_rwkv @ w_branch_rwkv[l])
        h = h + mixed @ w_out[l]
        if l == DEPTH - 1:
            h = h[:, N_META:]
        h = h + peer_ffn(rmsnorm(h, norm2_g[l]), peer_w_q[l], peer_sub_k1[l],
                         peer_sub_k2[l], peer_u[l], peer_v[l])
    return h


_drawn_inputs = setup_inputs


def setup_inputs(seed=0):
    import zlib

    import numpy as np

    out = dict(_drawn_inputs(seed))
    spreads = {}
    factors = {'fox_q_norm': 5.257, 'fox_k_norm': 5.183, 'rwkv_ln_g': 2.832, 'rwkv_ln_b': 2.907}
    for name, (base, spread) in spreads.items():
        noise = np.random.default_rng([zlib.crc32(name.encode()), seed]).standard_normal(out[name].shape)
        drawn = base * np.exp(spread * noise) if base else spread * noise
        out[name] = __import__('jax').numpy.asarray(drawn.astype(out[name].dtype))
    for name, factor in factors.items():
        out[name] = (out[name] * factor).astype(out[name].dtype)
    return out
```

```python
from contextlib import ExitStack

import numpy as np

import concourse.bass as bass
from concourse import mybir

F32 = mybir.dt.float32
F32R = mybir.dt.float32r
BF16 = mybir.dt.bfloat16
U32 = mybir.dt.uint32
ALU = mybir.AluOpType
ACT = mybir.ActivationFunctionType
AX = mybir.AxisListType

P = 128
D = 1024
KD = D // P
N_META = 16
SEQ = 512
T = N_META + SEQ
TH = T // 2
HD = 64
NH = 8
W5 = NH * HD
NP4 = W5 // P
NQ = SEQ // P
CONSTS = ("ident", "blockones", "blockmean", "ones")
EPS = 1e-6
GN_EPS = 64e-5
MASKED = -1e30

ZQ, ZK, ZV, ZR, ZRK, ZRV = 0, 4, 8, 12, 16, 20
ZWA, ZGD, ZFG = 24, 25, 26
ZGF, ZGR = 27, 35
NZ = 43
GD2 = 160 - P

(C_QN, C_KN, C_W0, C_A0, C_KK, C_KA, C_RK, C_LG, C_LB) = [4 * i for i in range(9)]
C_MU = 36
C_FB = C_MU + 15
C_G1 = C_FB + 1
C_G2 = C_G1 + KD
NC_COLS = C_G2 + KD

C = 48
NCH = T // C
LEVELS = [2, 4, 8, 16, 32]

PH = 8
NK = 128
TOPK = 16
NCHUNK = 128
GROUP = 2


def matmul3(nc, out, a, b, start, stop):
    nc.tensor.matmul(out, a[0], b[0], start=start, stop=False)
    nc.tensor.matmul(out, a[1], b[0], start=False, stop=False)
    return nc.tensor.matmul(out, a[0], b[1], start=False, stop=stop)


def norm_and_project(nc, d, keep):
    cols, zT = keep["cols"], keep["zT"]
    with ExitStack() as ctx:
        def sb(name, shape, dt=F32):
            return ctx.enter_context(nc.sbuf_tensor(name, shape, dt))

        def sem(name):
            return ctx.enter_context(nc.semaphore(name))

        hT = sb("hT", [P, KD, T])
        sq = sb("sq", [P, KD, T])
        root = sb("root", [P, T])
        rstd = sb("rstd", [P, T])
        xh = sb("xh", [P, KD, T], F32R)
        xl = sb("xl", [P, KD, T], F32R)
        wraw = sb("wraw", [P, 3, KD, P])
        wh = sb("wh", [P, 3, KD, P], F32R)
        wl = sb("wl", [P, 3, KD, P], F32R)
        ps = ctx.enter_context(nc.psum_tensor("ps_z", [P, 6, 512], F32))
        ps_ms = ctx.enter_context(nc.psum_tensor("ps_ms", [P, 2, 512], F32))

        loaded = sem("loaded")
        squared = sem("squared")
        summed = sem("summed")
        rooted = sem("rooted")
        rstd_ready = sem("rstd_ready")
        scaled = sem("scaled")
        x_hi = sem("x_hi")
        x_lo = sem("x_lo")
        w_in = [sem(f"w_arrived{s}") for s in range(3)]
        w_hi = sem("w_hi")
        w_lo = sem("w_lo")
        z_done = sem("z_done")
        evac_a = sem("evac_a")
        evac_b = sem("evac_b")

        def loop(eng, tile):
            for n in range(3):
                tile(n, n % 3)
            with eng.Fori(3, 39, 3) as n0:
                for s in range(3):
                    tile(n0 + s, s)
            for n in range(39, NZ):
                tile(n, n % 3)

        def isn(n, k):
            return not isinstance(n, int) or n >= k

        block = ctx.enter_context(nc.Block())

        @block.sync
        def _(sp):
            sp.dma_start(hT[:], d["hT"]).then_inc(loaded, 16)
            sp.dma_start(cols[:], d["cols"]).then_inc(loaded, 16)
            for name in CONSTS:
                sp.dma_start(keep[name][:], d[name]).then_inc(loaded, 16)

            def tile(n, s):
                if isn(n, 3):
                    sp.wait_ge(w_lo, n - 2)
                sp.dma_start(wraw[:, s], d["w_z"][n]).then_inc(w_in[s], 16)
            loop(sp, tile)

        @block.scalar
        def _(act):
            act.wait_ge(loaded, 32 + 16 * len(CONSTS))
            for k in range(KD):
                nc.scalar.activation(sq[:, k], hT[:, k], ACT.Square).then_inc(squared, 1)
            act.wait_ge(summed, 1)
            nc.scalar.activation(root[:], ps_ms[:, :, 0:TH], ACT.Sqrt, bias=keep["eps"][:, 0:1],
                                 scale=1.0 / D).then_inc(rooted, 1)
            for k in range(KD):
                act.wait_ge(scaled, k + 1)
                nc.scalar.copy(xh[:, k], sq[:, k]).then_inc(x_hi, 1)

            def split(n, s):
                act.wait_ge(w_in[s], (n // 3) * 16 + 16 if isinstance(n, int) else
                            (n - s) * 16 // 3 + 16)
                if isn(n, 3):
                    act.wait_ge(z_done, n - 2)
                nc.scalar.copy(wh[:, s], wraw[:, s]).then_inc(w_hi, 1)

            def evac(n, s):
                act.wait_ge(z_done, n + 1)
                nc.scalar.copy(zT[:, n, 0:TH], ps[:, 2 * s, 0:TH]).then_inc(evac_a, 1)

            split(0, 0)
            split(1, 1)
            evac(0, 0)
            split(2, 2)
            evac(1, 1)
            with act.Fori(3, 39, 3) as n0:
                for s in range(3):
                    split(n0 + s, s)
                    evac(n0 + (s - 1), (s - 1) % 3)
            for n in range(39, NZ):
                split(n, n % 3)
                evac(n - 1, (n - 1) % 3)
            evac(NZ - 1, (NZ - 1) % 3)

        @block.vector
        def _(dve):
            dve.wait_ge(rooted, 1)
            nc.vector.reciprocal(rstd[:], root[:]).then_inc(rstd_ready, 1)
            dve.wait_ge(rstd_ready, 1)
            for k in range(KD):
                nc.vector.scalar_tensor_tensor(out=sq[:, k], in0=hT[:, k], scalar=cols[:, C_G1 + k:C_G1 + k + 1],
                                               in1=rstd[:], op0=ALU.mult, op1=ALU.mult).then_inc(scaled, 1)
            for k in range(KD):
                dve.wait_ge(x_hi, k + 1)
                nc.vector.tensor_tensor(xl[:, k], sq[:, k], xh[:, k].bitcast(F32), ALU.subtract).then_inc(x_lo, 1)

            def split(n, s):
                dve.wait_ge(w_hi, n + 1)
                nc.vector.tensor_tensor(wl[:, s], wraw[:, s], wh[:, s].bitcast(F32), ALU.subtract).then_inc(w_lo, 1)

            def evac(n, s):
                dve.wait_ge(z_done, n + 1)
                nc.vector.tensor_copy(zT[:, n, TH:T], ps[:, 2 * s + 1, 0:TH]).then_inc(evac_b, 1)

            split(0, 0)
            split(1, 1)
            evac(0, 0)
            split(2, 2)
            evac(1, 1)
            with dve.Fori(3, 39, 3) as n0:
                for s in range(3):
                    split(n0 + s, s)
                    evac(n0 + (s - 1), (s - 1) % 3)
            for n in range(39, NZ):
                split(n, n % 3)
                evac(n - 1, (n - 1) % 3)
            evac(NZ - 1, (NZ - 1) % 3)

        @block.tensor
        def _(pe):
            pe.wait_ge(loaded, 32 + 16 * len(CONSTS))
            for k in range(KD):
                pe.wait_ge(squared, k + 1)
                for half in range(2):
                    mm = nc.tensor.matmul(ps_ms[:, half, 0:TH], keep["ones"][:], sq[:, k, half * TH:(half + 1) * TH],
                                          start=(k == 0), stop=(k == KD - 1))
            mm.then_inc(summed, 1)

            def tile(n, s):
                pe.wait_ge(w_lo, n + 1)
                if isn(n, 3):
                    pe.wait_ge(evac_a, n - 2)
                    pe.wait_ge(evac_b, n - 2)
                for k in range(KD):
                    if isinstance(n, int) and n == 0:
                        pe.wait_ge(x_lo, k + 1)
                    for half in range(2):
                        t = slice(half * TH, (half + 1) * TH)
                        mm = matmul3(nc, ps[:, 2 * s + half, 0:TH], (wh[:, s, k], wl[:, s, k]),
                                     (xh[:, k, t], xl[:, k, t]), k == 0, k == KD - 1)
                mm.then_inc(z_done, 1)
            loop(pe, tile)


class Chain:

    def __init__(self, eng, sem, base=0):
        self.eng, self.sem, self.base, self.n = eng, sem, base, 0

    def __call__(self, instruction):
        self.n += 1
        instruction.then_inc(self.sem, 1)
        self.eng.wait_ge(self.sem, self.base + self.n)


def fox_attention(nc, d, keep):
    zT, cols, yfT = keep["zT"], keep["cols"], keep["yfT"]
    UNITS = [(u // NQ, u % NQ) for u in range(2 * NQ)]
    NU = len(UNITS)
    DVE_STEPS = 2 + NU
    keys = [N_META + P * (i + 1) for i in range(NQ)]

    def pieces(a, b):
        return [(a, b)] if b <= 512 or a >= 512 else [(a, 512), (512, b)]

    with ExitStack() as ctx:
        def sb(name, shape, dt=F32):
            return ctx.enter_context(nc.sbuf_tensor(name, shape, dt))

        def sem(name):
            return ctx.enter_context(nc.semaphore(name))

        mask = sb("mask", [P, P])
        selall = sb("selall", [NH, NH, 512])
        sel = sb("sel", [NH, 2, 512])
        fg = sb("fg", [NH, 6, T])
        cum, ncum = fg[:, 4], fg[:, 5]
        sqk = sb("sqk", [P, 2, T])
        rqk = sb("rqk", [P, 2, T])
        qk = sb("qk", [P, 2, T])
        vT = sb("vT", [P, T])
        vtok = sb("vtok", [P, 5, P])
        pr = sb("pr", [P, 2, T])
        ptS = sb("ptS", [P, 2, 5, P])
        mx = sb("mx", [P, 2])
        nmx = sb("nmx", [P, 2])
        rsum = sb("rsum", [P, 2])
        rinv = sb("rinv", [P, 2])
        s_ps = ctx.enter_context(nc.psum_tensor("s_ps", [P, 2, 1024], F32))
        pt_ps = ctx.enter_context(nc.psum_tensor("pt_ps", [P, 1024], F32))
        pv_ps = ctx.enter_context(nc.psum_tensor("pv_ps", [P, 512], F32))

        loaded = sem("f_loaded")
        logit = sem("f_logit")
        softplus = sem("f_softplus")
        steps = sem("f_dve_steps")
        gate_steps = sem("f_gate_steps")
        act_steps = sem("f_act_steps")
        c_ready = sem("f_c_ready")
        squares = sem("f_squares")
        ms_done = sem("f_ms_done")
        roots = sem("f_roots")
        qk_ready = sem("f_qk_ready")
        sel_ready = sem("f_sel_ready")
        v_copied = sem("f_v_copied")
        v_turned = sem("f_v_turned")
        v_ready = sem("f_v_ready")
        scores = sem("f_scores")
        maxed = sem("f_maxed")
        expd = sem("f_expd")
        normed = sem("f_normed")
        turned = sem("f_turned")
        pt_ready = sem("f_pt_ready")
        pv_done = sem("f_pv_done")
        y_out = sem("f_y_out")

        block = ctx.enter_context(nc.Block())

        @block.sync
        def _(sp):
            sp.dma_start(mask[:], d["mask"]).then_inc(loaded, 16)
            sp.dma_start(selall[:], d["sel"]).then_inc(loaded, 16)

        @block.scalar
        def _(act):
            act.wait_ge(logit, 1)
            link = Chain(act, act_steps)
            link(nc.scalar.activation(fg[:, 1], fg[:, 0], ACT.Abs))
            link(nc.scalar.activation(fg[:, 1], fg[:, 1], ACT.Exp, scale=-1.0))
            nc.scalar.activation(fg[:, 2], fg[:, 1], ACT.Ln, bias=1.0).then_inc(softplus, 1)
            act.wait_ge(loaded, 32)
            with act.Fori(0, NP4) as it:
                act.wait_ge(pv_done, it * NU)
                for j, z0 in enumerate((ZQ, ZK)):
                    nc.scalar.activation(sqk[:, j], zT[:, it + z0], ACT.Square).then_inc(squares, 1)
                nc.scalar.copy(vT[:], zT[:, it + ZV]).then_inc(v_copied, 1)
                nc.scalar.copy(sel[:], selall[:, bass.ds(it * 2, 2)]).then_inc(sel_ready, 1)
                act.wait_ge(ms_done, it + 1)
                nc.scalar.activation(rqk[:, 0], s_ps[:, 0].rearrange("p (a b) -> p a b", a=2)[:, :, 0:TH], ACT.Sqrt,
                                     bias=keep["eps"][:, 1:2], scale=1.0).then_inc(roots, 1)
                nc.scalar.activation(rqk[:, 1], s_ps[:, 1].rearrange("p (a b) -> p a b", a=2)[:, :, 0:TH], ACT.Sqrt,
                                     bias=keep["eps"][:, 0:1], scale=1.0 / HD).then_inc(roots, 1)
                act.wait_ge(v_turned, it + 1)
                nc.scalar.copy(vtok[:, 0:4], pt_ps[:, 0:512]).then_inc(v_ready, 1)
                nc.scalar.copy(vtok[0:16, 4], pt_ps[0:16, 512:640]).then_inc(v_ready, 1)

                def exp(u):
                    n, b = keys[UNITS[u][1]], u % 2
                    act.wait_ge(maxed, it * NU + u + 1)
                    if u >= 2:
                        act.wait_ge(turned, it * NU + u - 1)
                        act.wait_ge(normed, it * NU + u - 1)
                    nc.scalar.activation(pr[:, b, 0:n], s_ps[:, b, 0:n], ACT.Exp, bias=nmx[:, b:b + 1],
                                         scale=1.0, accum_out=rsum[:, b:b + 1]).then_inc(expd, 1)

                def pt_out(u):
                    i, b = UNITS[u][1], u % 2
                    act.wait_ge(turned, it * NU + u + 1)
                    if u >= 2:
                        act.wait_ge(pv_done, it * NU + u - 1)
                    nc.scalar.copy(ptS[:, b, 0:i + 1], pt_ps[:, 0:P * (i + 1)]).then_inc(pt_ready, 1)
                    nc.scalar.copy(ptS[0:16, b, i + 1], pt_ps[0:16, 512:640]).then_inc(pt_ready, 1)

                exp(0)
                for u in range(NU):
                    if u + 1 < NU:
                        exp(u + 1)
                    pt_out(u)

        @block.vector
        def _(dve):
            link = Chain(dve, gate_steps)
            nc.vector.tensor_scalar(fg[:, 0], zT[0:NH, ZFG], cols[0:NH, C_FB:C_FB + 1], None,
                                    ALU.add).then_inc(logit, 1)
            dve.wait_ge(logit, 1)
            link(nc.vector.tensor_scalar(fg[:, 3], fg[:, 0], 0.0, None, ALU.min))
            dve.wait_ge(softplus, 1)
            link(nc.vector.tensor_tensor(fg[:, 3], fg[:, 3], fg[:, 2], ALU.subtract))
            link(nc.vector.memset(fg[:, 2], 0.0))
            link(nc.vector.tensor_tensor_scan(cum, fg[:, 3], fg[:, 2], 0.0, ALU.add, ALU.add))
            nc.vector.tensor_scalar(ncum, cum, -1.0, None, ALU.mult).then_inc(c_ready, 1)
            with dve.Fori(0, NP4) as it:
                link = Chain(dve, steps, it * DVE_STEPS)
                dve.wait_ge(roots, it * 2 + 2)
                for j, c0 in enumerate((C_QN, C_KN)):
                    link(nc.vector.reciprocal(rqk[:, j], rqk[:, j]))
                    nc.vector.scalar_tensor_tensor(out=qk[:, j], in0=zT[:, it + 4 * j], scalar=cols[:, bass.ds(it + c0, 1)],
                                                   in1=rqk[:, j], op0=ALU.mult, op1=ALU.mult).then_inc(qk_ready, 1)

                def row_max(u):
                    n, b = keys[UNITS[u][1]], u % 2
                    dve.wait_ge(scores, it * NU + u + 1)
                    nc.vector.reduce_max(nmx[:, b:b + 1], s_ps[:, b, 0:n], AX.X, negate=True).then_inc(maxed, 1)

                def norm(u):
                    n, b = keys[UNITS[u][1]], u % 2
                    dve.wait_ge(expd, it * NU + u + 1)
                    link(nc.vector.reciprocal(rinv[:, b:b + 1], rsum[:, b:b + 1]))
                    nc.vector.tensor_scalar(pr[:, b, 0:n], pr[:, b, 0:n], rinv[:, b:b + 1], None,
                                            ALU.mult).then_inc(normed, 1)

                row_max(0)
                for u in range(NU):
                    if u + 1 < NU:
                        row_max(u + 1)
                    norm(u)
                dve.wait_ge(pv_done, it * NU + NU)
                nc.vector.tensor_copy(yfT[:, it], pv_ps[:]).then_inc(y_out, 1)

        @block.tensor
        def _(pe):
            pe.wait_ge(loaded, 32)
            pe.wait_ge(c_ready, 1)
            with pe.Fori(0, NP4) as it:
                pe.wait_ge(expd, it * NU)
                pe.wait_ge(squares, it * 2 + 2)
                for j in range(2):
                    for half in range(2):
                        mm = nc.tensor.matmul(s_ps[:, j, half * 512:half * 512 + TH], keep["blockones"][:],
                                              sqk[:, j, half * TH:half * TH + TH], start=True, stop=True)
                mm.then_inc(ms_done, 1)
                pe.wait_ge(pt_ready, it * 2 * NU)
                pe.wait_ge(v_copied, it + 1)
                for j in range(4):
                    nc.tensor.transpose(pt_ps[:, j * P:j * P + P], vT[:, j * P:j * P + P], keep["ident"][:])
                nc.tensor.transpose(pt_ps[0:16, 512:640], vT[:, 512:T], keep["ident"][:]).then_inc(v_turned, 1)
                pe.wait_ge(roots, it * 2 + 2)
                pe.wait_ge(sel_ready, it + 1)
                pe.wait_ge(qk_ready, it * 2 + 2)

                def score(u):
                    (e, i), b = UNITS[u], u % 2
                    n, q0, r = keys[i], N_META + P * i, slice(e * HD, e * HD + HD)
                    if u >= 2:
                        pe.wait_ge(expd, it * NU + u - 1)
                    for x, y in pieces(0, n):
                        w = y - x
                        nc.tensor.matmul(s_ps[:, b, x:y], qk[r, 0, q0:q0 + P], qk[r, 1, x:y], start=True, stop=False)
                        x0 = max(x, n - P)
                        if x0 < y:
                            nc.tensor.matmul(s_ps[:, b, x0:y], keep["ident"][:], mask[:, x0 - (n - P):y - (n - P)],
                                             start=False, stop=False)
                        nc.tensor.matmul(s_ps[:, b, x:y], sel[:, e, 0:P], ncum[:, x:y], start=False, stop=False)
                        mm = nc.tensor.matmul(s_ps[:, b, x:y], cum[:, q0:q0 + P], sel[:, e, 0:w], start=False,
                                              stop=True)
                    mm.then_inc(scores, 1)

                def turn(u):
                    i, b = UNITS[u][1], u % 2
                    pe.wait_ge(normed, it * NU + u + 1)
                    pe.wait_ge(pt_ready, it * 2 * NU + 2 * u)
                    for j in range(i + 1):
                        nc.tensor.transpose(pt_ps[:, j * P:j * P + P], pr[:, b, j * P:j * P + P], keep["ident"][:])
                    nc.tensor.transpose(pt_ps[0:16, 512:640], pr[:, b, (i + 1) * P:(i + 1) * P + 16],
                                        keep["ident"][:]).then_inc(turned, 1)

                def values(u):
                    (e, i), b = UNITS[u], u % 2
                    out = pv_ps[e * HD:e * HD + HD, i * P:i * P + P]
                    pe.wait_ge(pt_ready, it * 2 * NU + 2 * u + 2)
                    for j in range(i + 2):
                        k = P if j <= i else 16
                        mm = nc.tensor.matmul(out, vtok[0:k, j, e * HD:e * HD + HD], ptS[0:k, b, j],
                                              start=(j == 0), stop=(j == i + 1))
                    mm.then_inc(pv_done, 1)

                score(0)
                score(1)
                pe.wait_ge(v_ready, it * 2 + 2)
                pe.wait_ge(y_out, it)
                for u in range(NU):
                    turn(u)
                    if u + 2 < NU:
                        score(u + 2)
                    values(u)


def rwkv_inputs(nc, d, keep):
    zT, cols = keep["zT"], keep["cols"]
    L, Lx, kk, ka, bonus, g = (keep[n] for n in ("L", "Lx", "kk", "ka", "bonus", "g"))
    NSH = 15
    with ExitStack() as ctx:
        def sb(name, shape, dt=F32):
            return ctx.enter_context(nc.sbuf_tensor(name, shape, dt))

        def sem(name):
            return ctx.enter_context(nc.semaphore(name))

        diff = sb("diff", [P, NSH, T])
        tanh_w = sb("tanh_w", [HD, T])
        wa_up = sb("wa_up", [P, W5])
        g_up = sb("g_up", [P, 2, W5])
        reset = sb("reset", [P, T])
        a = sb("a_rate", [P, 2, T])
        sq = sb("r_sq", [P, T])
        rk = sb("r_rk", [P, T])
        rn = sb("r_rn", [P, T])
        lora_ps = ctx.enter_context(nc.psum_tensor("lora_ps", [P, 3, 2, 512], F32))
        sum_ps = ctx.enter_context(nc.psum_tensor("sum_ps", [P, 2, 512], F32))

        loaded = sem("r_loaded")
        diffed = sem("r_diffed")
        shifted = sem("r_shifted")
        squashed = sem("r_squashed")
        lora_done = sem("r_lora_done")
        lora_out = sem("r_lora_out")
        kk_raw = sem("r_kk_raw")
        squared = sem("r_squared")
        summed = sem("r_summed")
        rooted = sem("r_rooted")
        rk_ready = sem("r_rk_ready")
        rk_summed = sem("r_rk_summed")
        bonus_out = sem("r_bonus_out")
        steps = sem("r_steps")
        block = ctx.enter_context(nc.Block())

        @block.sync
        def _(sp):
            sp.dma_start(wa_up[:], d["wa_up"]).then_inc(loaded, 16)
            sp.dma_start(g_up[:], d["g_up"]).then_inc(loaded, 16)
            sp.dma_start(reset[:], d["reset"]).then_inc(loaded, 16)

        @block.gpsimd
        def _(pool):
            def shift(i):
                z = zT[:, ZR + i]
                nc.gpsimd.tensor_tensor(diff[:, i, 0:1], keep["eps"][:, 3:4], z[:, 0:1], ALU.subtract).then_inc(diffed, 1)
                nc.gpsimd.tensor_tensor(diff[:, i, 1:T], z[:, 0:T - 1], z[:, 1:T], ALU.subtract).then_inc(diffed, 1)
            for i in range(12, NSH):
                shift(i)
            with pool.Fori(0, 12) as it:
                shift(it)

        @block.vector
        def _(dve):
            def shift(i, n):
                dve.wait_ge(diffed, n * 2 + 2)
                nc.vector.scalar_tensor_tensor(out=zT[:, ZR + i], in0=diff[:, i], scalar=cols[:, bass.ds(i + C_MU, 1)],
                                               in1=zT[:, ZR + i], op0=ALU.mult, op1=ALU.add).then_inc(shifted, 1)
            for i in range(12, NSH):
                shift(i, i - 12)
            with dve.Fori(0, 12) as it:
                shift(it, it + 3)
            link = Chain(dve, steps)
            dve.wait_ge(loaded, 48)
            dve.wait_ge(shifted, NSH)
            for m in range(NP4):
                def col(c):
                    return cols[:, c + m:c + m + 1]
                r, k, v = zT[:, ZR + m], zT[:, ZRK + m], zT[:, ZRV + m]
                nc.vector.tensor_scalar(kk[:, m], k, col(C_KK), None, ALU.mult).then_inc(kk_raw, 1)
                dve.wait_ge(lora_out, 3 * m + 3)
                link(nc.vector.tensor_scalar(Lx[:, m], L[:, m], -float(np.exp(-0.5)), None, ALU.mult))
                link(nc.vector.tensor_tensor_scan(L[:, m], reset[:], Lx[:, m], 0.0, ALU.mult, ALU.add))
                link(nc.vector.tensor_tensor(Lx[:, m], L[:, m], Lx[:, m], ALU.subtract))
                link(nc.vector.tensor_scalar(ka[:, m], a[:, m % 2], 1.0, col(C_KA), ALU.subtract, ALU.mult))
                link(nc.vector.scalar_tensor_tensor(out=k, in0=ka[:, m], scalar=1.0, in1=k, op0=ALU.add, op1=ALU.mult))
                if m >= 1:
                    dve.wait_ge(rk_summed, m)
                nc.vector.scalar_tensor_tensor(out=rk[:], in0=r, scalar=col(C_RK), in1=k, op0=ALU.mult,
                                               op1=ALU.mult).then_inc(rk_ready, 1)
                dve.wait_ge(rooted, m + 1)
                link(nc.vector.tensor_scalar(rn[:], rn[:], 1e-12, None, ALU.max))
                link(nc.vector.reciprocal(rn[:], rn[:]))
                link(nc.vector.tensor_tensor(kk[:, m], kk[:, m], rn[:], ALU.mult))
                link(nc.vector.tensor_tensor(ka[:, m], kk[:, m], a[:, m % 2], ALU.mult))
                dve.wait_ge(rk_summed, m + 1)
                nc.vector.tensor_tensor(bonus[:, m], sum_ps[:, :, 0:TH], v, ALU.mult).then_inc(bonus_out, 1)

        @block.scalar
        def _(act):
            act.wait_ge(shifted, 3)
            nc.scalar.activation(tanh_w[:], zT[0:HD, ZWA], ACT.Tanh).then_inc(squashed, 1)
            nc.scalar.activation(zT[:, ZGD], zT[:, ZGD], ACT.Sigmoid).then_inc(squashed, 1)
            nc.scalar.activation(zT[32:64, ZFG], zT[32:64, ZFG], ACT.Sigmoid).then_inc(squashed, 1)
            for m in range(NP4):
                act.wait_ge(lora_done, m + 1)
                if m >= 2:
                    act.wait_ge(bonus_out, m - 1)
                nc.scalar.activation(L[:, m], lora_ps[:, 0, :, 0:TH], ACT.Sigmoid,
                                     bias=cols[:, C_W0 + m:C_W0 + m + 1]).then_inc(lora_out, 1)
                nc.scalar.activation(a[:, m % 2], lora_ps[:, 1, :, 0:TH], ACT.Sigmoid,
                                     bias=cols[:, C_A0 + m:C_A0 + m + 1]).then_inc(lora_out, 1)
                nc.scalar.copy(g[:, m], lora_ps[:, 2, :, 0:TH]).then_inc(lora_out, 1)
                act.wait_ge(kk_raw, m + 1)
                nc.scalar.activation(sq[:], kk[:, m], ACT.Square).then_inc(squared, 1)
                act.wait_ge(summed, m + 1)
                nc.scalar.activation(rn[:], sum_ps[:, :, 0:TH], ACT.Sqrt).then_inc(rooted, 1)

        @block.tensor
        def _(pe):
            pe.wait_ge(loaded, 48)
            pe.wait_ge(squashed, 3)
            for m in range(NP4):
                c = slice(m * P, m * P + P)
                if m >= 1:
                    pe.wait_ge(lora_out, 3 * m)
                for half in range(2):
                    t = slice(half * TH, half * TH + TH)
                    nc.tensor.matmul(lora_ps[:, 0, half, 0:TH], wa_up[0:HD, c], tanh_w[:, t], start=True, stop=True)
                    nc.tensor.matmul(lora_ps[:, 1, half, 0:TH], wa_up[HD:P, c], zT[HD:P, ZWA, t], start=True, stop=True)
                    nc.tensor.matmul(lora_ps[:, 2, half, 0:TH], g_up[:, 0, c], zT[:, ZGD, t], start=True, stop=False)
                    mm = nc.tensor.matmul(lora_ps[:, 2, half, 0:TH], g_up[32:64, 1, c], zT[32:64, ZFG, t], start=False,
                                          stop=True)
                mm.then_inc(lora_done, 1)
                if m >= 1:
                    pe.wait_ge(bonus_out, m)
                for x, ready, done in ((sq, squared, summed), (rk, rk_ready, rk_summed)):
                    pe.wait_ge(ready, m + 1)
                    if x is rk:
                        pe.wait_ge(rooted, m + 1)
                    for half in range(2):
                        mm = nc.tensor.matmul(sum_ps[:, half, 0:TH], keep["blockones"][:],
                                              x[:, half * TH:half * TH + TH], start=True, stop=True)
                    mm.then_inc(done, 1)


def rwkv_recurrence(nc, d, keep):
    zT, L, Lx, kk, ka, yT = (keep[n] for n in ("zT", "L", "Lx", "kk", "ka", "yT"))
    NLEV = len(LEVELS)
    with ExitStack() as ctx:
        def sb(name, shape, dt=F32):
            return ctx.enter_context(nc.sbuf_tensor(name, shape, dt))

        def sem(name):
            return ctx.enter_context(nc.semaphore(name))

        mgram = sb("mgram", [C, NP4, 2 * C])
        mlev = sb("mlev", [C, NLEV + 2, C])
        eye8 = sb("eye8", [C, 2, NP4, C])
        ex = sb("ex", [P, 2, 3, NP4, C])
        ar = sb("ar", [P, 2, NP4, 2, C])
        bt = sb("bt", [P, 2, NP4, C])
        kt = sb("kt", [P, 2, NP4, C])
        vt = sb("vt", [P, 2, NP4, C])
        mb = sb("mb", [C, 2, 2, NP4, 2 * C])
        mk = sb("mk", [C, 2, 2, NP4, 2 * C])
        inv = sb("inv", [C, 2, 2, 2, NP4, C])
        off = sb("off", [C, 2, 4, C])
        toks = sb("toks", [C, 2, 3, W5])
        rhs = sb("rhs", [C, W5])
        nu = sb("nu", [C, W5])
        ST = sb("ST", [P, NP4, P])
        ps = ctx.enter_context(nc.psum_tensor("r_ps", [P, 8, 512], F32))

        loaded = sem("k_loaded")
        zeroed = sem("k_zeroed")
        exps = sem("k_exps")
        scaled = sem("k_scaled")
        gram = sem("k_gram")
        masked = sem("k_masked")
        inv1 = sem("k_inv1")
        turned = sem("k_turned")
        tok_out = sem("k_tok_out")
        offs = sem("k_offs")
        off_out = sem("k_off_out")
        grown = sem("k_grown")
        grown_out = sem("k_grown_out")
        steps = sem("k_steps")
        passed = sem("k_passed")
        rhs_done = sem("k_rhs_done")
        rhs_out = sem("k_rhs_out")
        u_done = sem("k_u_done")
        u_out = sem("k_u_out")
        y_done = sem("k_y_done")
        y_out = sem("k_y_out")
        s_done = sem("k_s_done")
        s_add = sem("k_s_add")
        s_out = sem("k_s_out")
        block = ctx.enter_context(nc.Block())
        NSTEP = 4

        def order(eng, prepare, level, recur):
            def both(c, b):
                prepare(c, b)
                for lv in range(NLEV):
                    level(c, b, lv)
                    if not (isinstance(c, int) and c == 0):
                        recur(c - 1, 1 - b, lv)
            both(0, 0)
            with eng.Fori(1, NCH - 1, 2) as c:
                both(c, 1)
                both(c + 1, 0)
            for lv in range(NLEV):
                recur(NCH - 1, 0, lv)

        def isn(c, k):
            return not isinstance(c, int) or c >= k

        @block.sync
        def _(sp):
            sp.dma_start(mgram[:], d["mgram"]).then_inc(loaded, 16)
            sp.dma_start(mlev[:], d["mlev"]).then_inc(loaded, 16)
            sp.dma_start(eye8[:], d["eye8"]).then_inc(loaded, 16)

        @block.scalar
        def _(act):
            def prepare(c, b):
                t = bass.ds(c * C, C)
                if isn(c, 2):
                    act.wait_ge(s_out, 2 * c - 2)
                    act.wait_ge(turned, 3 * c - 3)
                nc.scalar.activation(ex[:, b, 0], L[:, :, t], ACT.Exp).then_inc(exps, 1)
                nc.scalar.activation(ex[:, b, 1], L[:, :, t], ACT.Exp, scale=-1.0).then_inc(exps, 1)
                nc.scalar.activation(ex[:, b, 2], Lx[:, :, t], ACT.Exp).then_inc(exps, 1)
                nc.scalar.copy(vt[:, b], zT[:, ZRV:ZRV + 4, t]).then_inc(exps, 1)
                for j, bank in enumerate((6, 7, 0)):
                    act.wait_ge(turned, 3 * c + j + 1)
                    nc.scalar.copy(toks[:, b, j], ps[0:C, bank]).then_inc(tok_out, 1)

            def level(c, b, lv):
                pass

            def recur(c, b, lv):
                if lv == 0:
                    act.wait_ge(rhs_done, c + 1)
                    nc.scalar.copy(rhs[:], ps[0:C, 6]).then_inc(rhs_out, 1)
                if lv == 1:
                    act.wait_ge(u_done, c + 1)
                    nc.scalar.mul(nu[:], ps[0:C, 1], -1.0).then_inc(u_out, 1)
            order(act, prepare, level, recur)

        @block.vector
        def _(dve):
            dve.wait_ge(loaded, 48)
            nc.vector.memset(ST[:], 0.0).then_inc(zeroed, 1)
            dve.wait_ge(zeroed, 1)

            def prepare(c, b):
                t = bass.ds(c * C, C)
                dve.wait_ge(exps, 4 * c + 4)
                if isn(c, 2):
                    dve.wait_ge(y_done, c - 1)
                nc.vector.tensor_tensor(bt[:, b], ex[:, b, 1], ka[:, :, t], ALU.mult).then_inc(scaled, 1)
                nc.vector.tensor_tensor(ar[:, b, :, 0], ex[:, b, 2], kk[:, :, t], ALU.mult).then_inc(scaled, 1)
                nc.vector.tensor_tensor(ar[:, b, :, 1], ex[:, b, 0], zT[:, ZR:ZR + 4, t], ALU.mult).then_inc(scaled, 1)
                nc.vector.tensor_tensor(kt[:, b], ex[:, b, 1], zT[:, ZRK:ZRK + 4, t], ALU.mult).then_inc(scaled, 1)
                for j, m in enumerate((mb, mk)):
                    dve.wait_ge(gram, 3 * c + j + 1)
                    for e in range(2):
                        nc.vector.tensor_tensor(m[:, b, e], ps[0:C, 2 * j + e, 0:384].rearrange("p (a b) -> p a b", a=4),
                                                mgram[:], ALU.mult).then_inc(masked, 1)
                dve.wait_ge(gram, 3 * c + 3)
                dve.wait_ge(masked, 4 * c + 2)
                link = Chain(dve, steps, c * NSTEP)
                for e in range(2):
                    link(nc.vector.tensor_tensor(inv[:, b, e, 0], ps[0:C, 4 + e, 0:192].rearrange("p (a b) -> p a b", a=4),
                                                 mlev[:, NLEV:NLEV + 1].broadcast_to([C, 4, C]), ALU.mult))
                    link(nc.vector.tensor_tensor(inv[:, b, e, 1], mb[:, b, e, :, 0:C],
                                                 mlev[:, NLEV + 1:NLEV + 2].broadcast_to([C, 4, C]), ALU.mult))
                for e in range(2):
                    nc.vector.tensor_tensor(inv[:, b, e], inv[:, b, e], eye8[:], ALU.add).then_inc(inv1, 1)

            def level(c, b, lv):
                n = c * NLEV + lv
                for h in range(2):
                    dve.wait_ge(offs, n * 2 + h + 1)
                    nc.vector.tensor_tensor(off[:, h], ps[0:C, 2 + h, 0:192].rearrange("p (a b) -> p a b", a=4),
                                            mlev[:, lv:lv + 1].broadcast_to([C, 4, C]), ALU.mult).then_inc(off_out, 1)
                for h in range(2):
                    dve.wait_ge(grown, n * 2 + h + 1)
                    nc.vector.tensor_tensor(inv[:, b, h], inv[:, b, h],
                                            ps[0:C, 4 + h, 0:384].rearrange("p (x a b) -> p x a b", x=2, a=4),
                                            ALU.add).then_inc(grown_out, 1)

            def recur(c, b, lv):
                if lv == 3:
                    dve.wait_ge(s_done, c + 1)
                    dve.wait_ge(y_done, c + 1)
                    for e in range(2):
                        r, o = slice(e * HD, e * HD + HD), slice(e * HD, e * HD + HD)
                        nc.vector.tensor_tensor(ST[r, :, o], ps[r, 7, 256:512].rearrange("p (a b) -> p a b", a=NP4),
                                                ST[r, :, o], ALU.add).then_inc(s_add, 1)
                    for e in range(2):
                        r, o = slice(e * HD, e * HD + HD), slice(e * HD, e * HD + HD)
                        dve.wait_ge(s_add, 2 * c + e + 1)
                        nc.vector.tensor_tensor(ST[r, :, o], ST[r, :, o],
                                                ex[r, b, 0, :, C - 1:C].broadcast_to([HD, NP4, HD]),
                                                ALU.mult).then_inc(s_out, 1)
                    nc.vector.tensor_copy(yT[:, :, bass.ds(c * C, C)],
                                          ps[:, 7, 0:NP4 * C].rearrange("p (a b) -> p a b", a=NP4)).then_inc(y_out, 1)
            order(dve, prepare, level, recur)

        @block.tensor
        def _(pe):
            pe.wait_ge(loaded, 48)
            pe.wait_ge(zeroed, 1)

            def alone():
                pe.sem_inc(passed, 1)

            def head(h):
                return h // 2, slice(h % 2 * HD, h % 2 * HD + HD)

            def prepare(c, b):
                pe.wait_ge(scaled, 4 * c + 3)
                if isn(c, 1):
                    pe.wait_ge(grown_out, c * 2 * NLEV)
                    pe.wait_ge(tok_out, 3 * c)
                if isn(c, 2):
                    pe.wait_ge(u_out, c - 1)
                alone()
                for h in range(NH):
                    p, r = head(h)
                    mm = nc.tensor.matmul(ps[0:C, h % 2, p * 96:p * 96 + 96], bt[r, b, p], ar[r, b, p],
                                          start=True, stop=True)
                mm.then_inc(gram, 1)
                pe.wait_ge(scaled, 4 * c + 4)
                alone()
                for h in range(NH):
                    p, r = head(h)
                    mm = nc.tensor.matmul(ps[0:C, 2 + h % 2, p * 96:p * 96 + 96], kt[r, b, p], ar[r, b, p],
                                          start=True, stop=True)
                mm.then_inc(gram, 1)
                for h in range(NH):
                    p, r = head(h)
                    mm = nc.tensor.matmul(ps[0:C, 4 + h % 2, p * C:p * C + C], ar[r, b, p, 0], bt[r, b, p],
                                          start=True, stop=True)
                mm.then_inc(gram, 1)
                if isn(c, 2):
                    pe.wait_ge(rhs_out, c - 1)
                    pe.wait_ge(y_out, c - 1)
                    pe.wait_ge(s_add, 2 * c - 2)
                alone()
                for j, (x, bank) in enumerate(((kt, 6), (bt, 7), (vt, 0))):
                    if j == 2:
                        pe.wait_ge(exps, 4 * c + 4)
                        pe.wait_ge(masked, 4 * c + 2)
                    alone()
                    for p in range(NP4):
                        mm = nc.tensor.transpose(ps[0:C, bank, p * P:p * P + P], x[:, b, p], keep["ident"][:])
                    mm.then_inc(turned, 1)

            def level(c, b, lv):
                n = c * NLEV + lv
                if lv == 0:
                    pe.wait_ge(inv1, 2 * c + 2)
                    pe.wait_ge(masked, 4 * c + 4)
                alone()
                for e in range(2):
                    if lv >= 1:
                        pe.wait_ge(grown_out, n * 2 + e - 1)
                    alone()
                    for i in range(NP4):
                        mm = nc.tensor.matmul(ps[0:C, 2 + e, i * C:i * C + C], mb[:, b, e, i, 0:C],
                                              inv[:, b, e, 0, i], start=True, stop=True)
                    mm.then_inc(offs, 1)
                for e in range(2):
                    pe.wait_ge(off_out, n * 2 + e + 1)
                    alone()
                    for i in range(NP4):
                        nc.tensor.matmul(ps[0:C, 4 + e, i * C:i * C + C], inv[:, b, e, 1, i], off[:, e, i],
                                         start=True, stop=True)
                        mm = nc.tensor.matmul(ps[0:C, 4 + e, 192 + i * C:192 + i * C + C], off[:, e, i],
                                              inv[:, b, e, 1, i], start=True, stop=True)
                    mm.then_inc(grown, 1)

            def recur(c, b, lv):
                if lv == 0:
                    pe.wait_ge(s_out, 2 * c)
                    pe.wait_ge(grown_out, (c + 1) * 2 * NLEV)
                    pe.wait_ge(tok_out, 3 * NCH if isinstance(c, int) else 3 * c + 6)
                    alone()
                    for p in range(NP4):
                        nc.tensor.matmul(ps[0:C, 6, p * P:p * P + P], ar[:, b, p, 0], ST[:, p], start=(p == 0),
                                         stop=False, skip_group_check=True)
                    for h in range(NH):
                        mm = nc.tensor.matmul(ps[0:C, 6, h * HD:h * HD + HD], mk[:, b, h % 2, h // 2, 0:C],
                                              toks[:, b, 2, h * HD:h * HD + HD], start=False, stop=True,
                                              skip_group_check=True)
                    mm.then_inc(rhs_done, 1)
                if lv == 1:
                    pe.wait_ge(rhs_out, c + 1)
                    alone()
                    for h in range(NH):
                        mm = nc.tensor.matmul(ps[0:C, 1, h * HD:h * HD + HD], inv[:, b, h % 2, 1, h // 2],
                                              rhs[:, h * HD:h * HD + HD], start=True, stop=True)
                    mm.then_inc(u_done, 1)
                if lv == 2:
                    pe.wait_ge(u_out, c + 1)
                    pe.wait_ge(y_out, c)
                    alone()
                    for h in range(NH):
                        p, r = head(h)
                        c64 = slice(h * HD, h * HD + HD)
                        o = ps[r, 7, 256 + p * HD:256 + p * HD + HD]
                        nc.tensor.matmul(o, toks[:, b, 0, c64], toks[:, b, 2, c64], start=True, stop=False)
                        mm = nc.tensor.matmul(o, toks[:, b, 1, c64], nu[:, c64], start=False, stop=True)
                    mm.then_inc(s_done, 1)
                    for p in range(NP4):
                        nc.tensor.matmul(ps[:, 7, p * C:p * C + C], ST[:, p], ar[:, b, p, 1], start=(p == 0),
                                         stop=False, skip_group_check=True)
                    for h in range(NH):
                        p, r = head(h)
                        c64 = slice(h * HD, h * HD + HD)
                        o = ps[r, 7, p * C:p * C + C]
                        nc.tensor.matmul(o, toks[:, b, 2, c64], mk[:, b, h % 2, p, C:2 * C], start=False, stop=False,
                                         skip_group_check=True)
                        mm = nc.tensor.matmul(o, nu[:, c64], mb[:, b, h % 2, p, C:2 * C], start=False, stop=True,
                                              skip_group_check=True)
                    mm.then_inc(y_done, 1)

            order(pe, prepare, level, recur)


def rwkv_output(nc, d, keep):
    cols, yT, bonus, g, yrT = (keep[n] for n in ("cols", "yT", "bonus", "g", "yrT"))
    X = slice(N_META, T)
    with ExitStack() as ctx:
        def sb(name, shape, dt=F32):
            return ctx.enter_context(nc.sbuf_tensor(name, shape, dt))

        def sem(name):
            return ctx.enter_context(nc.semaphore(name))

        yc = sb("o_yc", [P, NP4, SEQ])
        sq = sb("o_sq", [P, NP4, SEQ])
        rt = sb("o_rt", [P, NP4, SEQ])
        ps = ctx.enter_context(nc.psum_tensor("o_ps", [P, 8, 512], F32))
        mean, centred, squared, var, rooted, steps = (sem("o_" + n) for n in (
            "mean", "centred", "squared", "var", "rooted", "steps"))
        block = ctx.enter_context(nc.Block())

        @block.tensor
        def _(pe):
            for m in range(NP4):
                nc.tensor.matmul(ps[:, m], keep["blockmean"][:], yT[:, m, X], start=True, stop=True).then_inc(mean, 1)
            for m in range(NP4):
                pe.wait_ge(squared, m + 1)
                nc.tensor.matmul(ps[:, 4 + m], keep["blockmean"][:], sq[:, m], start=True, stop=True).then_inc(var, 1)

        @block.scalar
        def _(act):
            for m in range(NP4):
                act.wait_ge(centred, m + 1)
                nc.scalar.activation(sq[:, m], yc[:, m], ACT.Square).then_inc(squared, 1)
            for m in range(NP4):
                act.wait_ge(var, m + 1)
                nc.scalar.activation(rt[:, m], ps[:, 4 + m], ACT.Sqrt, bias=keep["eps"][:, 2:3]).then_inc(rooted, 1)

        @block.vector
        def _(dve):
            link = Chain(dve, steps)
            for m in range(NP4):
                dve.wait_ge(mean, m + 1)
                nc.vector.tensor_tensor(yc[:, m], yT[:, m, X], ps[:, m], ALU.subtract).then_inc(centred, 1)
            for m in range(NP4):
                def col(c):
                    return cols[:, c + m:c + m + 1]
                dve.wait_ge(rooted, m + 1)
                link(nc.vector.reciprocal(rt[:, m], rt[:, m]))
                link(nc.vector.tensor_tensor(yc[:, m], yc[:, m], rt[:, m], ALU.mult))
                link(nc.vector.tensor_scalar(yc[:, m], yc[:, m], col(C_LG), col(C_LB), ALU.mult, ALU.add))
                link(nc.vector.tensor_tensor(yc[:, m], yc[:, m], bonus[:, m, X], ALU.add))
                link(nc.vector.tensor_tensor(yrT[:, m], yc[:, m], g[:, m, X], ALU.mult))


def branches_and_residual(nc, d, keep):
    cols, zT, yfT, yrT, acc = (keep[n] for n in ("cols", "zT", "yfT", "yrT", "acc"))
    X = slice(N_META, T)
    with ExitStack() as ctx:
        def sb(name, shape, dt=F32):
            return ctx.enter_context(nc.sbuf_tensor(name, shape, dt))

        def sem(name):
            return ctx.enter_context(nc.semaphore(name))

        wb = sb("wb", [P, 2, NP4, D])
        wo = sb("wo", [P, KD, D])
        part = sb("b_part", [P, 2, 2, SEQ])
        mixed = sb("mixed", [P, KD, SEQ])
        ps = ctx.enter_context(nc.psum_tensor("b_ps", [P, 8, 512], F32))
        loaded_b, loaded_o, x_loaded, gates, branch, parts, mixed_done, wout_done, h2_done = (sem("b_" + n) for n in (
            "loaded_b", "loaded_o", "x_loaded", "gates", "branch", "parts", "mixed", "wout", "h2"))
        block = ctx.enter_context(nc.Block())

        @block.sync
        def _(sp):
            sp.dma_start(wb[:], d["w_branch"]).then_inc(loaded_b, 16)
            sp.dma_start(wo[:], d["w_out"]).then_inc(loaded_o, 16)
            sp.dma_start(acc[:], d["x_tok"]).then_inc(x_loaded, 16)

        @block.scalar
        def _(act):
            for m in range(2 * KD):
                nc.scalar.activation(zT[:, ZGF + m, X], zT[:, ZGF + m, X], ACT.Sigmoid).then_inc(gates, 1)

        @block.tensor
        def _(pe):
            pe.wait_ge(loaded_b, 16)
            for m in range(KD):
                for br, y in enumerate((yfT, yrT)):
                    if m >= 2:
                        pe.wait_ge(parts, 2 * (m - 2) + br + 1)
                    for k in range(NP4):
                        mm = nc.tensor.matmul(ps[:, m % 2 * 2 + br], wb[:, br, k, m * P:m * P + P], y[:, k],
                                              start=(k == 0), stop=(k == NP4 - 1))
                    mm.then_inc(branch, 1)
            pe.wait_ge(loaded_o, 16)
            for i in range(NQ):
                for half in range(2):
                    n = 2 * i + half
                    if n >= 4:
                        pe.wait_ge(h2_done, n - 3)
                    for k in range(KD):
                        if n == 0:
                            pe.wait_ge(mixed_done, k + 1)
                        mm = nc.tensor.matmul(ps[:, 4 + n % 4], mixed[:, k, i * P:i * P + P],
                                              wo[:, k, half * 512:half * 512 + 512], start=(k == 0), stop=(k == KD - 1))
                    mm.then_inc(wout_done, 1)

        @block.vector
        def _(dve):
            for m in range(KD):
                for br in range(2):
                    dve.wait_ge(gates, KD * br + m + 1)
                    dve.wait_ge(branch, 2 * m + br + 1)
                    if m >= 2:
                        dve.wait_ge(mixed_done, m - 1)
                    nc.vector.tensor_tensor(part[:, m % 2, br], ps[:, m % 2 * 2 + br], zT[:, ZGF + KD * br + m, X],
                                            ALU.mult).then_inc(parts, 1)
                dve.wait_ge(parts, 2 * m + 2)
                nc.vector.tensor_tensor(mixed[:, m], part[:, m % 2, 0], part[:, m % 2, 1], ALU.add).then_inc(mixed_done, 1)
            dve.wait_ge(x_loaded, 16)
            for n in range(2 * NQ):
                dve.wait_ge(wout_done, n + 1)
                o = acc[:, n // 2, n % 2 * 512:n % 2 * 512 + 512]
                nc.vector.tensor_tensor(o, ps[:, 4 + n % 4], o, ALU.add).then_inc(h2_done, 1)


def second_norm(nc, d, keep):
    cols, acc, x2h, x2l = (keep[n] for n in ("cols", "acc", "x2h", "x2l"))
    with ExitStack() as ctx:
        def sb(name, shape, dt=F32):
            return ctx.enter_context(nc.sbuf_tensor(name, shape, dt))

        def sem(name):
            return ctx.enter_context(nc.semaphore(name))

        sq = sb("n_sq", [P, 2, D])
        ms = sb("n_ms", [P, 2, NQ])
        xn = sb("n_xn", [P, NQ, D])
        xT = sb("n_xT", [P, KD, SEQ])
        ps = ctx.enter_context(nc.psum_tensor("n_ps", [P, 8, 512], F32))
        squared, rooted, inverted, scaled, turned, gained, x_hi, x_lo = (sem("n_" + n) for n in (
            "squared", "rooted", "inverted", "scaled", "turned", "gained", "x_hi", "x_lo"))
        block = ctx.enter_context(nc.Block())

        @block.scalar
        def _(act):
            for i in range(NQ):
                if i >= 2:
                    act.wait_ge(squared, i - 1)
                nc.scalar.activation(sq[:, i % 2], acc[:, i], ACT.Square, accum_out=ms[:, 0, i:i + 1]).then_inc(squared, 1)
            act.wait_ge(squared, NQ)
            nc.scalar.activation(ms[:, 1], ms[:, 0], ACT.Sqrt, bias=keep["eps"][:, 0:1], scale=1.0 / D).then_inc(rooted, 1)
            for k in range(KD):
                act.wait_ge(turned, k + 1)
                nc.scalar.activation(xT[:, k], ps[:, k], ACT.Copy, scale=cols[:, C_G2 + k:C_G2 + k + 1]).then_inc(gained, 1)
            for k in range(KD):
                act.wait_ge(gained, k + 1)
                nc.scalar.copy(x2h[:, k], xT[:, k]).then_inc(x_hi, 1)

        @block.vector
        def _(dve):
            dve.wait_ge(rooted, 1)
            nc.vector.reciprocal(ms[:, 0], ms[:, 1]).then_inc(inverted, 1)
            dve.wait_ge(inverted, 1)
            for i in range(NQ):
                nc.vector.tensor_scalar(xn[:, i], acc[:, i], ms[:, 0, i:i + 1], None, ALU.mult).then_inc(scaled, 1)
            for k in range(KD):
                dve.wait_ge(x_hi, k + 1)
                nc.vector.tensor_tensor(x2l[:, k], xT[:, k], x2h[:, k].bitcast(F32), ALU.subtract).then_inc(x_lo, 1)

        @block.tensor
        def _(pe):
            pe.wait_ge(scaled, NQ)
            for k in range(KD):
                for i in range(NQ):
                    mm = nc.tensor.transpose(ps[:, k, i * P:i * P + P], xn[:, i, k * P:k * P + P], keep["ident"][:])
                mm.then_inc(turned, 1)


def peer_retrieval(nc, d, keep):
    x2h, x2l, picksT = (keep[n] for n in ("x2h", "x2l", "picksT"))
    NV = TOPK * TOPK
    with ExitStack() as ctx:
        def sb(name, shape, dt=F32):
            return ctx.enter_context(nc.sbuf_tensor(name, shape, dt))

        def sem(name):
            return ctx.enter_context(nc.semaphore(name))

        wraw = sb("q_wraw", [P, 2, KD, P])
        wh = sb("q_wh", [P, 2, KD, P], F32R)
        wl = sb("q_wl", [P, 2, KD, P], F32R)
        subk = sb("subk", [P, 2, NK])
        iota = sb("iota16", [P, TOPK])
        qT = sb("qT", [P, 2, SEQ])
        s = sb("s", [P, 2, NQ, NK])
        rest = sb("rest", [P, NQ, NK])
        top = sb("top", [P, 2, NQ, TOPK])
        idx = sb("idx", [P, 2, NQ, TOPK], U32)
        idxf = sb("idxf", [P, 2, NQ, TOPK])
        cand = sb("cand", [P, NQ, NV])
        crest = sb("crest", [P, NQ, NV])
        ctop = sb("ctop", [P, NQ, TOPK])
        cpos = sb("cpos", [P, NQ, TOPK], U32)
        cab = sb("cab", [P, 2, NQ, TOPK], U32)
        cabf = sb("cabf", [P, 2, NQ, TOPK])
        eq = sb("eq", [P, NQ, TOPK, TOPK])
        shifted = sb("shifted", [P, NQ, TOPK])
        gates = sb("gates", [P, NQ, TOPK])
        gsum = sb("gsum", [P, 2, NQ])
        picks = sb("picks", [P, 3, NQ, PH, TOPK])
        q_ps = ctx.enter_context(nc.psum_tensor("q_ps", [P, 2, 512], F32))
        s_ps = ctx.enter_context(nc.psum_tensor("qs_ps", [P, 2, 512], F32))
        t_ps = ctx.enter_context(nc.psum_tensor("qt_ps", [P, 3, 512], F32))

        loaded = sem("q_loaded")
        w_in = [sem(f"q_w_arrived{b}") for b in range(2)]
        w_hi, w_lo, q_done, q_out, s_done, s_out, found, shift_done, exp_done, listed, turned, t_out, steps = (
            sem("q_" + n) for n in ("w_hi", "w_lo", "q_done", "q_out", "s_done", "s_out", "found", "shift_done",
                                    "exp_done", "listed", "turned", "t_out", "steps"))
        block = ctx.enter_context(nc.Block())

        @block.sync
        def _(sp):
            sp.dma_start(subk[:], d["subk"]).then_inc(loaded, 16)
            sp.dma_start(iota[:], d["iota16"]).then_inc(loaded, 16)
            for n in range(2):
                sp.dma_start(wraw[:, n], d["w_q"][n]).then_inc(w_in[n], 16)
            with sp.Fori(2, 2 * PH - 1, 2) as n:
                for b in range(2):
                    sp.wait_ge(w_lo, n + (b - 1))
                    sp.dma_start(wraw[:, b], d["w_q"][n + b]).then_inc(w_in[b], 16)

        @block.scalar
        def _(act):
            act.wait_ge(loaded, 32)
            with act.Fori(0, PH) as h:
                for b in range(2):
                    act.wait_ge(w_in[b], h * 16 + 16)
                    act.wait_ge(q_done, h * 2)
                    nc.scalar.copy(wh[:, b], wraw[:, b]).then_inc(w_hi, 1)
                for b in range(2):
                    act.wait_ge(q_done, h * 2 + b + 1)
                    act.wait_ge(s_done, h * 2)
                    nc.scalar.copy(qT[:, b], q_ps[:, b]).then_inc(q_out, 1)
                for b in range(2):
                    act.wait_ge(s_done, h * 2 + b + 1)
                    act.wait_ge(found, h * 2)
                    nc.scalar.copy(s[:, b], s_ps[:, b]).then_inc(s_out, 1)
                act.wait_ge(shift_done, h + 1)
                nc.scalar.activation(gates[:], shifted[:], ACT.Exp).then_inc(exp_done, 1)
            for j in range(3):
                act.wait_ge(turned, j + 1)
                nc.scalar.copy(picksT[:, j], t_ps[:, j]).then_inc(t_out, 1)

        @block.vector
        def _(dve):
            link = Chain(dve, steps)
            for h in range(PH):
                for b in range(2):
                    dve.wait_ge(w_hi, h * 2 + b + 1)
                    nc.vector.tensor_tensor(wl[:, b], wraw[:, b], wh[:, b].bitcast(F32), ALU.subtract).then_inc(w_lo, 1)
                for b in range(2):
                    dve.wait_ge(s_out, h * 2 + b + 1)
                    for i in range(NQ):
                        link(nc.vector.max(top[:, b, i, 0:8], s[:, b, i]))
                        link(nc.vector.match_replace(rest[:, i], top[:, b, i, 0:8], s[:, b, i], -3.0e38))
                        nc.vector.max_index(idx[:, b, i, 0:8], top[:, b, i, 0:8], s[:, b, i])
                        link(nc.vector.max(top[:, b, i, 8:16], rest[:, i]))
                        link(nc.vector.max_index(idx[:, b, i, 8:16], top[:, b, i, 8:16], rest[:, i]))
                    nc.vector.tensor_copy(idxf[:, b], idx[:, b]).then_inc(found, 1)
                    dve.wait_ge(found, h * 2 + b + 1)
                link(nc.vector.tensor_tensor(
                    cand[:].rearrange("p q (a b) -> p q a b", a=TOPK),
                    top[:, 0].unsqueeze(3).broadcast_to([P, NQ, TOPK, TOPK]),
                    top[:, 1].unsqueeze(2).broadcast_to([P, NQ, TOPK, TOPK]), ALU.add))
                for i in range(NQ):
                    link(nc.vector.max(ctop[:, i, 0:8], cand[:, i]))
                    link(nc.vector.match_replace(crest[:, i], ctop[:, i, 0:8], cand[:, i], -3.0e38))
                    nc.vector.max_index(cpos[:, i, 0:8], ctop[:, i, 0:8], cand[:, i])
                    link(nc.vector.max(ctop[:, i, 8:16], crest[:, i]))
                    link(nc.vector.max_index(cpos[:, i, 8:16], ctop[:, i, 8:16], crest[:, i]))
                nc.vector.tensor_tensor(shifted[:], ctop[:], ctop[:, :, 0:1].broadcast_to([P, NQ, TOPK]),
                                        ALU.subtract).then_inc(shift_done, 1)
                link(nc.vector.tensor_scalar(cab[:, 0], cpos[:], 4, None, ALU.logical_shift_right))
                link(nc.vector.tensor_scalar(cab[:, 1], cpos[:], 15, None, ALU.bitwise_and))
                link(nc.vector.tensor_copy(cabf[:], cab[:]))
                for j in range(2):
                    link(nc.vector.tensor_tensor(
                        eq[:], cabf[:, j].unsqueeze(3).broadcast_to([P, NQ, TOPK, TOPK]),
                        iota[:].unsqueeze(1).unsqueeze(1).broadcast_to([P, NQ, TOPK, TOPK]), ALU.is_equal))
                    link(nc.vector.tensor_tensor(eq[:], eq[:], idxf[:, j].unsqueeze(2).broadcast_to([P, NQ, TOPK, TOPK]),
                                                 ALU.mult))
                    link(nc.vector.reduce_sum(picks[:, j, :, h], eq[:], AX.X))
                dve.wait_ge(exp_done, h + 1)
                link(nc.vector.reduce_sum(gsum[:, 0], gates[:], AX.X))
                link(nc.vector.reciprocal(gsum[:, 1], gsum[:, 0]))
                nc.vector.tensor_tensor(picks[:, 2, :, h], gates[:],
                                        gsum[:, 1].unsqueeze(2).broadcast_to([P, NQ, TOPK]), ALU.mult).then_inc(listed, 1)
                dve.wait_ge(listed, h + 1)

        @block.tensor
        def _(pe):
            pe.wait_ge(loaded, 32)
            with pe.Fori(0, PH) as h:
                for b in range(2):
                    pe.wait_ge(w_lo, h * 2 + b + 1)
                    pe.wait_ge(q_out, h * 2)
                    for k in range(KD):
                        mm = matmul3(nc, q_ps[:, b], (wh[:, b, k], wl[:, b, k]), (x2h[:, k], x2l[:, k]), k == 0, k == KD - 1)
                    mm.then_inc(q_done, 1)
                for b in range(2):
                    pe.wait_ge(q_out, h * 2 + b + 1)
                    pe.wait_ge(s_out, h * 2)
                    for i in range(NQ):
                        mm = nc.tensor.matmul(s_ps[:, b, i * NK:i * NK + NK], qT[:, b, i * P:i * P + P], subk[:, b],
                                              start=True, stop=True)
                    mm.then_inc(s_done, 1)
            pe.wait_ge(listed, PH)
            for j in range(3):
                for i in range(NQ):
                    mm = nc.tensor.transpose(t_ps[:, j, i * P:i * P + P],
                                             picks[:, j, i].rearrange("p h k -> p (h k)"), keep["ident"][:])
                mm.then_inc(turned, 1)


def gate_matrix(nc, d, keep):
    picksT = keep["picksT"]
    TB = 4
    NS = P // TB
    with ExitStack() as ctx:
        def sb(name, shape, dt=F32):
            return ctx.enter_context(nc.sbuf_tensor(name, shape, dt))

        def sem(name):
            return ctx.enter_context(nc.semaphore(name))

        iota = sb("iota128", [P, NK])
        hot1 = sb("hot1", [P, 2, TB, NK])
        hot2 = sb("hot2", [P, 2, TB, NK])
        stage = sb("stage", [P, NK, P])
        ps = ctx.enter_context(nc.psum_tensor("g_ps", [P, 2, TB, NK], F32))
        loaded, hot, placed, staged, stored = (sem("g_" + n) for n in ("loaded", "hot", "placed", "staged", "stored"))
        block = ctx.enter_context(nc.Block())

        @block.sync
        def _(sp):
            sp.dma_start(iota[:], d["iota128"]).then_inc(loaded, 16)
            for i in range(NQ):
                sp.wait_ge(staged, NS * (i + 1))
                sp.dma_start(keep["G"][:, :, i * P:i * P + P].rearrange("a b t -> b a t"), stage[:]).then_inc(stored, 16)
            sp.wait_ge(stored, 16 * NQ)

        @block.vector
        def _(dve):
            dve.wait_ge(loaded, 16)

            def step(n, b):
                if not isinstance(n, int):
                    dve.wait_ge(placed, n - 1)
                for t in range(TB):
                    t1 = bass.ds(n * TB + t, 1)
                    nc.vector.tensor_scalar(hot1[:, b, t], iota[:], picksT[:, 0, t1], picksT[:, 2, t1],
                                            ALU.is_equal, ALU.mult).then_inc(hot, 1)
                    nc.vector.tensor_scalar(hot2[:, b, t], iota[:], picksT[:, 1, t1], None,
                                            ALU.is_equal).then_inc(hot, 1)
            for n in range(2):
                step(n, n)
            with dve.Fori(2, NQ * NS - 1, 2) as n:
                for b in range(2):
                    step(n + b, b)

        @block.tensor
        def _(pe):
            def step(n, b):
                pe.wait_ge(hot, (n + 1) * 2 * TB)
                if not isinstance(n, int):
                    pe.wait_ge(staged, n - 1)
                for t in range(TB):
                    mm = nc.tensor.matmul(ps[:, b, t], hot2[:, b, t], hot1[:, b, t], start=True, stop=True)
                mm.then_inc(placed, 1)
            for n in range(2):
                step(n, n)
            with pe.Fori(2, NQ * NS - 1, 2) as n:
                for b in range(2):
                    step(n + b, b)

        @block.scalar
        def _(act):
            for i in range(NQ):
                if i:
                    act.wait_ge(stored, 16 * i)
                with act.Fori(0, NS - 1, 2) as n:
                    for b in range(2):
                        act.wait_ge(placed, n + (i * NS + b + 1))
                        nc.scalar.copy(stage[:, :, bass.ds((n + b) * TB, TB)].rearrange("p a t -> p t a"),
                                       ps[:, b]).then_inc(staged, 1)


def experts(nc, d, keep):
    x2h, x2l, acc, G = (keep[n] for n in ("x2h", "x2l", "acc", "G"))
    NG = NCHUNK // GROUP
    NB = 2 * NQ
    with ExitStack() as ctx:
        def sb(name, shape, dt=F32):
            return ctx.enter_context(nc.sbuf_tensor(name, shape, dt))

        def sem(name):
            return ctx.enter_context(nc.semaphore(name))

        uraw = sb("uraw", [P, GROUP, KD, P])
        uh = sb("uh", [P, GROUP, KD, P], F32R)
        ul = sb("ul", [P, GROUP, KD, P], F32R)
        vraw = sb("vraw", [P, GROUP, D])
        vh = sb("vh", [P, 2, GROUP, D], F32R)
        vl = sb("vl", [P, 2, GROUP, D], F32R)
        gm = sb("gm", [P, GROUP, SEQ])
        hid = sb("hid", [P, GROUP, SEQ])
        wt = sb("wt", [P, GROUP, SEQ])
        wh = sb("e_wh", [P, 2, GROUP, SEQ], F32R)
        wl = sb("e_wl", [P, 2, GROUP, SEQ], F32R)
        h_ps = ctx.enter_context(nc.psum_tensor("h_ps", [P, GROUP, 512], F32))
        o_ps = ctx.enter_context(nc.psum_tensor("eo_ps", [P, 4, 512], F32))
        u_in = [sem(f"e_u_arrived{s}") for s in range(GROUP)]
        v_in = [sem(f"e_v_arrived{s}") for s in range(GROUP)]
        g_in = [sem(f"e_g_arrived{s}") for s in range(GROUP)]
        u_hi, u_lo, v_hi, v_lo, u_done, hid_out, w_done, w_hi, w_lo, v_done, added, stored = (sem("e_" + n) for n in (
            "u_hi", "u_lo", "v_hi", "v_lo", "u_done", "hid_out", "w_done", "w_hi", "w_lo", "v_done", "added", "stored"))
        block = ctx.enter_context(nc.Block())

        def groups(eng, group):
            group(0, 0)
            group(1, 1)
            with eng.Fori(2, NG - 3, 2) as g:
                group(g, 0)
                group(g + 1, 1)
            group(NG - 2, 0)
            group(NG - 1, 1)

        def isn(g, k):
            return not isinstance(g, int) or g >= k

        def more(g):
            return not isinstance(g, int) or g + 1 < NG

        @block.sync
        def _(sp):
            def group(g, b):
                for s in range(GROUP):
                    n = g * GROUP + s
                    if isn(g, 1):
                        sp.wait_ge(u_lo, (g - 1) * GROUP + s + 1)
                    sp.dma_start(uraw[:, s], d["u"][n]).then_inc(u_in[s], 16)
                    if isn(g, 1):
                        sp.wait_ge(v_lo, (g - 1) * GROUP + s + 1)
                        sp.wait_ge(w_done, (g - 1) * GROUP + s + 1)
                    sp.dma_start(vraw[:, s], d["v"][n]).then_inc(v_in[s], 16)
                    sp.dma_start(gm[:, s], G[n]).then_inc(g_in[s], 16)
            groups(sp, group)
            sp.wait_ge(added, NG * NB)
            sp.dma_start(d["out"].rearrange("(i p) n -> p i n", p=P), acc[:]).then_inc(stored, 16)
            sp.wait_ge(stored, 16)

        @block.scalar
        def _(act):
            def split_u(g, s):
                act.wait_ge(u_in[s], (g + 1) * 16)
                if isn(g, 1):
                    act.wait_ge(u_done, (g - 1) * GROUP + s + 1)
                nc.scalar.copy(uh[:, s], uraw[:, s]).then_inc(u_hi, 1)

            def group(g, b):
                for s in range(GROUP):
                    act.wait_ge(v_in[s], (g + 1) * 16)
                    if isn(g, 2):
                        act.wait_ge(v_done, (g - 1) * NB)
                    nc.scalar.copy(vh[:, b, s], vraw[:, s]).then_inc(v_hi, 1)
                for s in range(GROUP):
                    n = g * GROUP + s
                    act.wait_ge(u_done, n + 1)
                    if isn(g, 1):
                        act.wait_ge(w_done, n - GROUP + 1)
                    nc.scalar.activation(hid[:, s], h_ps[:, s], ACT.Gelu).then_inc(hid_out, 1)
                    act.wait_ge(w_done, n + 1)
                    nc.scalar.copy(wh[:, b, s], wt[:, s]).then_inc(w_hi, 1)
                if more(g):
                    for s in range(GROUP):
                        split_u(g + 1, s)
            for s in range(GROUP):
                split_u(0, s)
            groups(act, group)

        @block.vector
        def _(dve):
            def add(g, o):
                dve.wait_ge(v_done, g * NB + o + 1)
                a = acc[:, o // 2, o % 2 * 512:o % 2 * 512 + 512]
                nc.vector.tensor_tensor(a, o_ps[:, o % 4], a, ALU.add).then_inc(added, 1)

            def split_u(g, s):
                dve.wait_ge(u_hi, g * GROUP + s + 1)
                nc.vector.tensor_tensor(ul[:, s], uraw[:, s], uh[:, s].bitcast(F32), ALU.subtract).then_inc(u_lo, 1)

            def group(g, b):
                for s in range(GROUP):
                    dve.wait_ge(v_hi, g * GROUP + s + 1)
                    nc.vector.tensor_tensor(vl[:, b, s], vraw[:, s], vh[:, b, s].bitcast(F32), ALU.subtract).then_inc(v_lo, 1)
                for s in range(GROUP):
                    n = g * GROUP + s
                    dve.wait_ge(hid_out, n + 1)
                    dve.wait_ge(g_in[s], (g + 1) * 16)
                    nc.vector.tensor_tensor(wt[:, s], hid[:, s], gm[:, s], ALU.mult).then_inc(w_done, 1)
                    dve.wait_ge(w_hi, n + 1)
                    nc.vector.tensor_tensor(wl[:, b, s], wt[:, s], wh[:, b, s].bitcast(F32), ALU.subtract).then_inc(w_lo, 1)
                for o in range(NB):
                    if isn(g, 1):
                        add(g - 1, o)
                    if o % 3 == 1 and o // 3 < GROUP and more(g):
                        split_u(g + 1, o // 3)
            for s in range(GROUP):
                split_u(0, s)
            groups(dve, group)
            for o in range(NB):
                add(NG - 1, o)

        @block.tensor
        def _(pe):
            def vs(g, b):
                pe.wait_ge(w_lo, (g + 1) * GROUP)
                pe.wait_ge(v_lo, (g + 1) * GROUP)
                for o in range(NB):
                    i, half = o // 2, o % 2
                    if isn(g, 1) or o >= 4:
                        pe.wait_ge(added, g * NB + (o - 3))
                    for s in range(GROUP):
                        mm = matmul3(nc, o_ps[:, o % 4], (wh[:, b, s, i * P:i * P + P], wl[:, b, s, i * P:i * P + P]),
                                     (vh[:, b, s, half * 512:half * 512 + 512], vl[:, b, s, half * 512:half * 512 + 512]),
                                     s == 0, s == GROUP - 1)
                    mm.then_inc(v_done, 1)

            def group(g, b):
                for s in range(GROUP):
                    n = g * GROUP + s
                    pe.wait_ge(u_lo, n + 1)
                    if isn(g, 1):
                        pe.wait_ge(hid_out, n - GROUP + 1)
                    for k in range(KD):
                        mm = matmul3(nc, h_ps[:, s], (uh[:, s, k], ul[:, s, k]), (x2h[:, k], x2l[:, k]), k == 0, k == KD - 1)
                    mm.then_inc(u_done, 1)
                if isn(g, 1):
                    vs(g - 1, 1 - b)
            groups(pe, group)
            vs(NG - 1, 1)


def build(nc, d, stop=99, tap=None):
    with ExitStack() as ctx:
        def sb(name, shape, dt=F32):
            return ctx.enter_context(nc.sbuf_tensor(name, shape, dt))
        keep = {}
        for name in CONSTS:
            keep[name] = sb(name, [P, P])
        keep["cols"] = sb("cols", [P, NC_COLS])
        keep["eps"] = sb("eps", [P, 8])
        EPS_COLS = [EPS, HD * EPS, GN_EPS, 0.0]
        with nc.Block() as block:
            @block.gpsimd
            def _(pool):
                for i, e in enumerate(EPS_COLS):
                    nc.gpsimd.memset(keep["eps"][:, i:i + 1], e)
        keep["G"] = nc.dram_tensor("G_scratch", (NK, NK, SEQ), F32, kind="Internal").ap()
        early = ctx.enter_context(ExitStack())
        keep["zT"] = early.enter_context(nc.sbuf_tensor("zT", [P, NZ, T], F32, side="right"))
        keep["yfT"] = early.enter_context(nc.sbuf_tensor("yfT", [P, NP4, SEQ], F32, side="right"))
        norm_and_project(nc, d, keep)
        if stop == 1: return tap(nc, keep)
        fox_attention(nc, d, keep)
        if stop == 2: return tap(nc, keep)
        with ExitStack() as rwkv:
            for name in ("bonus", "g", "L", "Lx", "kk", "ka"):
                keep[name] = rwkv.enter_context(nc.sbuf_tensor("r_" + name, [P, NP4, T], F32, side="right"))
            rwkv_inputs(nc, d, keep)
            if stop == 3: return tap(nc, keep)
            keep["yT"] = keep["zT"][:, ZQ:ZQ + NP4]
            rwkv_recurrence(nc, d, keep)
            if stop == 4: return tap(nc, keep)
            keep["yrT"] = keep["zT"][:, ZK:ZK + NP4, 0:SEQ]
            rwkv_output(nc, d, keep)
            if stop == 5: return tap(nc, keep)
        keep["acc"] = sb("acc", [P, NQ, D])
        branches_and_residual(nc, d, keep)
        if stop == 6: return tap(nc, keep)
        early.close()
        keep["x2h"] = sb("x2h", [P, KD, SEQ], F32R)
        keep["x2l"] = sb("x2l", [P, KD, SEQ], F32R)
        keep["picksT"] = sb("picksT", [P, 3, SEQ])
        second_norm(nc, d, keep)
        peer_retrieval(nc, d, keep)
        if stop == 7: return tap(nc, keep)
        gate_matrix(nc, d, keep)
        if stop == 8: return tap(nc, keep)
        experts(nc, d, keep)


def _columns(vectors):
    return np.concatenate([v.reshape(-1, P).T for v in vectors], axis=1)


def layout(x, meta_tokens, norm1_g, w_in, fox_q_norm, fox_k_norm, fox_f_bias,
           rwkv_mu, rwkv_w0, rwkv_w_up, rwkv_a0, rwkv_a_up, rwkv_g_up, rwkv_k_k,
           rwkv_k_a, rwkv_r_k, rwkv_ln_g, rwkv_ln_b, w_branch_fox, w_branch_rwkv,
           w_out, norm2_g, peer_w_q, peer_sub_k1, peer_sub_k2, peer_u, peer_v):
    f = lambda a: np.asarray(a)
    x, meta = f(x)[0], f(meta_tokens)
    z = lambda *s: np.zeros(s, np.float32)
    d = {}
    h = np.concatenate([meta, x], axis=0)
    d["hT"] = h.T.reshape(KD, P, T).transpose(1, 0, 2)
    d["x_tok"] = x.reshape(NQ, P, D).transpose(1, 0, 2)
    w = f(w_in)[0]
    fox, rwkv, gates = w[:, :1544], w[:, 1544:1544 + 1824], w[:, 3368:]
    pad = lambda n: z(D, n)
    wz = np.concatenate([fox[:, :1536], rwkv[:, :1536], rwkv[:, 1536:1664], rwkv[:, 1664:1792],
                         fox[:, 1536:1544], pad(24), rwkv[:, 1792:1824], pad(64), gates], axis=1)
    d["w_z"] = wz.reshape(KD, P, NZ, P).transpose(2, 1, 0, 3)
    mu = f(rwkv_mu)[0]
    mu = np.concatenate([mu[:1792], z(32), mu[1792:1824], z(64)])
    fb = np.concatenate([f(fox_f_bias)[0], z(P - NH)])
    d["cols"] = _columns([f(a)[0].reshape(-1) for a in (
        fox_q_norm, fox_k_norm, rwkv_w0, rwkv_a0, rwkv_k_k, rwkv_k_a, rwkv_r_k, rwkv_ln_g,
        rwkv_ln_b)] + [mu, fb, f(norm1_g)[0], f(norm2_g)[0]])
    d["ident"] = np.eye(P, dtype=np.float32)
    d["blockones"] = np.kron(np.eye(2), np.ones((HD, HD))).astype(np.float32)
    d["ones"] = np.ones((P, P), np.float32)
    d["mask"] = np.where(np.tril(np.ones((P, P), bool)), 0.0, MASKED).astype(np.float32)
    d["sel"] = np.repeat(np.eye(NH, dtype=np.float32)[:, :, None], 512, axis=2)
    d["wa_up"] = np.concatenate([f(rwkv_w_up)[0], f(rwkv_a_up)[0]])
    gu = f(rwkv_g_up)[0]
    d["g_up"] = np.stack([gu[:P], np.concatenate([z(32, W5), gu[P:], z(64, W5)])], axis=1)
    d["blockmean"] = d["blockones"] / HD
    d["reset"] = np.broadcast_to((np.arange(T) % C != 0).astype(np.float32), (P, T))
    s_, t_ = np.arange(C)[:, None], np.arange(C)[None, :]
    gram = np.concatenate([s_ < t_, s_ <= t_], axis=1).astype(np.float32)
    d["mgram"] = np.repeat(gram[:, None], NP4, axis=1)
    lev = [-((s_ // m % 2 == 1) & (t_ // m == s_ // m - 1)).astype(np.float32) for m in LEVELS + [1]]
    d["mlev"] = np.stack(lev + [lev[-1].T], axis=1)
    d["eye8"] = np.broadcast_to(np.eye(C, dtype=np.float32)[:, None, None], (C, 2, NP4, C))
    wb = np.stack([f(w_branch_fox)[0], f(w_branch_rwkv)[0]])
    d["w_branch"] = wb.reshape(2, NP4, P, D).transpose(2, 0, 1, 3)
    d["w_out"] = f(w_out)[0].reshape(KD, P, D).transpose(1, 0, 2)
    d["w_q"] = f(peer_w_q)[0].reshape(KD, P, 2 * PH, P).transpose(2, 1, 0, 3)
    d["subk"] = np.stack([f(peer_sub_k1)[0].T, f(peer_sub_k2)[0].T], axis=1)
    d["iota16"] = np.broadcast_to(np.arange(TOPK, dtype=np.float32), (P, TOPK))
    d["iota128"] = np.broadcast_to(np.arange(NK, dtype=np.float32), (P, NK))
    d["u"] = f(peer_u)[0].reshape(NCHUNK, P, KD, P).transpose(0, 3, 2, 1)
    d["v"] = f(peer_v)[0].reshape(NCHUNK, P, D)
    return {k: np.ascontiguousarray(v) for k, v in d.items()}


def kernel(**inputs):
    import concourse.bacc as bacc
    from concourse.bass_utils import run_bass_kernel_spmd as run

    arrays = layout(**inputs)
    nc = bacc.Bacc("TRN2", target_bir_lowering=False, num_devices=1)
    d = {k: nc.dram_tensor(f"in_{k}", v.shape, mybir.dt.from_np(v.dtype), kind="ExternalInput").ap()
         for k, v in arrays.items()}
    d["out"] = nc.dram_tensor("out", (SEQ, D), F32, kind="ExternalOutput").ap()
    build(nc, d)
    r = run(nc, [{f"in_{k}": v for k, v in arrays.items()}], core_ids=[0])
    return r.results[0]["out"].reshape(1, SEQ, D)
```

```python
from contextlib import ExitStack

import numpy as np

import concourse.bass as bass
from concourse import mybir

F32 = mybir.dt.float32
F32R = mybir.dt.float32r
BF16 = mybir.dt.bfloat16
U32 = mybir.dt.uint32
ALU = mybir.AluOpType
ACT = mybir.ActivationFunctionType
AX = mybir.AxisListType

P = 128
D = 1024
KD = D // P
N_META = 16
SEQ = 512
T = N_META + SEQ
TH = T // 2
HD = 64
NH = 8
W5 = NH * HD
NP4 = W5 // P
NQ = SEQ // P
CONSTS = ("ident", "blockones", "blockmean", "ones")
EPS = 1e-6
GN_EPS = 64e-5
MASKED = -1e30

ZQ, ZK, ZV, ZR, ZRK, ZRV = 0, 4, 8, 12, 16, 20
ZWA, ZGD, ZFG = 24, 25, 26
ZGF, ZGR = 27, 35
NZ = 43
GD2 = 160 - P

(C_QN, C_KN, C_W0, C_A0, C_KK, C_KA, C_RK, C_LG, C_LB) = [4 * i for i in range(9)]
C_MU = 36
C_FB = C_MU + 15
C_G1 = C_FB + 1
C_G2 = C_G1 + KD
NC_COLS = C_G2 + KD

C = 48
NCH = T // C
LEVELS = [2, 4, 8, 16, 32]

PH = 8
NK = 128
TOPK = 16
NCHUNK = 128
GROUP = 4


def matmul3(nc, out, a, b, start, stop):
    nc.tensor.matmul(out, a[0], b[0], start=start, stop=False)
    nc.tensor.matmul(out, a[1], b[0], start=False, stop=False)
    return nc.tensor.matmul(out, a[0], b[1], start=False, stop=stop)


def norm_and_project(nc, d, keep):
    cols, zT = keep["cols"], keep["zT"]
    with ExitStack() as ctx:
        def sb(name, shape, dt=F32):
            return ctx.enter_context(nc.sbuf_tensor(name, shape, dt))

        def sem(name):
            return ctx.enter_context(nc.semaphore(name))

        hT = sb("hT", [P, KD, T])
        sq = sb("sq", [P, KD, T])
        root = sb("root", [P, T])
        rstd = sb("rstd", [P, T])
        xh = sb("xh", [P, KD, T], F32R)
        xl = sb("xl", [P, KD, T], F32R)
        wraw = sb("wraw", [P, 3, KD, P])
        wh = sb("wh", [P, 3, KD, P], F32R)
        wl = sb("wl", [P, 3, KD, P], F32R)
        ps = ctx.enter_context(nc.psum_tensor("ps_z", [P, 6, 512], F32))
        ps_ms = ctx.enter_context(nc.psum_tensor("ps_ms", [P, 2, 512], F32))

        loaded = sem("loaded")
        squared = sem("squared")
        summed = sem("summed")
        rooted = sem("rooted")
        rstd_ready = sem("rstd_ready")
        scaled = sem("scaled")
        x_hi = sem("x_hi")
        x_lo = sem("x_lo")
        w_in = [sem(f"w_arrived{s}") for s in range(3)]
        w_hi = sem("w_hi")
        w_lo = sem("w_lo")
        z_done = sem("z_done")
        evac_a = sem("evac_a")
        evac_b = sem("evac_b")

        def loop(eng, tile):
            for n in range(3):
                tile(n, n % 3)
            with eng.Fori(3, 39, 3) as n0:
                for s in range(3):
                    tile(n0 + s, s)
            for n in range(39, NZ):
                tile(n, n % 3)

        def isn(n, k):
            return not isinstance(n, int) or n >= k

        block = ctx.enter_context(nc.Block())

        @block.sync
        def _(sp):
            sp.dma_start(hT[:], d["hT"]).then_inc(loaded, 16)
            sp.dma_start(cols[:], d["cols"]).then_inc(loaded, 16)
            for name in CONSTS:
                sp.dma_start(keep[name][:], d[name]).then_inc(loaded, 16)

            def tile(n, s):
                if isn(n, 3):
                    sp.wait_ge(w_lo, n - 2)
                sp.dma_start(wraw[:, s], d["w_z"][n]).then_inc(w_in[s], 16)
            loop(sp, tile)

        @block.scalar
        def _(act):
            act.wait_ge(loaded, 32 + 16 * len(CONSTS))
            for k in range(KD):
                nc.scalar.activation(sq[:, k], hT[:, k], ACT.Square).then_inc(squared, 1)
            act.wait_ge(summed, 1)
            nc.scalar.activation(root[:], ps_ms[:, :, 0:TH], ACT.Sqrt, bias=keep["eps"][:, 0:1],
                                 scale=1.0 / D).then_inc(rooted, 1)
            for k in range(KD):
                act.wait_ge(scaled, k + 1)
                nc.scalar.copy(xh[:, k], sq[:, k]).then_inc(x_hi, 1)

            def split(n, s):
                act.wait_ge(w_in[s], (n // 3) * 16 + 16 if isinstance(n, int) else
                            (n - s) * 16 // 3 + 16)
                if isn(n, 3):
                    act.wait_ge(z_done, n - 2)
                nc.scalar.copy(wh[:, s], wraw[:, s]).then_inc(w_hi, 1)

            def evac(n, s):
                act.wait_ge(z_done, n + 1)
                nc.scalar.copy(zT[:, n, 0:TH], ps[:, 2 * s, 0:TH]).then_inc(evac_a, 1)

            split(0, 0)
            split(1, 1)
            evac(0, 0)
            split(2, 2)
            evac(1, 1)
            with act.Fori(3, 39, 3) as n0:
                for s in range(3):
                    split(n0 + s, s)
                    evac(n0 + (s - 1), (s - 1) % 3)
            for n in range(39, NZ):
                split(n, n % 3)
                evac(n - 1, (n - 1) % 3)
            evac(NZ - 1, (NZ - 1) % 3)

        @block.vector
        def _(dve):
            dve.wait_ge(rooted, 1)
            nc.vector.reciprocal(rstd[:], root[:]).then_inc(rstd_ready, 1)
            dve.wait_ge(rstd_ready, 1)
            for k in range(KD):
                nc.vector.scalar_tensor_tensor(out=sq[:, k], in0=hT[:, k], scalar=cols[:, C_G1 + k:C_G1 + k + 1],
                                               in1=rstd[:], op0=ALU.mult, op1=ALU.mult).then_inc(scaled, 1)
            for k in range(KD):
                dve.wait_ge(x_hi, k + 1)
                nc.vector.tensor_tensor(xl[:, k], sq[:, k], xh[:, k].bitcast(F32), ALU.subtract).then_inc(x_lo, 1)

            def split(n, s):
                dve.wait_ge(w_hi, n + 1)
                nc.vector.tensor_tensor(wl[:, s], wraw[:, s], wh[:, s].bitcast(F32), ALU.subtract).then_inc(w_lo, 1)

            def evac(n, s):
                dve.wait_ge(z_done, n + 1)
                nc.vector.tensor_copy(zT[:, n, TH:T], ps[:, 2 * s + 1, 0:TH]).then_inc(evac_b, 1)

            split(0, 0)
            split(1, 1)
            evac(0, 0)
            split(2, 2)
            evac(1, 1)
            with dve.Fori(3, 39, 3) as n0:
                for s in range(3):
                    split(n0 + s, s)
                    evac(n0 + (s - 1), (s - 1) % 3)
            for n in range(39, NZ):
                split(n, n % 3)
                evac(n - 1, (n - 1) % 3)
            evac(NZ - 1, (NZ - 1) % 3)

        @block.tensor
        def _(pe):
            pe.wait_ge(loaded, 32 + 16 * len(CONSTS))
            for k in range(KD):
                pe.wait_ge(squared, k + 1)
                for half in range(2):
                    mm = nc.tensor.matmul(ps_ms[:, half, 0:TH], keep["ones"][:], sq[:, k, half * TH:(half + 1) * TH],
                                          start=(k == 0), stop=(k == KD - 1))
            mm.then_inc(summed, 1)

            def tile(n, s):
                pe.wait_ge(w_lo, n + 1)
                if isn(n, 3):
                    pe.wait_ge(evac_a, n - 2)
                    pe.wait_ge(evac_b, n - 2)
                for k in range(KD):
                    if isinstance(n, int) and n == 0:
                        pe.wait_ge(x_lo, k + 1)
                    for half in range(2):
                        t = slice(half * TH, (half + 1) * TH)
                        mm = matmul3(nc, ps[:, 2 * s + half, 0:TH], (wh[:, s, k], wl[:, s, k]),
                                     (xh[:, k, t], xl[:, k, t]), k == 0, k == KD - 1)
                mm.then_inc(z_done, 1)
            loop(pe, tile)


class Chain:

    def __init__(self, eng, sem, base=0):
        self.eng, self.sem, self.base, self.n = eng, sem, base, 0

    def __call__(self, instruction):
        self.n += 1
        instruction.then_inc(self.sem, 1)
        self.eng.wait_ge(self.sem, self.base + self.n)


def fox_attention(nc, d, keep):
    zT, cols, yfT = keep["zT"], keep["cols"], keep["yfT"]
    UNITS = [(u // NQ, u % NQ) for u in range(2 * NQ)]
    NU = len(UNITS)
    DVE_STEPS = 2 + NU
    keys = [N_META + P * (i + 1) for i in range(NQ)]

    def pieces(a, b):
        return [(a, b)] if b <= 512 or a >= 512 else [(a, 512), (512, b)]

    with ExitStack() as ctx:
        def sb(name, shape, dt=F32):
            return ctx.enter_context(nc.sbuf_tensor(name, shape, dt))

        def sem(name):
            return ctx.enter_context(nc.semaphore(name))

        mask = sb("mask", [P, P])
        selall = sb("selall", [NH, NH, 512])
        sel = sb("sel", [NH, 2, 512])
        fg = sb("fg", [NH, 6, T])
        cum, ncum = fg[:, 4], fg[:, 5]
        sqk = sb("sqk", [P, 2, T])
        rqk = sb("rqk", [P, 2, T])
        qk = sb("qk", [P, 2, T])
        vT = sb("vT", [P, T])
        vtok = sb("vtok", [P, 5, P])
        pr = sb("pr", [P, 2, T])
        ptS = sb("ptS", [P, 2, 5, P])
        mx = sb("mx", [P, 2])
        nmx = sb("nmx", [P, 2])
        rsum = sb("rsum", [P, 2])
        rinv = sb("rinv", [P, 2])
        s_ps = ctx.enter_context(nc.psum_tensor("s_ps", [P, 2, 1024], F32))
        pt_ps = ctx.enter_context(nc.psum_tensor("pt_ps", [P, 1024], F32))
        pv_ps = ctx.enter_context(nc.psum_tensor("pv_ps", [P, 512], F32))

        loaded = sem("f_loaded")
        logit = sem("f_logit")
        softplus = sem("f_softplus")
        steps = sem("f_dve_steps")
        gate_steps = sem("f_gate_steps")
        act_steps = sem("f_act_steps")
        c_ready = sem("f_c_ready")
        squares = sem("f_squares")
        ms_done = sem("f_ms_done")
        roots = sem("f_roots")
        qk_ready = sem("f_qk_ready")
        sel_ready = sem("f_sel_ready")
        v_copied = sem("f_v_copied")
        v_turned = sem("f_v_turned")
        v_ready = sem("f_v_ready")
        scores = sem("f_scores")
        maxed = sem("f_maxed")
        expd = sem("f_expd")
        normed = sem("f_normed")
        turned = sem("f_turned")
        pt_ready = sem("f_pt_ready")
        pv_done = sem("f_pv_done")
        y_out = sem("f_y_out")

        block = ctx.enter_context(nc.Block())

        @block.sync
        def _(sp):
            sp.dma_start(mask[:], d["mask"]).then_inc(loaded, 16)
            sp.dma_start(selall[:], d["sel"]).then_inc(loaded, 16)

        @block.scalar
        def _(act):
            act.wait_ge(logit, 1)
            link = Chain(act, act_steps)
            link(nc.scalar.activation(fg[:, 1], fg[:, 0], ACT.Abs))
            link(nc.scalar.activation(fg[:, 1], fg[:, 1], ACT.Exp, scale=-1.0))
            nc.scalar.activation(fg[:, 2], fg[:, 1], ACT.Ln, bias=1.0).then_inc(softplus, 1)
            act.wait_ge(loaded, 32)
            with act.Fori(0, NP4) as it:
                act.wait_ge(pv_done, it * NU)
                for j, z0 in enumerate((ZQ, ZK)):
                    nc.scalar.activation(sqk[:, j], zT[:, it + z0], ACT.Square).then_inc(squares, 1)
                nc.scalar.copy(vT[:], zT[:, it + ZV]).then_inc(v_copied, 1)
                nc.scalar.copy(sel[:], selall[:, bass.ds(it * 2, 2)]).then_inc(sel_ready, 1)
                act.wait_ge(ms_done, it + 1)
                nc.scalar.activation(rqk[:, 0], s_ps[:, 0].rearrange("p (a b) -> p a b", a=2)[:, :, 0:TH], ACT.Sqrt,
                                     bias=keep["eps"][:, 1:2], scale=1.0).then_inc(roots, 1)
                nc.scalar.activation(rqk[:, 1], s_ps[:, 1].rearrange("p (a b) -> p a b", a=2)[:, :, 0:TH], ACT.Sqrt,
                                     bias=keep["eps"][:, 0:1], scale=1.0 / HD).then_inc(roots, 1)
                act.wait_ge(v_turned, it + 1)
                nc.scalar.copy(vtok[:, 0:4], pt_ps[:, 0:512]).then_inc(v_ready, 1)
                nc.scalar.copy(vtok[0:16, 4], pt_ps[0:16, 512:640]).then_inc(v_ready, 1)

                def exp(u):
                    n, b = keys[UNITS[u][1]], u % 2
                    act.wait_ge(maxed, it * NU + u + 1)
                    if u >= 2:
                        act.wait_ge(turned, it * NU + u - 1)
                        act.wait_ge(normed, it * NU + u - 1)
                    nc.scalar.activation(pr[:, b, 0:n], s_ps[:, b, 0:n], ACT.Exp, bias=nmx[:, b:b + 1],
                                         scale=1.0, accum_out=rsum[:, b:b + 1]).then_inc(expd, 1)

                def pt_out(u):
                    i, b = UNITS[u][1], u % 2
                    act.wait_ge(turned, it * NU + u + 1)
                    if u >= 2:
                        act.wait_ge(pv_done, it * NU + u - 1)
                    nc.scalar.copy(ptS[:, b, 0:i + 1], pt_ps[:, 0:P * (i + 1)]).then_inc(pt_ready, 1)
                    nc.scalar.copy(ptS[0:16, b, i + 1], pt_ps[0:16, 512:640]).then_inc(pt_ready, 1)

                exp(0)
                for u in range(NU):
                    if u + 1 < NU:
                        exp(u + 1)
                    pt_out(u)

        @block.vector
        def _(dve):
            link = Chain(dve, gate_steps)
            nc.vector.tensor_scalar(fg[:, 0], zT[0:NH, ZFG], cols[0:NH, C_FB:C_FB + 1], None,
                                    ALU.add).then_inc(logit, 1)
            dve.wait_ge(logit, 1)
            link(nc.vector.tensor_scalar(fg[:, 3], fg[:, 0], 0.0, None, ALU.min))
            dve.wait_ge(softplus, 1)
            link(nc.vector.tensor_tensor(fg[:, 3], fg[:, 3], fg[:, 2], ALU.subtract))
            link(nc.vector.memset(fg[:, 2], 0.0))
            link(nc.vector.tensor_tensor_scan(cum, fg[:, 3], fg[:, 2], 0.0, ALU.add, ALU.add))
            nc.vector.tensor_scalar(ncum, cum, -1.0, None, ALU.mult).then_inc(c_ready, 1)
            with dve.Fori(0, NP4) as it:
                link = Chain(dve, steps, it * DVE_STEPS)
                dve.wait_ge(roots, it * 2 + 2)
                for j, c0 in enumerate((C_QN, C_KN)):
                    link(nc.vector.reciprocal(rqk[:, j], rqk[:, j]))
                    nc.vector.scalar_tensor_tensor(out=qk[:, j], in0=zT[:, it + 4 * j], scalar=cols[:, bass.ds(it + c0, 1)],
                                                   in1=rqk[:, j], op0=ALU.mult, op1=ALU.mult).then_inc(qk_ready, 1)

                def row_max(u):
                    n, b = keys[UNITS[u][1]], u % 2
                    dve.wait_ge(scores, it * NU + u + 1)
                    nc.vector.reduce_max(nmx[:, b:b + 1], s_ps[:, b, 0:n], AX.X, negate=True).then_inc(maxed, 1)

                def norm(u):
                    n, b = keys[UNITS[u][1]], u % 2
                    dve.wait_ge(expd, it * NU + u + 1)
                    link(nc.vector.reciprocal(rinv[:, b:b + 1], rsum[:, b:b + 1]))
                    nc.vector.tensor_scalar(pr[:, b, 0:n], pr[:, b, 0:n], rinv[:, b:b + 1], None,
                                            ALU.mult).then_inc(normed, 1)

                row_max(0)
                for u in range(NU):
                    if u + 1 < NU:
                        row_max(u + 1)
                    norm(u)
                dve.wait_ge(pv_done, it * NU + NU)
                nc.vector.tensor_copy(yfT[:, it], pv_ps[:]).then_inc(y_out, 1)

        @block.tensor
        def _(pe):
            pe.wait_ge(loaded, 32)
            pe.wait_ge(c_ready, 1)
            with pe.Fori(0, NP4) as it:
                pe.wait_ge(expd, it * NU)
                pe.wait_ge(squares, it * 2 + 2)
                for j in range(2):
                    for half in range(2):
                        mm = nc.tensor.matmul(s_ps[:, j, half * 512:half * 512 + TH], keep["blockones"][:],
                                              sqk[:, j, half * TH:half * TH + TH], start=True, stop=True)
                mm.then_inc(ms_done, 1)
                pe.wait_ge(pt_ready, it * 2 * NU)
                pe.wait_ge(v_copied, it + 1)
                for j in range(4):
                    nc.tensor.transpose(pt_ps[:, j * P:j * P + P], vT[:, j * P:j * P + P], keep["ident"][:])
                nc.tensor.transpose(pt_ps[0:16, 512:640], vT[:, 512:T], keep["ident"][:]).then_inc(v_turned, 1)
                pe.wait_ge(roots, it * 2 + 2)
                pe.wait_ge(sel_ready, it + 1)
                pe.wait_ge(qk_ready, it * 2 + 2)

                def score(u):
                    (e, i), b = UNITS[u], u % 2
                    n, q0, r = keys[i], N_META + P * i, slice(e * HD, e * HD + HD)
                    if u >= 2:
                        pe.wait_ge(expd, it * NU + u - 1)
                    for x, y in pieces(0, n):
                        w = y - x
                        nc.tensor.matmul(s_ps[:, b, x:y], qk[r, 0, q0:q0 + P], qk[r, 1, x:y], start=True, stop=False)
                        x0 = max(x, n - P)
                        if x0 < y:
                            nc.tensor.matmul(s_ps[:, b, x0:y], keep["ident"][:], mask[:, x0 - (n - P):y - (n - P)],
                                             start=False, stop=False)
                        nc.tensor.matmul(s_ps[:, b, x:y], sel[:, e, 0:P], ncum[:, x:y], start=False, stop=False)
                        mm = nc.tensor.matmul(s_ps[:, b, x:y], cum[:, q0:q0 + P], sel[:, e, 0:w], start=False,
                                              stop=True)
                    mm.then_inc(scores, 1)

                def turn(u):
                    i, b = UNITS[u][1], u % 2
                    pe.wait_ge(normed, it * NU + u + 1)
                    pe.wait_ge(pt_ready, it * 2 * NU + 2 * u)
                    for j in range(i + 1):
                        nc.tensor.transpose(pt_ps[:, j * P:j * P + P], pr[:, b, j * P:j * P + P], keep["ident"][:])
                    nc.tensor.transpose(pt_ps[0:16, 512:640], pr[:, b, (i + 1) * P:(i + 1) * P + 16],
                                        keep["ident"][:]).then_inc(turned, 1)

                def values(u):
                    (e, i), b = UNITS[u], u % 2
                    out = pv_ps[e * HD:e * HD + HD, i * P:i * P + P]
                    pe.wait_ge(pt_ready, it * 2 * NU + 2 * u + 2)
                    for j in range(i + 2):
                        k = P if j <= i else 16
                        mm = nc.tensor.matmul(out, vtok[0:k, j, e * HD:e * HD + HD], ptS[0:k, b, j],
                                              start=(j == 0), stop=(j == i + 1))
                    mm.then_inc(pv_done, 1)

                score(0)
                score(1)
                pe.wait_ge(v_ready, it * 2 + 2)
                pe.wait_ge(y_out, it)
                for u in range(NU):
                    turn(u)
                    if u + 2 < NU:
                        score(u + 2)
                    values(u)


def rwkv_inputs(nc, d, keep):
    zT, cols = keep["zT"], keep["cols"]
    L, Lx, kk, ka, bonus, g = (keep[n] for n in ("L", "Lx", "kk", "ka", "bonus", "g"))
    NSH = 15
    with ExitStack() as ctx:
        def sb(name, shape, dt=F32):
            return ctx.enter_context(nc.sbuf_tensor(name, shape, dt))

        def sem(name):
            return ctx.enter_context(nc.semaphore(name))

        diff = sb("diff", [P, NSH, T])
        tanh_w = sb("tanh_w", [HD, T])
        wa_up = sb("wa_up", [P, W5])
        g_up = sb("g_up", [P, 2, W5])
        reset = sb("reset", [P, T])
        a = sb("a_rate", [P, 2, T])
        sq = sb("r_sq", [P, T])
        rk = sb("r_rk", [P, T])
        rn = sb("r_rn", [P, T])
        lora_ps = ctx.enter_context(nc.psum_tensor("lora_ps", [P, 3, 2, 512], F32))
        sum_ps = ctx.enter_context(nc.psum_tensor("sum_ps", [P, 2, 512], F32))

        loaded = sem("r_loaded")
        diffed = sem("r_diffed")
        shifted = sem("r_shifted")
        squashed = sem("r_squashed")
        lora_done = sem("r_lora_done")
        lora_out = sem("r_lora_out")
        kk_raw = sem("r_kk_raw")
        squared = sem("r_squared")
        summed = sem("r_summed")
        rooted = sem("r_rooted")
        rk_ready = sem("r_rk_ready")
        rk_summed = sem("r_rk_summed")
        bonus_out = sem("r_bonus_out")
        steps = sem("r_steps")
        block = ctx.enter_context(nc.Block())

        @block.sync
        def _(sp):
            sp.dma_start(wa_up[:], d["wa_up"]).then_inc(loaded, 16)
            sp.dma_start(g_up[:], d["g_up"]).then_inc(loaded, 16)
            sp.dma_start(reset[:], d["reset"]).then_inc(loaded, 16)

        @block.gpsimd
        def _(pool):
            def shift(i):
                z = zT[:, ZR + i]
                nc.gpsimd.tensor_tensor(diff[:, i, 0:1], keep["eps"][:, 3:4], z[:, 0:1], ALU.subtract).then_inc(diffed, 1)
                nc.gpsimd.tensor_tensor(diff[:, i, 1:T], z[:, 0:T - 1], z[:, 1:T], ALU.subtract).then_inc(diffed, 1)
            for i in range(12, NSH):
                shift(i)
            with pool.Fori(0, 12) as it:
                shift(it)

        @block.vector
        def _(dve):
            def shift(i, n):
                dve.wait_ge(diffed, n * 2 + 2)
                nc.vector.scalar_tensor_tensor(out=zT[:, ZR + i], in0=diff[:, i], scalar=cols[:, bass.ds(i + C_MU, 1)],
                                               in1=zT[:, ZR + i], op0=ALU.mult, op1=ALU.add).then_inc(shifted, 1)
            for i in range(12, NSH):
                shift(i, i - 12)
            with dve.Fori(0, 12) as it:
                shift(it, it + 3)
            link = Chain(dve, steps)
            dve.wait_ge(loaded, 48)
            dve.wait_ge(shifted, NSH)
            for m in range(NP4):
                def col(c):
                    return cols[:, c + m:c + m + 1]
                r, k, v = zT[:, ZR + m], zT[:, ZRK + m], zT[:, ZRV + m]
                nc.vector.tensor_scalar(kk[:, m], k, col(C_KK), None, ALU.mult).then_inc(kk_raw, 1)
                dve.wait_ge(lora_out, 3 * m + 3)
                link(nc.vector.tensor_scalar(Lx[:, m], L[:, m], -float(np.exp(-0.5)), None, ALU.mult))
                link(nc.vector.tensor_tensor_scan(L[:, m], reset[:], Lx[:, m], 0.0, ALU.mult, ALU.add))
                link(nc.vector.tensor_tensor(Lx[:, m], L[:, m], Lx[:, m], ALU.subtract))
                link(nc.vector.tensor_scalar(ka[:, m], a[:, m % 2], 1.0, col(C_KA), ALU.subtract, ALU.mult))
                link(nc.vector.scalar_tensor_tensor(out=k, in0=ka[:, m], scalar=1.0, in1=k, op0=ALU.add, op1=ALU.mult))
                if m >= 1:
                    dve.wait_ge(rk_summed, m)
                nc.vector.scalar_tensor_tensor(out=rk[:], in0=r, scalar=col(C_RK), in1=k, op0=ALU.mult,
                                               op1=ALU.mult).then_inc(rk_ready, 1)
                dve.wait_ge(rooted, m + 1)
                link(nc.vector.tensor_scalar(rn[:], rn[:], 1e-12, None, ALU.max))
                link(nc.vector.reciprocal(rn[:], rn[:]))
                link(nc.vector.tensor_tensor(kk[:, m], kk[:, m], rn[:], ALU.mult))
                link(nc.vector.tensor_tensor(ka[:, m], kk[:, m], a[:, m % 2], ALU.mult))
                dve.wait_ge(rk_summed, m + 1)
                nc.vector.tensor_tensor(bonus[:, m], sum_ps[:, :, 0:TH], v, ALU.mult).then_inc(bonus_out, 1)

        @block.scalar
        def _(act):
            act.wait_ge(shifted, 3)
            nc.scalar.activation(tanh_w[:], zT[0:HD, ZWA], ACT.Tanh).then_inc(squashed, 1)
            nc.scalar.activation(zT[:, ZGD], zT[:, ZGD], ACT.Sigmoid).then_inc(squashed, 1)
            nc.scalar.activation(zT[32:64, ZFG], zT[32:64, ZFG], ACT.Sigmoid).then_inc(squashed, 1)
            for m in range(NP4):
                act.wait_ge(lora_done, m + 1)
                if m >= 2:
                    act.wait_ge(bonus_out, m - 1)
                nc.scalar.activation(L[:, m], lora_ps[:, 0, :, 0:TH], ACT.Sigmoid,
                                     bias=cols[:, C_W0 + m:C_W0 + m + 1]).then_inc(lora_out, 1)
                nc.scalar.activation(a[:, m % 2], lora_ps[:, 1, :, 0:TH], ACT.Sigmoid,
                                     bias=cols[:, C_A0 + m:C_A0 + m + 1]).then_inc(lora_out, 1)
                nc.scalar.copy(g[:, m], lora_ps[:, 2, :, 0:TH]).then_inc(lora_out, 1)
                act.wait_ge(kk_raw, m + 1)
                nc.scalar.activation(sq[:], kk[:, m], ACT.Square).then_inc(squared, 1)
                act.wait_ge(summed, m + 1)
                nc.scalar.activation(rn[:], sum_ps[:, :, 0:TH], ACT.Sqrt).then_inc(rooted, 1)

        @block.tensor
        def _(pe):
            pe.wait_ge(loaded, 48)
            pe.wait_ge(squashed, 3)
            for m in range(NP4):
                c = slice(m * P, m * P + P)
                if m >= 1:
                    pe.wait_ge(lora_out, 3 * m)
                for half in range(2):
                    t = slice(half * TH, half * TH + TH)
                    nc.tensor.matmul(lora_ps[:, 0, half, 0:TH], wa_up[0:HD, c], tanh_w[:, t], start=True, stop=True)
                    nc.tensor.matmul(lora_ps[:, 1, half, 0:TH], wa_up[HD:P, c], zT[HD:P, ZWA, t], start=True, stop=True)
                    nc.tensor.matmul(lora_ps[:, 2, half, 0:TH], g_up[:, 0, c], zT[:, ZGD, t], start=True, stop=False)
                    mm = nc.tensor.matmul(lora_ps[:, 2, half, 0:TH], g_up[32:64, 1, c], zT[32:64, ZFG, t], start=False,
                                          stop=True)
                mm.then_inc(lora_done, 1)
                if m >= 1:
                    pe.wait_ge(bonus_out, m)
                for x, ready, done in ((sq, squared, summed), (rk, rk_ready, rk_summed)):
                    pe.wait_ge(ready, m + 1)
                    if x is rk:
                        pe.wait_ge(rooted, m + 1)
                    for half in range(2):
                        mm = nc.tensor.matmul(sum_ps[:, half, 0:TH], keep["blockones"][:],
                                              x[:, half * TH:half * TH + TH], start=True, stop=True)
                    mm.then_inc(done, 1)


def rwkv_recurrence(nc, d, keep):
    zT, L, Lx, kk, ka, yT = (keep[n] for n in ("zT", "L", "Lx", "kk", "ka", "yT"))
    NLEV = len(LEVELS)
    with ExitStack() as ctx:
        def sb(name, shape, dt=F32):
            return ctx.enter_context(nc.sbuf_tensor(name, shape, dt))

        def sem(name):
            return ctx.enter_context(nc.semaphore(name))

        mgram = sb("mgram", [C, NP4, 2 * C])
        mlev = sb("mlev", [C, NLEV + 2, C])
        eye8 = sb("eye8", [C, 2, NP4, C])
        ex = sb("ex", [P, 2, 3, NP4, C])
        ar = sb("ar", [P, 2, NP4, 2, C])
        bt = sb("bt", [P, 2, NP4, C])
        kt = sb("kt", [P, 2, NP4, C])
        vt = sb("vt", [P, 2, NP4, C])
        mb = sb("mb", [C, 2, 2, NP4, 2 * C])
        mk = sb("mk", [C, 2, 2, NP4, 2 * C])
        inv = sb("inv", [C, 2, 2, 2, NP4, C])
        off = sb("off", [C, 2, 4, C])
        toks = sb("toks", [C, 2, 3, W5])
        rhs = sb("rhs", [C, W5])
        nu = sb("nu", [C, W5])
        ST = sb("ST", [P, NP4, P])
        ps = ctx.enter_context(nc.psum_tensor("r_ps", [P, 8, 512], F32))

        loaded = sem("k_loaded")
        zeroed = sem("k_zeroed")
        exps = sem("k_exps")
        scaled = sem("k_scaled")
        gram = sem("k_gram")
        masked = sem("k_masked")
        inv1 = sem("k_inv1")
        turned = sem("k_turned")
        tok_out = sem("k_tok_out")
        offs = sem("k_offs")
        off_out = sem("k_off_out")
        grown = sem("k_grown")
        grown_out = sem("k_grown_out")
        steps = sem("k_steps")
        passed = sem("k_passed")
        rhs_done = sem("k_rhs_done")
        rhs_out = sem("k_rhs_out")
        u_done = sem("k_u_done")
        u_out = sem("k_u_out")
        y_done = sem("k_y_done")
        y_out = sem("k_y_out")
        s_done = sem("k_s_done")
        s_add = sem("k_s_add")
        s_out = sem("k_s_out")
        block = ctx.enter_context(nc.Block())
        NSTEP = 4

        def order(eng, prepare, level, recur):
            def both(c, b):
                prepare(c, b)
                for lv in range(NLEV):
                    level(c, b, lv)
                    if not (isinstance(c, int) and c == 0):
                        recur(c - 1, 1 - b, lv)
            both(0, 0)
            with eng.Fori(1, NCH - 1, 2) as c:
                both(c, 1)
                both(c + 1, 0)
            for lv in range(NLEV):
                recur(NCH - 1, 0, lv)

        def isn(c, k):
            return not isinstance(c, int) or c >= k

        @block.sync
        def _(sp):
            sp.dma_start(mgram[:], d["mgram"]).then_inc(loaded, 16)
            sp.dma_start(mlev[:], d["mlev"]).then_inc(loaded, 16)
            sp.dma_start(eye8[:], d["eye8"]).then_inc(loaded, 16)

        @block.scalar
        def _(act):
            def prepare(c, b):
                t = bass.ds(c * C, C)
                if isn(c, 2):
                    act.wait_ge(s_out, 2 * c - 2)
                    act.wait_ge(turned, 3 * c - 3)
                nc.scalar.activation(ex[:, b, 0], L[:, :, t], ACT.Exp).then_inc(exps, 1)
                nc.scalar.activation(ex[:, b, 1], L[:, :, t], ACT.Exp, scale=-1.0).then_inc(exps, 1)
                nc.scalar.activation(ex[:, b, 2], Lx[:, :, t], ACT.Exp).then_inc(exps, 1)
                nc.scalar.copy(vt[:, b], zT[:, ZRV:ZRV + 4, t]).then_inc(exps, 1)
                for j, bank in enumerate((6, 7, 0)):
                    act.wait_ge(turned, 3 * c + j + 1)
                    nc.scalar.copy(toks[:, b, j], ps[0:C, bank]).then_inc(tok_out, 1)

            def level(c, b, lv):
                pass

            def recur(c, b, lv):
                if lv == 0:
                    act.wait_ge(rhs_done, c + 1)
                    nc.scalar.copy(rhs[:], ps[0:C, 6]).then_inc(rhs_out, 1)
                if lv == 1:
                    act.wait_ge(u_done, c + 1)
                    nc.scalar.mul(nu[:], ps[0:C, 1], -1.0).then_inc(u_out, 1)
            order(act, prepare, level, recur)

        @block.vector
        def _(dve):
            dve.wait_ge(loaded, 48)
            nc.vector.memset(ST[:], 0.0).then_inc(zeroed, 1)
            dve.wait_ge(zeroed, 1)

            def prepare(c, b):
                t = bass.ds(c * C, C)
                dve.wait_ge(exps, 4 * c + 4)
                if isn(c, 2):
                    dve.wait_ge(y_done, c - 1)
                nc.vector.tensor_tensor(bt[:, b], ex[:, b, 1], ka[:, :, t], ALU.mult).then_inc(scaled, 1)
                nc.vector.tensor_tensor(ar[:, b, :, 0], ex[:, b, 2], kk[:, :, t], ALU.mult).then_inc(scaled, 1)
                nc.vector.tensor_tensor(ar[:, b, :, 1], ex[:, b, 0], zT[:, ZR:ZR + 4, t], ALU.mult).then_inc(scaled, 1)
                nc.vector.tensor_tensor(kt[:, b], ex[:, b, 1], zT[:, ZRK:ZRK + 4, t], ALU.mult).then_inc(scaled, 1)
                for j, m in enumerate((mb, mk)):
                    dve.wait_ge(gram, 3 * c + j + 1)
                    for e in range(2):
                        nc.vector.tensor_tensor(m[:, b, e], ps[0:C, 2 * j + e, 0:384].rearrange("p (a b) -> p a b", a=4),
                                                mgram[:], ALU.mult).then_inc(masked, 1)
                dve.wait_ge(gram, 3 * c + 3)
                dve.wait_ge(masked, 4 * c + 2)
                link = Chain(dve, steps, c * NSTEP)
                for e in range(2):
                    link(nc.vector.tensor_tensor(inv[:, b, e, 0], ps[0:C, 4 + e, 0:192].rearrange("p (a b) -> p a b", a=4),
                                                 mlev[:, NLEV:NLEV + 1].broadcast_to([C, 4, C]), ALU.mult))
                    link(nc.vector.tensor_tensor(inv[:, b, e, 1], mb[:, b, e, :, 0:C],
                                                 mlev[:, NLEV + 1:NLEV + 2].broadcast_to([C, 4, C]), ALU.mult))
                for e in range(2):
                    nc.vector.tensor_tensor(inv[:, b, e], inv[:, b, e], eye8[:], ALU.add).then_inc(inv1, 1)

            def level(c, b, lv):
                n = c * NLEV + lv
                for h in range(2):
                    dve.wait_ge(offs, n * 2 + h + 1)
                    nc.vector.tensor_tensor(off[:, h], ps[0:C, 2 + h, 0:192].rearrange("p (a b) -> p a b", a=4),
                                            mlev[:, lv:lv + 1].broadcast_to([C, 4, C]), ALU.mult).then_inc(off_out, 1)
                for h in range(2):
                    dve.wait_ge(grown, n * 2 + h + 1)
                    nc.vector.tensor_tensor(inv[:, b, h], inv[:, b, h],
                                            ps[0:C, 4 + h, 0:384].rearrange("p (x a b) -> p x a b", x=2, a=4),
                                            ALU.add).then_inc(grown_out, 1)

            def recur(c, b, lv):
                if lv == 3:
                    dve.wait_ge(s_done, c + 1)
                    dve.wait_ge(y_done, c + 1)
                    for e in range(2):
                        r, o = slice(e * HD, e * HD + HD), slice(e * HD, e * HD + HD)
                        nc.vector.tensor_tensor(ST[r, :, o], ps[r, 7, 256:512].rearrange("p (a b) -> p a b", a=NP4),
                                                ST[r, :, o], ALU.add).then_inc(s_add, 1)
                    for e in range(2):
                        r, o = slice(e * HD, e * HD + HD), slice(e * HD, e * HD + HD)
                        dve.wait_ge(s_add, 2 * c + e + 1)
                        nc.vector.tensor_tensor(ST[r, :, o], ST[r, :, o],
                                                ex[r, b, 0, :, C - 1:C].broadcast_to([HD, NP4, HD]),
                                                ALU.mult).then_inc(s_out, 1)
                    nc.vector.tensor_copy(yT[:, :, bass.ds(c * C, C)],
                                          ps[:, 7, 0:NP4 * C].rearrange("p (a b) -> p a b", a=NP4)).then_inc(y_out, 1)
            order(dve, prepare, level, recur)

        @block.tensor
        def _(pe):
            pe.wait_ge(loaded, 48)
            pe.wait_ge(zeroed, 1)

            def alone():
                pe.sem_inc(passed, 1)

            def head(h):
                return h // 2, slice(h % 2 * HD, h % 2 * HD + HD)

            def prepare(c, b):
                pe.wait_ge(scaled, 4 * c + 3)
                if isn(c, 1):
                    pe.wait_ge(grown_out, c * 2 * NLEV)
                    pe.wait_ge(tok_out, 3 * c)
                if isn(c, 2):
                    pe.wait_ge(u_out, c - 1)
                alone()
                for h in range(NH):
                    p, r = head(h)
                    mm = nc.tensor.matmul(ps[0:C, h % 2, p * 96:p * 96 + 96], bt[r, b, p], ar[r, b, p],
                                          start=True, stop=True)
                mm.then_inc(gram, 1)
                pe.wait_ge(scaled, 4 * c + 4)
                alone()
                for h in range(NH):
                    p, r = head(h)
                    mm = nc.tensor.matmul(ps[0:C, 2 + h % 2, p * 96:p * 96 + 96], kt[r, b, p], ar[r, b, p],
                                          start=True, stop=True)
                mm.then_inc(gram, 1)
                for h in range(NH):
                    p, r = head(h)
                    mm = nc.tensor.matmul(ps[0:C, 4 + h % 2, p * C:p * C + C], ar[r, b, p, 0], bt[r, b, p],
                                          start=True, stop=True)
                mm.then_inc(gram, 1)
                if isn(c, 2):
                    pe.wait_ge(rhs_out, c - 1)
                    pe.wait_ge(y_out, c - 1)
                    pe.wait_ge(s_add, 2 * c - 2)
                alone()
                for j, (x, bank) in enumerate(((kt, 6), (bt, 7), (vt, 0))):
                    if j == 2:
                        pe.wait_ge(exps, 4 * c + 4)
                        pe.wait_ge(masked, 4 * c + 2)
                    alone()
                    for p in range(NP4):
                        mm = nc.tensor.transpose(ps[0:C, bank, p * P:p * P + P], x[:, b, p], keep["ident"][:])
                    mm.then_inc(turned, 1)

            def level(c, b, lv):
                n = c * NLEV + lv
                if lv == 0:
                    pe.wait_ge(inv1, 2 * c + 2)
                    pe.wait_ge(masked, 4 * c + 4)
                alone()
                for e in range(2):
                    if lv >= 1:
                        pe.wait_ge(grown_out, n * 2 + e - 1)
                    alone()
                    for i in range(NP4):
                        mm = nc.tensor.matmul(ps[0:C, 2 + e, i * C:i * C + C], mb[:, b, e, i, 0:C],
                                              inv[:, b, e, 0, i], start=True, stop=True)
                    mm.then_inc(offs, 1)
                for e in range(2):
                    pe.wait_ge(off_out, n * 2 + e + 1)
                    alone()
                    for i in range(NP4):
                        nc.tensor.matmul(ps[0:C, 4 + e, i * C:i * C + C], inv[:, b, e, 1, i], off[:, e, i],
                                         start=True, stop=True)
                        mm = nc.tensor.matmul(ps[0:C, 4 + e, 192 + i * C:192 + i * C + C], off[:, e, i],
                                              inv[:, b, e, 1, i], start=True, stop=True)
                    mm.then_inc(grown, 1)

            def recur(c, b, lv):
                if lv == 0:
                    pe.wait_ge(s_out, 2 * c)
                    pe.wait_ge(grown_out, (c + 1) * 2 * NLEV)
                    pe.wait_ge(tok_out, 3 * NCH if isinstance(c, int) else 3 * c + 6)
                    alone()
                    for p in range(NP4):
                        nc.tensor.matmul(ps[0:C, 6, p * P:p * P + P], ar[:, b, p, 0], ST[:, p], start=(p == 0),
                                         stop=False, skip_group_check=True)
                    for h in range(NH):
                        mm = nc.tensor.matmul(ps[0:C, 6, h * HD:h * HD + HD], mk[:, b, h % 2, h // 2, 0:C],
                                              toks[:, b, 2, h * HD:h * HD + HD], start=False, stop=True,
                                              skip_group_check=True)
                    mm.then_inc(rhs_done, 1)
                if lv == 1:
                    pe.wait_ge(rhs_out, c + 1)
                    alone()
                    for h in range(NH):
                        mm = nc.tensor.matmul(ps[0:C, 1, h * HD:h * HD + HD], inv[:, b, h % 2, 1, h // 2],
                                              rhs[:, h * HD:h * HD + HD], start=True, stop=True)
                    mm.then_inc(u_done, 1)
                if lv == 2:
                    pe.wait_ge(u_out, c + 1)
                    pe.wait_ge(y_out, c)
                    alone()
                    for h in range(NH):
                        p, r = head(h)
                        c64 = slice(h * HD, h * HD + HD)
                        o = ps[r, 7, 256 + p * HD:256 + p * HD + HD]
                        nc.tensor.matmul(o, toks[:, b, 0, c64], toks[:, b, 2, c64], start=True, stop=False)
                        mm = nc.tensor.matmul(o, toks[:, b, 1, c64], nu[:, c64], start=False, stop=True)
                    mm.then_inc(s_done, 1)
                    for p in range(NP4):
                        nc.tensor.matmul(ps[:, 7, p * C:p * C + C], ST[:, p], ar[:, b, p, 1], start=(p == 0),
                                         stop=False, skip_group_check=True)
                    for h in range(NH):
                        p, r = head(h)
                        c64 = slice(h * HD, h * HD + HD)
                        o = ps[r, 7, p * C:p * C + C]
                        nc.tensor.matmul(o, toks[:, b, 2, c64], mk[:, b, h % 2, p, C:2 * C], start=False, stop=False,
                                         skip_group_check=True)
                        mm = nc.tensor.matmul(o, nu[:, c64], mb[:, b, h % 2, p, C:2 * C], start=False, stop=True,
                                              skip_group_check=True)
                    mm.then_inc(y_done, 1)

            order(pe, prepare, level, recur)


def rwkv_output(nc, d, keep):
    cols, yT, bonus, g, yrT = (keep[n] for n in ("cols", "yT", "bonus", "g", "yrT"))
    X = slice(N_META, T)
    with ExitStack() as ctx:
        def sb(name, shape, dt=F32):
            return ctx.enter_context(nc.sbuf_tensor(name, shape, dt))

        def sem(name):
            return ctx.enter_context(nc.semaphore(name))

        yc = sb("o_yc", [P, NP4, SEQ])
        sq = sb("o_sq", [P, NP4, SEQ])
        rt = sb("o_rt", [P, NP4, SEQ])
        ps = ctx.enter_context(nc.psum_tensor("o_ps", [P, 8, 512], F32))
        mean, centred, squared, var, rooted, steps = (sem("o_" + n) for n in (
            "mean", "centred", "squared", "var", "rooted", "steps"))
        block = ctx.enter_context(nc.Block())

        @block.tensor
        def _(pe):
            for m in range(NP4):
                nc.tensor.matmul(ps[:, m], keep["blockmean"][:], yT[:, m, X], start=True, stop=True).then_inc(mean, 1)
            for m in range(NP4):
                pe.wait_ge(squared, m + 1)
                nc.tensor.matmul(ps[:, 4 + m], keep["blockmean"][:], sq[:, m], start=True, stop=True).then_inc(var, 1)

        @block.scalar
        def _(act):
            for m in range(NP4):
                act.wait_ge(centred, m + 1)
                nc.scalar.activation(sq[:, m], yc[:, m], ACT.Square).then_inc(squared, 1)
            for m in range(NP4):
                act.wait_ge(var, m + 1)
                nc.scalar.activation(rt[:, m], ps[:, 4 + m], ACT.Sqrt, bias=keep["eps"][:, 2:3]).then_inc(rooted, 1)

        @block.vector
        def _(dve):
            link = Chain(dve, steps)
            for m in range(NP4):
                dve.wait_ge(mean, m + 1)
                nc.vector.tensor_tensor(yc[:, m], yT[:, m, X], ps[:, m], ALU.subtract).then_inc(centred, 1)
            for m in range(NP4):
                def col(c):
                    return cols[:, c + m:c + m + 1]
                dve.wait_ge(rooted, m + 1)
                link(nc.vector.reciprocal(rt[:, m], rt[:, m]))
                link(nc.vector.tensor_tensor(yc[:, m], yc[:, m], rt[:, m], ALU.mult))
                link(nc.vector.tensor_scalar(yc[:, m], yc[:, m], col(C_LG), col(C_LB), ALU.mult, ALU.add))
                link(nc.vector.tensor_tensor(yc[:, m], yc[:, m], bonus[:, m, X], ALU.add))
                link(nc.vector.tensor_tensor(yrT[:, m], yc[:, m], g[:, m, X], ALU.mult))


def branches_and_residual(nc, d, keep):
    cols, zT, yfT, yrT, acc = (keep[n] for n in ("cols", "zT", "yfT", "yrT", "acc"))
    X = slice(N_META, T)
    with ExitStack() as ctx:
        def sb(name, shape, dt=F32):
            return ctx.enter_context(nc.sbuf_tensor(name, shape, dt))

        def sem(name):
            return ctx.enter_context(nc.semaphore(name))

        wb = sb("wb", [P, 2, NP4, D])
        wo = sb("wo", [P, KD, D])
        part = sb("b_part", [P, 2, 2, SEQ])
        mixed = sb("mixed", [P, KD, SEQ])
        ps = ctx.enter_context(nc.psum_tensor("b_ps", [P, 8, 512], F32))
        loaded_b, loaded_o, x_loaded, gates, branch, parts, mixed_done, wout_done, h2_done = (sem("b_" + n) for n in (
            "loaded_b", "loaded_o", "x_loaded", "gates", "branch", "parts", "mixed", "wout", "h2"))
        block = ctx.enter_context(nc.Block())

        @block.sync
        def _(sp):
            sp.dma_start(wb[:], d["w_branch"]).then_inc(loaded_b, 16)
            sp.dma_start(wo[:], d["w_out"]).then_inc(loaded_o, 16)
            sp.dma_start(acc[:], d["x_tok"]).then_inc(x_loaded, 16)

        @block.scalar
        def _(act):
            for m in range(2 * KD):
                nc.scalar.activation(zT[:, ZGF + m, X], zT[:, ZGF + m, X], ACT.Sigmoid).then_inc(gates, 1)

        @block.tensor
        def _(pe):
            pe.wait_ge(loaded_b, 16)
            for m in range(KD):
                for br, y in enumerate((yfT, yrT)):
                    if m >= 2:
                        pe.wait_ge(parts, 2 * (m - 2) + br + 1)
                    for k in range(NP4):
                        mm = nc.tensor.matmul(ps[:, m % 2 * 2 + br], wb[:, br, k, m * P:m * P + P], y[:, k],
                                              start=(k == 0), stop=(k == NP4 - 1))
                    mm.then_inc(branch, 1)
            pe.wait_ge(loaded_o, 16)
            for i in range(NQ):
                for half in range(2):
                    n = 2 * i + half
                    if n >= 4:
                        pe.wait_ge(h2_done, n - 3)
                    for k in range(KD):
                        if n == 0:
                            pe.wait_ge(mixed_done, k + 1)
                        mm = nc.tensor.matmul(ps[:, 4 + n % 4], mixed[:, k, i * P:i * P + P],
                                              wo[:, k, half * 512:half * 512 + 512], start=(k == 0), stop=(k == KD - 1))
                    mm.then_inc(wout_done, 1)

        @block.vector
        def _(dve):
            for m in range(KD):
                for br in range(2):
                    dve.wait_ge(gates, KD * br + m + 1)
                    dve.wait_ge(branch, 2 * m + br + 1)
                    if m >= 2:
                        dve.wait_ge(mixed_done, m - 1)
                    nc.vector.tensor_tensor(part[:, m % 2, br], ps[:, m % 2 * 2 + br], zT[:, ZGF + KD * br + m, X],
                                            ALU.mult).then_inc(parts, 1)
                dve.wait_ge(parts, 2 * m + 2)
                nc.vector.tensor_tensor(mixed[:, m], part[:, m % 2, 0], part[:, m % 2, 1], ALU.add).then_inc(mixed_done, 1)
            dve.wait_ge(x_loaded, 16)
            for n in range(2 * NQ):
                dve.wait_ge(wout_done, n + 1)
                o = acc[:, n // 2, n % 2 * 512:n % 2 * 512 + 512]
                nc.vector.tensor_tensor(o, ps[:, 4 + n % 4], o, ALU.add).then_inc(h2_done, 1)


def second_norm(nc, d, keep):
    cols, acc, x2h, x2l = (keep[n] for n in ("cols", "acc", "x2h", "x2l"))
    with ExitStack() as ctx:
        def sb(name, shape, dt=F32):
            return ctx.enter_context(nc.sbuf_tensor(name, shape, dt))

        def sem(name):
            return ctx.enter_context(nc.semaphore(name))

        sq = sb("n_sq", [P, 2, D])
        ms = sb("n_ms", [P, 2, NQ])
        xn = sb("n_xn", [P, NQ, D])
        xT = sb("n_xT", [P, KD, SEQ])
        ps = ctx.enter_context(nc.psum_tensor("n_ps", [P, 8, 512], F32))
        squared, rooted, inverted, scaled, turned, gained, x_hi, x_lo, stored = (sem("n_" + n) for n in (
            "squared", "rooted", "inverted", "scaled", "turned", "gained", "x_hi", "x_lo", "stored"))
        block = ctx.enter_context(nc.Block())

        @block.sync
        def _(sp):
            sp.dma_start(keep["H2"], acc[:]).then_inc(stored, 16)
            sp.wait_ge(stored, 16)

        @block.scalar
        def _(act):
            for i in range(NQ):
                if i >= 2:
                    act.wait_ge(squared, i - 1)
                nc.scalar.activation(sq[:, i % 2], acc[:, i], ACT.Square, accum_out=ms[:, 0, i:i + 1]).then_inc(squared, 1)
            act.wait_ge(squared, NQ)
            nc.scalar.activation(ms[:, 1], ms[:, 0], ACT.Sqrt, bias=keep["eps"][:, 0:1], scale=1.0 / D).then_inc(rooted, 1)
            for k in range(KD):
                act.wait_ge(turned, k + 1)
                nc.scalar.activation(xT[:, k], ps[:, k], ACT.Copy, scale=cols[:, C_G2 + k:C_G2 + k + 1]).then_inc(gained, 1)
            for k in range(KD):
                act.wait_ge(gained, k + 1)
                nc.scalar.copy(x2h[:, k], xT[:, k]).then_inc(x_hi, 1)

        @block.vector
        def _(dve):
            dve.wait_ge(rooted, 1)
            nc.vector.reciprocal(ms[:, 0], ms[:, 1]).then_inc(inverted, 1)
            dve.wait_ge(inverted, 1)
            for i in range(NQ):
                nc.vector.tensor_scalar(xn[:, i], acc[:, i], ms[:, 0, i:i + 1], None, ALU.mult).then_inc(scaled, 1)
            for k in range(KD):
                dve.wait_ge(x_hi, k + 1)
                nc.vector.tensor_tensor(x2l[:, k], xT[:, k], x2h[:, k].bitcast(F32), ALU.subtract).then_inc(x_lo, 1)

        @block.tensor
        def _(pe):
            pe.wait_ge(scaled, NQ)
            for k in range(KD):
                for i in range(NQ):
                    mm = nc.tensor.transpose(ps[:, k, i * P:i * P + P], xn[:, i, k * P:k * P + P], keep["ident"][:])
                mm.then_inc(turned, 1)


def hidden_layer(nc, d, keep, sb, sem, count):
    first = keep["first"]
    x2h, x2l, HID = (keep[n] for n in ("x2h", "x2l", "HID"))
    uraw = sb("uraw", [P, 2, KD, P])
    uh = sb("uh", [P, 2, KD, P], F32R)
    ul = sb("ul", [P, 2, KD, P], F32R)
    hid = sb("hid", [P, 2, SEQ])
    h_ps = keep["h_ps"]
    u_in = [sem(f"u_arrived{s}") for s in range(2)]
    stored = [sem(f"hid_stored{s}") for s in range(2)]
    u_hi, u_lo, u_done, hid_out = (sem(n) for n in ("u_hi", "u_lo", "u_done", "hid_out"))

    def isn(m, k):
        return not isinstance(m, int) or m >= k

    def rounds(m, s):
        return (m // 2 + 1) * 16 if isinstance(m, int) else (m + (2 - s)) * 8

    def load(sp, m, s):
        if isn(m, 2):
            sp.wait_ge(u_lo, m - 1)
        sp.dma_start(uraw[:, s], d["u"][m + first]).then_inc(u_in[s], 16)

    def store(sp, m, s):
        sp.wait_ge(hid_out, m + 1)
        sp.dma_start(HID[m + first], hid[:, s]).then_inc(stored[s], 16)

    def split_hi(act, m, s):
        act.wait_ge(u_in[s], rounds(m, s))
        if isn(m, 2):
            act.wait_ge(u_done, m - 1)
        nc.scalar.copy(uh[:, s], uraw[:, s]).then_inc(u_hi, 1)

    def gelu(act, m, s):
        act.wait_ge(u_done, m + 1)
        if isn(m, 2):
            act.wait_ge(stored[s], rounds(m - 2, s))
        nc.scalar.activation(hid[:, s], h_ps[:, s], ACT.Gelu).then_inc(hid_out, 1)

    def split_lo(pool, m, s):
        pool.wait_ge(u_hi, m + 1)
        nc.gpsimd.tensor_tensor(ul[:, s], uraw[:, s], uh[:, s].bitcast(F32), ALU.subtract).then_inc(u_lo, 1)

    def product(pe, m, s):
        pe.wait_ge(u_lo, m + 1)
        if isn(m, 2):
            pe.wait_ge(hid_out, m - 1)
        for k in range(KD):
            mm = matmul3(nc, h_ps[:, s], (uh[:, s, k], ul[:, s, k]), (x2h[:, k], x2l[:, k]), k == 0, k == KD - 1)
        mm.then_inc(u_done, 1)

    def all_stored(sp):
        for s in range(2):
            sp.wait_ge(stored[s], count // 2 * 16)
    return load, store, split_hi, gelu, split_lo, product, all_stored


def peer_retrieval(nc, d, keep):
    x2h, x2l, picksT = (keep[n] for n in ("x2h", "x2l", "picksT"))
    NV = TOPK * TOPK
    UPH = 12
    with ExitStack() as ctx:
        def sb(name, shape, dt=F32):
            return ctx.enter_context(nc.sbuf_tensor("q_" + name, shape, dt))

        def sem(name):
            return ctx.enter_context(nc.semaphore("q_" + name))

        wraw = sb("wraw", [P, 2, KD, P])
        wh = sb("wh", [P, 2, KD, P], F32R)
        wl = sb("wl", [P, 2, KD, P], F32R)
        subk = sb("subk", [P, 2, NK])
        iota = sb("iota16", [P, TOPK])
        qT = sb("qT", [P, 2, SEQ])
        s = sb("s", [P, 2, NQ, NK])
        rest = sb("rest", [P, NQ, NK])
        top = sb("top", [P, 2, NQ, TOPK])
        idx = sb("idx", [P, 2, NQ, TOPK], U32)
        idxf = sb("idxf", [P, 2, NQ, TOPK])
        cand = sb("cand", [P, NQ, NV])
        crest = sb("crest", [P, NQ, NV])
        ctop = sb("ctop", [P, NQ, TOPK])
        cpos = sb("cpos", [P, NQ, TOPK], U32)
        cab = sb("cab", [P, 2, NQ, TOPK], U32)
        cabf = sb("cabf", [P, 2, NQ, TOPK])
        eq = sb("eq", [P, NQ, TOPK, TOPK])
        shifted = sb("shifted", [P, NQ, TOPK])
        gates = sb("gates", [P, NQ, TOPK])
        gsum = sb("gsum", [P, 2, NQ])
        picks = sb("picks", [P, 3, NQ, PH, TOPK])
        q_ps = ctx.enter_context(nc.psum_tensor("q_ps", [P, 2, 512], F32))
        s_ps = ctx.enter_context(nc.psum_tensor("qs_ps", [P, 2, 512], F32))
        keep["h_ps"] = ctx.enter_context(nc.psum_tensor("qh_ps", [P, 2, 512], F32))
        keep["first"] = 0
        load, store, split_hi, gelu, split_lo, product, all_stored = hidden_layer(nc, d, keep, sb, sem, PH * UPH)

        loaded = sem("loaded")
        w_in = [sem(f"w_arrived{b}") for b in range(2)]
        w_hi, w_lo, q_done, q_out, s_done, s_out, found, shift_done, exp_done, listed, turned, t_out, steps = (
            sem(n) for n in ("w_hi", "w_lo", "q_done", "q_out", "s_done", "s_out", "found", "shift_done",
                             "exp_done", "listed", "turned", "t_out", "steps"))
        block = ctx.enter_context(nc.Block())

        def heads(eng, head):
            head(0)
            with eng.Fori(1, PH - 1) as h:
                head(h)
            head(PH - 1)

        def chunks(eng, h, a, b, step):
            if isinstance(h, int) and h == 0 and a < 4:
                for m in range(a, 4):
                    step(m, m % 2)
                a = 4
            if a < b:
                with eng.Fori(a, b - 1, 2) as j:
                    for s in range(2):
                        step(h * UPH + j + s, s)

        @block.sync
        def _(sp):
            sp.dma_start(subk[:], d["subk"]).then_inc(loaded, 16)
            sp.dma_start(iota[:], d["iota16"]).then_inc(loaded, 16)
            for b in range(2):
                sp.dma_start(wraw[:, b], d["w_q"][b]).then_inc(w_in[b], 16)

            def both(m, s):
                load(sp, m, s)
                if not isinstance(m, int) or m >= 3:
                    store(sp, m - 3, 1 - s)

            def head(h):
                chunks(sp, h, 0, 6, both)
                if not isinstance(h, int) or h < PH - 1:
                    for b in range(2):
                        sp.wait_ge(w_lo, h * 2 + b + 1)
                        sp.dma_start(wraw[:, b], d["w_q"][h * 2 + b + 2]).then_inc(w_in[b], 16)
                chunks(sp, h, 6, UPH, both)
            heads(sp, head)
            for m in range(PH * UPH - 3, PH * UPH):
                store(sp, m, m % 2)
            all_stored(sp)

        @block.scalar
        def _(act):
            def split_w(h, b):
                act.wait_ge(w_in[b], h * 16 + 16)
                if not isinstance(h, int) or h > 0:
                    act.wait_ge(q_done, h * 2)
                nc.scalar.copy(wh[:, b], wraw[:, b]).then_inc(w_hi, 1)

            def head(h):
                for b in range(2):
                    act.wait_ge(q_done, h * 2 + b + 1)
                    if not isinstance(h, int) or h > 0:
                        act.wait_ge(s_done, h * 2)
                    nc.scalar.copy(qT[:, b], q_ps[:, b]).then_inc(q_out, 1)
                for b in range(2):
                    act.wait_ge(s_done, h * 2 + b + 1)
                    if not isinstance(h, int) or h > 0:
                        act.wait_ge(found, h * 2)
                    nc.scalar.copy(s[:, b], s_ps[:, b]).then_inc(s_out, 1)

                def step(m, sl):
                    if not (isinstance(m, int) and m + 1 == PH * UPH):
                        split_hi(act, m + 1, 1 - sl)
                    if not isinstance(m, int) or m >= 1:
                        gelu(act, m - 1, 1 - sl)
                chunks(act, h, 0, 4, step)
                if not isinstance(h, int) or h < PH - 1:
                    for b in range(2):
                        split_w(h + 1, b)
                chunks(act, h, 4, 10, step)
                act.wait_ge(shift_done, h + 1)
                nc.scalar.activation(gates[:], shifted[:], ACT.Exp).then_inc(exp_done, 1)
                if isinstance(h, int) and h == PH - 1:
                    for m in range(h * UPH + 10, h * UPH + UPH):
                        step(m, m % 2)
                else:
                    chunks(act, h, 10, UPH, step)
            for b in range(2):
                split_w(0, b)
            split_hi(act, 0, 0)
            heads(act, head)
            gelu(act, PH * UPH - 1, 1)
            act.wait_ge(turned, 3)
            for j, bank in enumerate((q_ps[:, 0], q_ps[:, 1], s_ps[:, 0])):
                nc.scalar.copy(picksT[:, j], bank).then_inc(t_out, 1)

        @block.gpsimd
        def _(pool):
            def split_w(h, b):
                pool.wait_ge(w_hi, h * 2 + b + 1)
                nc.gpsimd.tensor_tensor(wl[:, b], wraw[:, b], wh[:, b].bitcast(F32), ALU.subtract).then_inc(w_lo, 1)

            def head(h):
                def step(m, sl):
                    if not (isinstance(m, int) and m + 1 == PH * UPH):
                        split_lo(pool, m + 1, 1 - sl)
                chunks(pool, h, 0, 4, step)
                if not isinstance(h, int) or h < PH - 1:
                    for b in range(2):
                        split_w(h + 1, b)
                if isinstance(h, int) and h == PH - 1:
                    for m in range(h * UPH + 4, h * UPH + UPH):
                        step(m, m % 2)
                else:
                    chunks(pool, h, 4, UPH, step)
            for b in range(2):
                split_w(0, b)
            split_lo(pool, 0, 0)
            heads(pool, head)

        @block.vector
        def _(dve):
            link = Chain(dve, steps)
            for h in range(PH):
                for b in range(2):
                    dve.wait_ge(s_out, h * 2 + b + 1)
                    for i in range(NQ):
                        link(nc.vector.max(top[:, b, i, 0:8], s[:, b, i]))
                        link(nc.vector.match_replace(rest[:, i], top[:, b, i, 0:8], s[:, b, i], -3.0e38))
                        nc.vector.max_index(idx[:, b, i, 0:8], top[:, b, i, 0:8], s[:, b, i])
                        link(nc.vector.max(top[:, b, i, 8:16], rest[:, i]))
                        link(nc.vector.max_index(idx[:, b, i, 8:16], top[:, b, i, 8:16], rest[:, i]))
                    nc.vector.tensor_copy(idxf[:, b], idx[:, b]).then_inc(found, 1)
                    dve.wait_ge(found, h * 2 + b + 1)
                link(nc.vector.tensor_tensor(
                    cand[:].rearrange("p q (a b) -> p q a b", a=TOPK),
                    top[:, 0].unsqueeze(3).broadcast_to([P, NQ, TOPK, TOPK]),
                    top[:, 1].unsqueeze(2).broadcast_to([P, NQ, TOPK, TOPK]), ALU.add))
                for i in range(NQ):
                    link(nc.vector.max(ctop[:, i, 0:8], cand[:, i]))
                    link(nc.vector.match_replace(crest[:, i], ctop[:, i, 0:8], cand[:, i], -3.0e38))
                    nc.vector.max_index(cpos[:, i, 0:8], ctop[:, i, 0:8], cand[:, i])
                    link(nc.vector.max(ctop[:, i, 8:16], crest[:, i]))
                    link(nc.vector.max_index(cpos[:, i, 8:16], ctop[:, i, 8:16], crest[:, i]))
                nc.vector.tensor_tensor(shifted[:], ctop[:], ctop[:, :, 0:1].broadcast_to([P, NQ, TOPK]),
                                        ALU.subtract).then_inc(shift_done, 1)
                link(nc.vector.tensor_scalar(cab[:, 0], cpos[:], 4, None, ALU.logical_shift_right))
                link(nc.vector.tensor_scalar(cab[:, 1], cpos[:], 15, None, ALU.bitwise_and))
                link(nc.vector.tensor_copy(cabf[:], cab[:]))
                for j in range(2):
                    link(nc.vector.tensor_tensor(
                        eq[:], cabf[:, j].unsqueeze(3).broadcast_to([P, NQ, TOPK, TOPK]),
                        iota[:].unsqueeze(1).unsqueeze(1).broadcast_to([P, NQ, TOPK, TOPK]), ALU.is_equal))
                    link(nc.vector.tensor_tensor(eq[:], eq[:], idxf[:, j].unsqueeze(2).broadcast_to([P, NQ, TOPK, TOPK]),
                                                 ALU.mult))
                    link(nc.vector.reduce_sum(picks[:, j, :, h], eq[:], AX.X))
                dve.wait_ge(exp_done, h + 1)
                link(nc.vector.reduce_sum(gsum[:, 0], gates[:], AX.X))
                link(nc.vector.reciprocal(gsum[:, 1], gsum[:, 0]))
                nc.vector.tensor_tensor(picks[:, 2, :, h], gates[:],
                                        gsum[:, 1].unsqueeze(2).broadcast_to([P, NQ, TOPK]), ALU.mult).then_inc(listed, 1)
                dve.wait_ge(listed, h + 1)

        @block.tensor
        def _(pe):
            pe.wait_ge(loaded, 32)

            def head(h):
                later = not isinstance(h, int) or h > 0
                for b in range(2):
                    pe.wait_ge(w_lo, h * 2 + b + 1)
                    if later:
                        pe.wait_ge(q_out, h * 2)
                    for k in range(KD):
                        mm = matmul3(nc, q_ps[:, b], (wh[:, b, k], wl[:, b, k]), (x2h[:, k], x2l[:, k]), k == 0, k == KD - 1)
                    mm.then_inc(q_done, 1)
                for b in range(2):
                    pe.wait_ge(q_out, h * 2 + b + 1)
                    if later:
                        pe.wait_ge(s_out, h * 2)
                    for i in range(NQ):
                        mm = nc.tensor.matmul(s_ps[:, b, i * NK:i * NK + NK], qT[:, b, i * P:i * P + P], subk[:, b],
                                              start=True, stop=True)
                    mm.then_inc(s_done, 1)
                chunks(pe, h, 0, UPH, lambda m, sl: product(pe, m, sl))
            heads(pe, head)
            pe.wait_ge(listed, PH)
            for j, bank in enumerate((q_ps[:, 0], q_ps[:, 1], s_ps[:, 0])):
                for i in range(NQ):
                    mm = nc.tensor.transpose(bank[:, i * P:i * P + P],
                                             picks[:, j, i].rearrange("p h k -> p (h k)"), keep["ident"][:])
                mm.then_inc(turned, 1)


def gate_matrix(nc, d, keep):
    picksT, G = keep["picksT"], keep["G"]
    TB = 4
    NS = P // TB
    PER = 8
    NT = NQ * NS // PER
    COUNT = 2 * NT
    with ExitStack() as ctx:
        def sb(name, shape, dt=F32):
            return ctx.enter_context(nc.sbuf_tensor("g_" + name, shape, dt))

        def sem(name):
            return ctx.enter_context(nc.semaphore("g_" + name))

        iota = sb("iota128", [P, NK])
        hot1 = sb("hot1", [P, 2, TB, NK])
        hot2 = sb("hot2", [P, 2, TB, NK])
        stage = sb("stage", [P, 2, NK, P])
        ps = ctx.enter_context(nc.psum_tensor("g_ps", [P, 2, TB, NK], F32))
        keep["h_ps"] = ctx.enter_context(nc.psum_tensor("gh_ps", [P, 2, 512], F32))
        keep["first"] = NCHUNK - COUNT
        load, store, split_hi, gelu, split_lo, product, all_stored = hidden_layer(nc, d, keep, sb, sem, COUNT)
        loaded, hot, placed, staged = (sem(n) for n in ("loaded", "hot", "placed", "staged"))
        g_stored = [sem(f"stage_stored{b}") for b in range(2)]
        block = ctx.enter_context(nc.Block())

        def turns(eng, turn):
            turn(0)
            turn(1)
            with eng.Fori(2, NT - 1) as t:
                turn(t)
            turn(NT - 1)

        @block.sync
        def _(sp):
            sp.dma_start(iota[:], d["iota128"]).then_inc(loaded, 16)

            def turn(t):
                for s in range(2):
                    load(sp, 2 * t + s, s)
                    if not isinstance(t, int) or 2 * t + s >= 3:
                        store(sp, 2 * t + s - 3, 1 - s)
            turns(sp, turn)
            for m in range(COUNT - 3, COUNT):
                store(sp, m, m % 2)
            all_stored(sp)

        @block.gpsimd
        def _(pool):
            def turn(t):
                for s in range(2):
                    split_lo(pool, 2 * t + s, s)
            turns(pool, turn)

        @block.vector
        def _(dve):
            dve.wait_ge(loaded, 16)

            def step(n, b):
                if not isinstance(n, int) or n >= 2:
                    dve.wait_ge(placed, n - 1)
                for t in range(TB):
                    t1 = bass.ds(n * TB + t, 1)
                    nc.vector.tensor_scalar(hot1[:, b, t], iota[:], picksT[:, 0, t1], picksT[:, 2, t1],
                                            ALU.is_equal, ALU.mult).then_inc(hot, 1)
                    nc.vector.tensor_scalar(hot2[:, b, t], iota[:], picksT[:, 1, t1], None,
                                            ALU.is_equal).then_inc(hot, 1)
            for n in range(2):
                step(n, n)
            with dve.Fori(2, NQ * NS - 1, 2) as n:
                for b in range(2):
                    step(n + b, b)

        @block.tensor
        def _(pe):
            def turn(t):
                for s in range(2):
                    product(pe, 2 * t + s, s)
                    for i in range(PER // 2):
                        n, b = t * PER + s * (PER // 2) + i, i % 2
                        pe.wait_ge(hot, (n + 1) * 2 * TB)
                        if not isinstance(n, int) or n >= 2:
                            pe.wait_ge(staged, n - 1)
                        for j in range(TB):
                            mm = nc.tensor.matmul(ps[:, b, j], hot2[:, b, j], hot1[:, b, j], start=True, stop=True)
                        mm.then_inc(placed, 1)
            turns(pe, turn)

        @block.scalar
        def _(act):
            def turn(t, tile, r):
                for s in range(2):
                    m = 2 * t + s
                    if not (isinstance(t, int) and m + 1 >= COUNT):
                        split_hi(act, m + 1, 1 - s)
                    if not (isinstance(t, int) and m == 0):
                        gelu(act, m - 1, 1 - s)
                    for i in range(PER // 2):
                        n, b = s * (PER // 2) + i, i % 2
                        act.wait_ge(placed, t * PER + n + 1)
                        nc.scalar.copy(stage[:, tile % 2, :, bass.ds((r * PER + n) * TB, TB)].rearrange("p a t -> p t a"),
                                       ps[:, b]).then_inc(staged, 1)
            split_hi(act, 0, 0)
            for tile in range(NQ):
                t0 = tile * NT // NQ
                if tile >= 2:
                    act.wait_ge(g_stored[tile % 2], 16 * (tile // 2))
                turn(t0, tile, 0)
                if tile == 0:
                    turn(1, tile, 1)
                with act.Fori(2 if tile == 0 else 1, 3) as r:
                    turn(t0 + r, tile, r)
                turn(t0 + 3, tile, 3)
                act.wait_ge(staged, NS * (tile + 1))
                act.dma_start(G[:, :, tile * P:tile * P + P].rearrange("a b t -> b a t"),
                              stage[:, tile % 2]).then_inc(g_stored[tile % 2], 16)
            gelu(act, COUNT - 1, 1)
            for b in range(2):
                act.wait_ge(g_stored[b], 32)


def experts(nc, d, keep):
    acc, G, HID = (keep[n] for n in ("acc", "G", "HID"))
    NG = NCHUNK // GROUP
    NB = 2 * NQ
    with ExitStack() as ctx:
        def sb(name, shape, dt=F32):
            return ctx.enter_context(nc.sbuf_tensor(name, shape, dt))

        def sem(name):
            return ctx.enter_context(nc.semaphore(name))

        vraw = sb("vraw", [P, GROUP, D])
        vh = sb("vh", [P, 2, GROUP, D], F32R)
        vl = sb("vl", [P, 2, GROUP, D], F32R)
        gm = sb("gm", [P, GROUP, SEQ])
        hid = sb("e_hid", [P, GROUP, SEQ])
        wh = sb("e_wh", [P, 2, GROUP, SEQ], F32R)
        wl = sb("e_wl", [P, 2, GROUP, SEQ], F32R)
        o_ps = ctx.enter_context(nc.psum_tensor("eo_ps", [P, 8, 512], F32))
        v_in = [sem(f"e_v_arrived{s}") for s in range(GROUP)]
        g_in = [sem(f"e_g_arrived{s}") for s in range(GROUP)]
        acc_in, v_hi, v_lo, w_done, w_hi, w_lo, v_done, added, stored = (sem("e_" + n) for n in (
            "acc_in", "v_hi", "v_lo", "w_done", "w_hi", "w_lo", "v_done", "added", "stored"))
        block = ctx.enter_context(nc.Block())

        def groups(eng, group):
            group(0, 0)
            group(1, 1)
            with eng.Fori(2, NG - 3, 2) as g:
                group(g, 0)
                group(g + 1, 1)
            group(NG - 2, 0)
            group(NG - 1, 1)

        def isn(g, k):
            return not isinstance(g, int) or g >= k

        @block.sync
        def _(sp):
            sp.dma_start(acc[:], keep["H2"]).then_inc(acc_in, 16)

            def group(g, b):
                for s in range(GROUP):
                    n = g * GROUP + s
                    if isn(g, 1):
                        sp.wait_ge(v_lo, (g - 1) * GROUP + s + 1)
                        sp.wait_ge(w_lo, (g - 1) * GROUP + s + 1)
                    sp.dma_start(vraw[:, s], d["v"][n]).then_inc(v_in[s], 16)
                    sp.dma_start(gm[:, s], G[n]).then_inc(g_in[s], 16)
                    sp.dma_start(hid[:, s], HID[n]).then_inc(g_in[s], 16)
            groups(sp, group)
            sp.wait_ge(added, NG * NB)
            sp.dma_start(d["out"].rearrange("(i p) n -> p i n", p=P), acc[:]).then_inc(stored, 16)
            sp.wait_ge(stored, 16)

        @block.scalar
        def _(act):
            def group(g, b):
                for s in range(GROUP):
                    n = g * GROUP + s
                    act.wait_ge(v_in[s], (g + 1) * 16)
                    if isn(g, 2):
                        act.wait_ge(v_done, (g - 1) * NB)
                    nc.scalar.copy(vh[:, b, s], vraw[:, s]).then_inc(v_hi, 1)
                    act.wait_ge(w_done, n + 1)
                    nc.scalar.copy(wh[:, b, s], hid[:, s]).then_inc(w_hi, 1)
            groups(act, group)

        @block.gpsimd
        def _(pool):
            def group(g, b):
                for s in range(GROUP):
                    pool.wait_ge(v_hi, g * GROUP + s + 1)
                    nc.gpsimd.tensor_tensor(vl[:, b, s], vraw[:, s], vh[:, b, s].bitcast(F32), ALU.subtract).then_inc(v_lo, 1)
            groups(pool, group)

        @block.vector
        def _(dve):
            def add(g, o):
                dve.wait_ge(v_done, g * NB + o + 1)
                a = acc[:, o // 2, o % 2 * 512:o % 2 * 512 + 512]
                nc.vector.tensor_tensor(a, o_ps[:, o], a, ALU.add).then_inc(added, 1)

            def group(g, b):
                for s in range(GROUP):
                    n = g * GROUP + s
                    dve.wait_ge(g_in[s], (g + 1) * 32)
                    nc.vector.tensor_tensor(hid[:, s], hid[:, s], gm[:, s], ALU.mult).then_inc(w_done, 1)
                    dve.wait_ge(w_hi, n + 1)
                    nc.vector.tensor_tensor(wl[:, b, s], hid[:, s], wh[:, b, s].bitcast(F32), ALU.subtract).then_inc(w_lo, 1)
                    if isn(g, 1):
                        for o in range(s * NB // GROUP, (s + 1) * NB // GROUP):
                            add(g - 1, o)
            dve.wait_ge(acc_in, 16)
            groups(dve, group)
            for o in range(NB):
                add(NG - 1, o)

        @block.tensor
        def _(pe):
            def group(g, b):
                pe.wait_ge(w_lo, (g + 1) * GROUP)
                pe.wait_ge(v_lo, (g + 1) * GROUP)
                for o in range(NB):
                    i, half = o // 2, o % 2
                    if isn(g, 1):
                        pe.wait_ge(added, (g - 1) * NB + (o + 1))
                    for s in range(GROUP):
                        mm = matmul3(nc, o_ps[:, o], (wh[:, b, s, i * P:i * P + P], wl[:, b, s, i * P:i * P + P]),
                                     (vh[:, b, s, half * 512:half * 512 + 512], vl[:, b, s, half * 512:half * 512 + 512]),
                                     s == 0, s == GROUP - 1)
                    mm.then_inc(v_done, 1)
            groups(pe, group)


def build(nc, d, stop=99, tap=None):
    with ExitStack() as ctx:
        def sb(name, shape, dt=F32):
            return ctx.enter_context(nc.sbuf_tensor(name, shape, dt))
        keep = {}
        for name in CONSTS:
            keep[name] = sb(name, [P, P])
        keep["cols"] = sb("cols", [P, NC_COLS])
        keep["eps"] = sb("eps", [P, 8])
        EPS_COLS = [EPS, HD * EPS, GN_EPS, 0.0]
        with nc.Block() as block:
            @block.gpsimd
            def _(pool):
                for i, e in enumerate(EPS_COLS):
                    nc.gpsimd.memset(keep["eps"][:, i:i + 1], e)
        keep["G"] = nc.dram_tensor("G_scratch", (NK, NK, SEQ), F32, kind="Internal").ap()
        keep["HID"] = nc.dram_tensor("HID_scratch", (NCHUNK, P, SEQ), F32, kind="Internal").ap()
        keep["H2"] = nc.dram_tensor("H2_scratch", (P, NQ, D), F32, kind="Internal").ap()
        early = ctx.enter_context(ExitStack())
        keep["zT"] = early.enter_context(nc.sbuf_tensor("zT", [P, NZ, T], F32, side="right"))
        keep["yfT"] = early.enter_context(nc.sbuf_tensor("yfT", [P, NP4, SEQ], F32, side="right"))
        norm_and_project(nc, d, keep)
        if stop == 1: return tap(nc, keep)
        fox_attention(nc, d, keep)
        if stop == 2: return tap(nc, keep)
        with ExitStack() as rwkv:
            for name in ("bonus", "g", "L", "Lx", "kk", "ka"):
                keep[name] = rwkv.enter_context(nc.sbuf_tensor("r_" + name, [P, NP4, T], F32, side="right"))
            rwkv_inputs(nc, d, keep)
            if stop == 3: return tap(nc, keep)
            keep["yT"] = keep["zT"][:, ZQ:ZQ + NP4]
            rwkv_recurrence(nc, d, keep)
            if stop == 4: return tap(nc, keep)
            keep["yrT"] = keep["zT"][:, ZK:ZK + NP4, 0:SEQ]
            rwkv_output(nc, d, keep)
            if stop == 5: return tap(nc, keep)
        keep["acc"] = early.enter_context(nc.sbuf_tensor("acc", [P, NQ, D], F32, side="right"))
        branches_and_residual(nc, d, keep)
        if stop == 6: return tap(nc, keep)
        with ExitStack() as mid:
            keep["picksT"] = mid.enter_context(nc.sbuf_tensor("picksT", [P, 3, SEQ], F32))
            for name in ("x2h", "x2l"):
                keep[name] = mid.enter_context(nc.sbuf_tensor(name, [P, KD, SEQ], F32R))
            second_norm(nc, d, keep)
            early.close()
            peer_retrieval(nc, d, keep)
            if stop == 7: return tap(nc, keep)
            gate_matrix(nc, d, keep)
            if stop == 8: return tap(nc, keep)
        keep["acc"] = sb("acc2", [P, NQ, D])
        experts(nc, d, keep)


def _columns(vectors):
    return np.concatenate([v.reshape(-1, P).T for v in vectors], axis=1)


def layout(x, meta_tokens, norm1_g, w_in, fox_q_norm, fox_k_norm, fox_f_bias,
           rwkv_mu, rwkv_w0, rwkv_w_up, rwkv_a0, rwkv_a_up, rwkv_g_up, rwkv_k_k,
           rwkv_k_a, rwkv_r_k, rwkv_ln_g, rwkv_ln_b, w_branch_fox, w_branch_rwkv,
           w_out, norm2_g, peer_w_q, peer_sub_k1, peer_sub_k2, peer_u, peer_v):
    f = lambda a: np.asarray(a)
    x, meta = f(x)[0], f(meta_tokens)
    z = lambda *s: np.zeros(s, np.float32)
    d = {}
    h = np.concatenate([meta, x], axis=0)
    d["hT"] = h.T.reshape(KD, P, T).transpose(1, 0, 2)
    d["x_tok"] = x.reshape(NQ, P, D).transpose(1, 0, 2)
    w = f(w_in)[0]
    fox, rwkv, gates = w[:, :1544], w[:, 1544:1544 + 1824], w[:, 3368:]
    pad = lambda n: z(D, n)
    wz = np.concatenate([fox[:, :1536], rwkv[:, :1536], rwkv[:, 1536:1664], rwkv[:, 1664:1792],
                         fox[:, 1536:1544], pad(24), rwkv[:, 1792:1824], pad(64), gates], axis=1)
    d["w_z"] = wz.reshape(KD, P, NZ, P).transpose(2, 1, 0, 3)
    mu = f(rwkv_mu)[0]
    mu = np.concatenate([mu[:1792], z(32), mu[1792:1824], z(64)])
    fb = np.concatenate([f(fox_f_bias)[0], z(P - NH)])
    d["cols"] = _columns([f(a)[0].reshape(-1) for a in (
        fox_q_norm, fox_k_norm, rwkv_w0, rwkv_a0, rwkv_k_k, rwkv_k_a, rwkv_r_k, rwkv_ln_g,
        rwkv_ln_b)] + [mu, fb, f(norm1_g)[0], f(norm2_g)[0]])
    d["ident"] = np.eye(P, dtype=np.float32)
    d["blockones"] = np.kron(np.eye(2), np.ones((HD, HD))).astype(np.float32)
    d["ones"] = np.ones((P, P), np.float32)
    d["mask"] = np.where(np.tril(np.ones((P, P), bool)), 0.0, MASKED).astype(np.float32)
    d["sel"] = np.repeat(np.eye(NH, dtype=np.float32)[:, :, None], 512, axis=2)
    d["wa_up"] = np.concatenate([f(rwkv_w_up)[0], f(rwkv_a_up)[0]])
    gu = f(rwkv_g_up)[0]
    d["g_up"] = np.stack([gu[:P], np.concatenate([z(32, W5), gu[P:], z(64, W5)])], axis=1)
    d["blockmean"] = d["blockones"] / HD
    d["reset"] = np.broadcast_to((np.arange(T) % C != 0).astype(np.float32), (P, T))
    s_, t_ = np.arange(C)[:, None], np.arange(C)[None, :]
    gram = np.concatenate([s_ < t_, s_ <= t_], axis=1).astype(np.float32)
    d["mgram"] = np.repeat(gram[:, None], NP4, axis=1)
    lev = [-((s_ // m % 2 == 1) & (t_ // m == s_ // m - 1)).astype(np.float32) for m in LEVELS + [1]]
    d["mlev"] = np.stack(lev + [lev[-1].T], axis=1)
    d["eye8"] = np.broadcast_to(np.eye(C, dtype=np.float32)[:, None, None], (C, 2, NP4, C))
    wb = np.stack([f(w_branch_fox)[0], f(w_branch_rwkv)[0]])
    d["w_branch"] = wb.reshape(2, NP4, P, D).transpose(2, 0, 1, 3)
    d["w_out"] = f(w_out)[0].reshape(KD, P, D).transpose(1, 0, 2)
    d["w_q"] = f(peer_w_q)[0].reshape(KD, P, 2 * PH, P).transpose(2, 1, 0, 3)
    d["subk"] = np.stack([f(peer_sub_k1)[0].T, f(peer_sub_k2)[0].T], axis=1)
    d["iota16"] = np.broadcast_to(np.arange(TOPK, dtype=np.float32), (P, TOPK))
    d["iota128"] = np.broadcast_to(np.arange(NK, dtype=np.float32), (P, NK))
    d["u"] = f(peer_u)[0].reshape(NCHUNK, P, KD, P).transpose(0, 3, 2, 1)
    d["v"] = f(peer_v)[0].reshape(NCHUNK, P, D)
    return {k: np.ascontiguousarray(v) for k, v in d.items()}


def kernel(**inputs):
    import concourse.bacc as bacc
    from concourse.bass_utils import run_bass_kernel_spmd as run

    arrays = layout(**inputs)
    nc = bacc.Bacc("TRN2", target_bir_lowering=False, num_devices=1)
    d = {k: nc.dram_tensor(f"in_{k}", v.shape, mybir.dt.from_np(v.dtype), kind="ExternalInput").ap()
         for k, v in arrays.items()}
    d["out"] = nc.dram_tensor("out", (SEQ, D), F32, kind="ExternalOutput").ap()
    build(nc, d)
    r = run(nc, [{f"in_{k}": v for k, v in arrays.items()}], core_ids=[0])
    return r.results[0]["out"].reshape(1, SEQ, D)
```

```python
from contextlib import ExitStack

import numpy as np

import concourse.bass as bass
from concourse import mybir

F32 = mybir.dt.float32
F32R = mybir.dt.float32r
BF16 = mybir.dt.bfloat16
U32 = mybir.dt.uint32
ALU = mybir.AluOpType
ACT = mybir.ActivationFunctionType
AX = mybir.AxisListType

P = 128
D = 1024
KD = D // P
N_META = 16
SEQ = 512
T = N_META + SEQ
TH = T // 2
HD = 64
NH = 8
W5 = NH * HD
NP4 = W5 // P
NQ = SEQ // P
CONSTS = ("ident", "blockones", "blockmean", "ones")
EPS = 1e-6
GN_EPS = 64e-5
MASKED = -1e30

ZQ, ZK, ZV, ZR, ZRK, ZRV = 0, 4, 8, 12, 16, 20
ZWA, ZGD, ZFG = 24, 25, 26
ZGF, ZGR = 27, 35
NZ = 43
GD2 = 160 - P

(C_QN, C_KN, C_W0, C_A0, C_KK, C_KA, C_RK, C_LG, C_LB) = [4 * i for i in range(9)]
C_MU = 36
NSHIFT = 15
C_FB = C_MU + NSHIFT
C_G1 = C_FB + 1
C_G2 = C_G1 + KD
NC_COLS = C_G2 + KD

C = 48
NCH = T // C
LEVELS = [2, 4, 8, 16, 32]

PH = 8
NK = 128
TOPK = 16
NCHUNK = 128
GROUP = 4


def matmul3(nc, out, a, b, start, stop):
    nc.tensor.matmul(out, a[0], b[0], start=start, stop=False)
    nc.tensor.matmul(out, a[1], b[0], start=False, stop=False)
    return nc.tensor.matmul(out, a[0], b[1], start=False, stop=stop)


def norm_and_project(nc, d, keep):
    cols, zT = keep["cols"], keep["zT"]
    with ExitStack() as ctx:
        def sb(name, shape, dt=F32):
            return ctx.enter_context(nc.sbuf_tensor(name, shape, dt))

        def sem(name):
            return ctx.enter_context(nc.semaphore(name))

        hT = sb("hT", [P, KD, T])
        sq = sb("sq", [P, KD, T])
        root = sb("root", [P, T])
        rstd = sb("rstd", [P, T])
        xh = sb("xh", [P, KD, T], F32R)
        xl = sb("xl", [P, KD, T], F32R)
        wraw = sb("wraw", [P, 3, KD, P])
        wh = sb("wh", [P, 3, KD, P], F32R)
        wl = sb("wl", [P, 3, KD, P], F32R)
        ps = ctx.enter_context(nc.psum_tensor("ps_z", [P, 6, 512], F32))
        ps_ms = ctx.enter_context(nc.psum_tensor("ps_ms", [P, 2, 512], F32))

        loaded = sem("loaded")
        h_in = [sem(f"h_arrived{b}") for b in range(2)]
        squared = sem("squared")
        summed = sem("summed")
        rooted = sem("rooted")
        scaled = sem("scaled")
        x_hi = sem("x_hi")
        x_lo = sem("x_lo")
        w_in = [sem(f"w_arrived{s}") for s in range(3)]
        w_hi = sem("w_hi")
        w_lo = sem("w_lo")
        z_done = sem("z_done")
        evac_a = sem("evac_a")
        evac_b = sem("evac_b")

        def loop(eng, tile):
            for n in range(3):
                tile(n, n % 3)
            with eng.Fori(3, 39, 3) as n0:
                for s in range(3):
                    tile(n0 + s, s)
            for n in range(39, NZ):
                tile(n, n % 3)

        def isn(n, k):
            return not isinstance(n, int) or n >= k

        block = ctx.enter_context(nc.Block())

        @block.sync
        def _(sp):
            sp.dma_start(cols[:], d["cols"]).then_inc(loaded, 16)
            sp.dma_start(keep["ones"][:], d["ones"]).then_inc(loaded, 16)
            for b in range(2):
                part = slice(b * KD // 2, (b + 1) * KD // 2)
                sp.dma_start(hT[:, part], d["hT"][:, part]).then_inc(h_in[b], 16)

            def tile(n, s):
                if isn(n, 3):
                    sp.wait_ge(w_lo, n - 2)
                sp.dma_start(wraw[:, s], d["w_z"][n]).then_inc(w_in[s], 16)
            loop(sp, tile)
            for name in CONSTS:
                if name != "ones":
                    sp.dma_start(keep[name][:], d[name]).then_inc(loaded, 16)
            sp.wait_ge(loaded, 16 * (1 + len(CONSTS)))

        @block.scalar
        def _(act):
            def split(n, s):
                act.wait_ge(w_in[s], (n // 3) * 16 + 16 if isinstance(n, int) else
                            (n - s) * 16 // 3 + 16)
                if isn(n, 3):
                    act.wait_ge(z_done, n - 2)
                nc.scalar.copy(wh[:, s], wraw[:, s]).then_inc(w_hi, 1)

            act.wait_ge(loaded, 32)
            for k in range(KD):
                act.wait_ge(h_in[k * 2 // KD], 16)
                nc.scalar.activation(sq[:, k], hT[:, k], ACT.Square).then_inc(squared, 1)
            for n in range(2):
                split(n, n)
            act.wait_ge(summed, 1)
            nc.scalar.activation(root[:], ps_ms[:, :, 0:TH], ACT.Ln, bias=keep["eps"][:, 0:1],
                                 scale=1.0 / D).then_inc(rooted, 1)
            act.wait_ge(rooted, 1)
            nc.scalar.activation(rstd[:], root[:], ACT.Exp, scale=-0.5).then_inc(rooted, 1)
            for k in range(KD):
                act.wait_ge(scaled, k + 1)
                nc.scalar.copy(xh[:, k], sq[:, k]).then_inc(x_hi, 1)

            def evac(n, s):
                act.wait_ge(z_done, n + 1)
                nc.scalar.copy(zT[:, n, 0:TH], ps[:, 2 * s, 0:TH]).then_inc(evac_a, 1)

            evac(0, 0)
            split(2, 2)
            evac(1, 1)
            with act.Fori(3, 39, 3) as n0:
                for s in range(3):
                    split(n0 + s, s)
                    evac(n0 + (s - 1), (s - 1) % 3)
            for n in range(39, NZ):
                split(n, n % 3)
                evac(n - 1, (n - 1) % 3)
            evac(NZ - 1, (NZ - 1) % 3)

        @block.vector
        def _(dve):
            def split(n, s):
                dve.wait_ge(w_hi, n + 1)
                nc.vector.tensor_tensor(wl[:, s], wraw[:, s], wh[:, s].bitcast(F32), ALU.subtract).then_inc(w_lo, 1)

            for n in range(2):
                split(n, n)
            dve.wait_ge(rooted, 2)

            def x_low(k):
                dve.wait_ge(x_hi, k + 1)
                nc.vector.tensor_tensor(xl[:, k], sq[:, k], xh[:, k].bitcast(F32), ALU.subtract).then_inc(x_lo, 1)
            for k in range(KD):
                nc.vector.scalar_tensor_tensor(out=sq[:, k], in0=hT[:, k], scalar=cols[:, C_G1 + k:C_G1 + k + 1],
                                               in1=rstd[:], op0=ALU.mult, op1=ALU.mult).then_inc(scaled, 1)
                if k >= 1:
                    x_low(k - 1)
            x_low(KD - 1)

            def evac(n, s):
                dve.wait_ge(z_done, n + 1)
                nc.vector.tensor_copy(zT[:, n, TH:T], ps[:, 2 * s + 1, 0:TH]).then_inc(evac_b, 1)

            evac(0, 0)
            split(2, 2)
            evac(1, 1)
            with dve.Fori(3, 39, 3) as n0:
                for s in range(3):
                    split(n0 + s, s)
                    evac(n0 + (s - 1), (s - 1) % 3)
            for n in range(39, NZ):
                split(n, n % 3)
                evac(n - 1, (n - 1) % 3)
            evac(NZ - 1, (NZ - 1) % 3)

        @block.tensor
        def _(pe):
            pe.wait_ge(loaded, 32)
            for k in range(KD):
                pe.wait_ge(squared, k + 1)
                for half in range(2):
                    mm = nc.tensor.matmul(ps_ms[:, half, 0:TH], keep["ones"][:], sq[:, k, half * TH:(half + 1) * TH],
                                          start=(k == 0), stop=(k == KD - 1))
            mm.then_inc(summed, 1)

            def tile(n, s):
                pe.wait_ge(w_lo, n + 1)
                if isn(n, 3):
                    pe.wait_ge(evac_a, n - 2)
                    pe.wait_ge(evac_b, n - 2)
                for k in range(KD):
                    if isinstance(n, int) and n == 0:
                        pe.wait_ge(x_lo, k + 1)
                    for half in range(2):
                        t = slice(half * TH, (half + 1) * TH)
                        mm = matmul3(nc, ps[:, 2 * s + half, 0:TH], (wh[:, s, k], wl[:, s, k]),
                                     (xh[:, k, t], xl[:, k, t]), k == 0, k == KD - 1)
                mm.then_inc(z_done, 1)
            loop(pe, tile)


class Chain:

    def __init__(self, eng, sem, base=0):
        self.eng, self.sem, self.base, self.n = eng, sem, base, 0

    def __call__(self, instruction):
        self.n += 1
        instruction.then_inc(self.sem, 1)
        self.eng.wait_ge(self.sem, self.base + self.n)


def fox_attention(nc, d, keep):
    zT, cols, yfT = keep["zT"], keep["cols"], keep["yfT"]
    UNITS = [(u // NQ, u % NQ) for u in range(2 * NQ)]
    NU = len(UNITS)
    KQ = HD + 2
    NT = 2 * NP4
    TILES = [(n // 2, n % 2) for n in range(NT)]
    keys = [N_META + P * (i + 1) for i in range(NQ)]

    def pieces(a, b):
        return [(a, b)] if b <= 512 or a >= 512 else [(a, 512), (512, b)]

    def wait(eng, sem, value):
        if not isinstance(value, int) or value > 0:
            eng.wait_ge(sem, value)

    def pairs(eng, pair):
        pair(0)
        with eng.Fori(1, NP4 - 1) as it:
            pair(it)
        pair(NP4 - 1)

    def shifts(it):
        return range(NP4) if not isinstance(it, int) or it < NP4 - 1 else range(NSHIFT % NP4)

    with ExitStack() as ctx:
        def sb(name, shape, dt=F32):
            return ctx.enter_context(nc.sbuf_tensor(name, shape, dt))

        def sem(name):
            return ctx.enter_context(nc.semaphore(name))

        mask = sb("mask", [P, P])
        fg = sb("fg", [NH, 6, T])
        cum, ncum = fg[:, 4], fg[:, 5]
        sqk = sb("sqk", [P, 2, T])
        rqk = sb("rqk", [P, NP4, T])
        qk = sb("qk", [P, NH, 2, T])
        qcur = sb("qcur", [P, 2, T])
        vtok = sb("vtok", [P, NP4, 5, P])
        vcur = sb("vcur", [P, 5, P])
        pr = sb("pr", [P, 2, T])
        ptS = sb("ptS", [P, 2, 5, P])
        nmx = sb("nmx", [P, 2])
        rsum = sb("rsum", [P, 2])
        rinv = sb("rinv", [P, 2])
        diff = sb("diff", [P, NP4, T])
        def rstd(n):
            return (rqk, diff)[n // NP4][:, n % NP4]

        s_ps = ctx.enter_context(nc.psum_tensor("s_ps", [P, 2, 1024], F32))
        pt_ps = ctx.enter_context(nc.psum_tensor("pt_ps", [P, 1024], F32))
        pv_ps = ctx.enter_context(nc.psum_tensor("pv_ps", [P, 512], F32))

        (loaded, steps, act_steps, rows_made, gate_rows, squares, summed,
         roots, qk_ready, v_turned, v_ready, q_copied, v_copied, scores, maxed, expd, normed, turned, pt_ready,
         pv_done, y_out, diffed, shifted) = (sem("f_" + n) for n in (
             "loaded", "steps", "act_steps", "rows_made",
             "gate_rows", "squares", "summed", "roots", "qk_ready", "v_turned", "v_ready", "q_copied", "v_copied",
             "scores", "maxed", "expd", "normed", "turned", "pt_ready", "pv_done", "y_out", "diffed", "shifted"))

        block = ctx.enter_context(nc.Block())

        @block.sync
        def _(sp):
            sp.dma_start(mask[:], d["mask"]).then_inc(loaded, 16)
            sp.wait_ge(rows_made, 2)
            for h in range(NH):
                sp.dma_start(qk[HD:HD + 1, h, 0], cum[h:h + 1]).then_inc(gate_rows, 16)
                sp.dma_start(qk[HD + 1:HD + 2, h, 1], ncum[h:h + 1]).then_inc(gate_rows, 16)

        @block.gpsimd
        def _(pool):
            nc.gpsimd.memset(qk[HD:KQ], 1.0).then_inc(rows_made, 1)
            pool.wait_ge(gate_rows, 32 * NH)
            pool.wait_ge(qk_ready, 2 * NT)
            pool.wait_ge(v_ready, 2 * NP4)

            def pair(it):
                wait(pool, scores, it * NU)
                nc.gpsimd.tensor_copy(qcur[0:KQ], qk[0:KQ, bass.ds(it * 2, 2), 0]).then_inc(q_copied, 1)
                wait(pool, pv_done, it * NU)
                nc.gpsimd.tensor_copy(vcur[:, 0:4], vtok[:, it, 0:4]).then_inc(v_copied, 1)
                nc.gpsimd.tensor_copy(vcur[0:16, 4], vtok[0:16, it, 4]).then_inc(v_copied, 1)
                wait(pool, shifted, it * NP4)
                for i in shifts(it):
                    z = zT[:, it * NP4 + (ZR + i)]
                    nc.gpsimd.tensor_tensor(diff[:, i, 0:1], keep["eps"][:, 3:4], z[:, 0:1],
                                            ALU.subtract).then_inc(diffed, 1)
                    nc.gpsimd.tensor_tensor(diff[:, i, 1:T], z[:, 0:T - 1], z[:, 1:T], ALU.subtract).then_inc(diffed, 1)
            pairs(pool, pair)

        @block.scalar
        def _(act):
            act.wait_ge(steps, 1)
            link = Chain(act, act_steps)
            link(nc.scalar.activation(fg[:, 1], fg[:, 0], ACT.Abs))
            link(nc.scalar.activation(fg[:, 1], fg[:, 1], ACT.Exp, scale=-1.0))
            link(nc.scalar.activation(fg[:, 2], fg[:, 1], ACT.Ln, bias=1.0))

            def square(n):
                m, j = TILES[n]
                if n >= 2:
                    act.wait_ge(summed, n - 1)
                nc.scalar.activation(sqk[:, n % 2], zT[:, (ZQ, ZK)[j] + m], ACT.Square).then_inc(squares, 1)

            square(0)
            for n, (m, j) in enumerate(TILES):
                if n + 1 < NT:
                    square(n + 1)
                act.wait_ge(summed, n + 1)
                nc.scalar.activation(rstd(n), s_ps[:, n % 2].rearrange("p (a b) -> p a b", a=2)[:, :, 0:TH], ACT.Ln,
                                     bias=keep["eps"][:, 1 - j:2 - j], scale=(1.0, 1.0 / HD)[j]).then_inc(roots, 1)
            for n in range(NT):
                act.wait_ge(roots, NT + n)
                nc.scalar.activation(rstd(n), rstd(n), ACT.Exp, scale=-0.5).then_inc(roots, 1)
            for m in range(NP4):
                act.wait_ge(v_turned, m + 1)
                nc.scalar.copy(vtok[:, m, 0:4], pt_ps[:, 0:512]).then_inc(v_ready, 1)
                nc.scalar.copy(vtok[0:16, m, 4], pt_ps[0:16, 512:640]).then_inc(v_ready, 1)

            def pair(it):
                def exp(u):
                    n, b = keys[UNITS[u][1]], u % 2
                    act.wait_ge(maxed, it * NU + u + 1)
                    wait(act, turned, it * NU + (u - 1))
                    wait(act, normed, it * NU + (u - 1))
                    nc.scalar.activation(pr[:, b, 0:n], s_ps[:, b, 0:n], ACT.Exp, bias=nmx[:, b:b + 1],
                                         scale=1.0, accum_out=rsum[:, b:b + 1]).then_inc(expd, 1)

                def pt_out(u):
                    i, b = UNITS[u][1], u % 2
                    act.wait_ge(turned, it * NU + u + 1)
                    wait(act, pv_done, it * NU + (u - 1))
                    nc.scalar.copy(ptS[:, b, 0:i + 1], pt_ps[:, 0:P * (i + 1)]).then_inc(pt_ready, 1)
                    nc.scalar.copy(ptS[0:16, b, i + 1], pt_ps[0:16, 512:640]).then_inc(pt_ready, 1)

                exp(0)
                for u in range(NU):
                    if u + 1 < NU:
                        exp(u + 1)
                    pt_out(u)
            pairs(act, pair)

        @block.vector
        def _(dve):
            link = Chain(dve, steps)
            link(nc.vector.tensor_scalar(fg[:, 0], zT[0:NH, ZFG], cols[0:NH, C_FB:C_FB + 1], None, ALU.add))
            link(nc.vector.tensor_scalar(fg[:, 3], fg[:, 0], 0.0, None, ALU.min))
            dve.wait_ge(act_steps, 3)
            link(nc.vector.tensor_tensor(fg[:, 3], fg[:, 3], fg[:, 2], ALU.subtract))
            link(nc.vector.memset(fg[:, 2], 0.0))
            link(nc.vector.tensor_tensor_scan(cum, fg[:, 3], fg[:, 2], 0.0, ALU.add, ALU.add))
            nc.vector.tensor_scalar(ncum, cum, -1.0, None, ALU.mult).then_inc(rows_made, 1)
            for n, (m, j) in enumerate(TILES):
                dve.wait_ge(roots, NT + n + 1)
                for e in range(2):
                    r, c0 = slice(e * HD, e * HD + HD), (C_QN, C_KN)[j] + m
                    nc.vector.scalar_tensor_tensor(out=qk[0:HD, 2 * m + e, j], in0=zT[r, (ZQ, ZK)[j] + m],
                                                   scalar=cols[r, c0:c0 + 1], in1=rstd(n)[r], op0=ALU.mult,
                                                   op1=ALU.mult).then_inc(qk_ready, 1)

            prepared = link.n

            def values_out(it):
                dve.wait_ge(pv_done, it * NU + NU)
                nc.vector.tensor_copy(yfT[:, it], pv_ps[:]).then_inc(y_out, 1)

            def pair(it):
                link = Chain(dve, steps, it * NU + prepared)

                def row_max(u):
                    n, b = keys[UNITS[u][1]], u % 2
                    dve.wait_ge(scores, it * NU + u + 1)
                    nc.vector.reduce_max(nmx[:, b:b + 1], s_ps[:, b, 0:n], AX.X, negate=True).then_inc(maxed, 1)

                def norm(u):
                    n, b = keys[UNITS[u][1]], u % 2
                    dve.wait_ge(expd, it * NU + u + 1)
                    link(nc.vector.reciprocal(rinv[:, b:b + 1], rsum[:, b:b + 1]))
                    nc.vector.tensor_scalar(pr[:, b, 0:n], pr[:, b, 0:n], rinv[:, b:b + 1], None,
                                            ALU.mult).then_inc(normed, 1)

                def shift(i):
                    dve.wait_ge(diffed, it * 2 * NP4 + 2 * i + 2)
                    nc.vector.scalar_tensor_tensor(out=zT[:, it * NP4 + (ZR + i)], in0=diff[:, i],
                                                   scalar=cols[:, bass.ds(it * NP4 + (C_MU + i), 1)],
                                                   in1=zT[:, it * NP4 + (ZR + i)], op0=ALU.mult,
                                                   op1=ALU.add).then_inc(shifted, 1)

                row_max(0)
                for u in range(NU):
                    if u + 1 < NU:
                        row_max(u + 1)
                    norm(u)
                    if u % 2 and u // 2 in shifts(it):
                        shift(u // 2)
                    if u == 0 and not (isinstance(it, int) and it == 0):
                        values_out(it - 1)
            pairs(dve, pair)
            values_out(NP4 - 1)

        @block.tensor
        def _(pe):
            for n in range(NT):
                pe.wait_ge(squares, n + 1)
                if n >= 2:
                    pe.wait_ge(roots, n - 1)
                for half in range(2):
                    mm = nc.tensor.matmul(s_ps[:, n % 2, half * 512:half * 512 + TH], keep["blockones"][:],
                                          sqk[:, n % 2, half * TH:half * TH + TH], start=True, stop=True)
                mm.then_inc(summed, 1)
            for m in range(NP4):
                if m >= 1:
                    pe.wait_ge(v_ready, 2 * m)
                for j in range(4):
                    nc.tensor.transpose(pt_ps[:, j * P:j * P + P], zT[:, ZV + m, j * P:j * P + P], keep["ident"][:])
                nc.tensor.transpose(pt_ps[0:16, 512:640], zT[:, ZV + m, 512:T], keep["ident"][:]).then_inc(v_turned, 1)

            def score(it, u):
                (e, i), b = UNITS[u], u % 2
                n, q0 = keys[i], N_META + P * i
                if u == 0:
                    pe.wait_ge(q_copied, it + 1)
                wait(pe, expd, it * NU + (u - 1))
                for x, y in pieces(0, n):
                    x0 = max(x, n - P)
                    kt = qk[0:KQ, it * 2 + e, 1]
                    if x < x0:
                        nc.tensor.matmul(s_ps[:, b, x:x0], qcur[0:KQ, e, q0:q0 + P], kt[:, x:x0], start=True, stop=True)
                    nc.tensor.matmul(s_ps[:, b, x0:y], qcur[0:KQ, e, q0:q0 + P], kt[:, x0:y], start=True, stop=False)
                    mm = nc.tensor.matmul(s_ps[:, b, x0:y], keep["ident"][:], mask[:, x0 - (n - P):y - (n - P)],
                                          start=False, stop=True)
                mm.then_inc(scores, 1)

            def pair(it):
                def turn(u):
                    i, b = UNITS[u][1], u % 2
                    pe.wait_ge(normed, it * NU + u + 1)
                    wait(pe, pt_ready, it * 2 * NU + 2 * u)
                    for j in range(i + 1):
                        nc.tensor.transpose(pt_ps[:, j * P:j * P + P], pr[:, b, j * P:j * P + P], keep["ident"][:])
                    nc.tensor.transpose(pt_ps[0:16, 512:640], pr[:, b, (i + 1) * P:(i + 1) * P + 16],
                                        keep["ident"][:]).then_inc(turned, 1)

                def values(u):
                    (e, i), b = UNITS[u], u % 2
                    out = pv_ps[e * HD:e * HD + HD, i * P:i * P + P]
                    if u == 0:
                        pe.wait_ge(v_copied, it * 2 + 2)
                        wait(pe, y_out, it)
                    pe.wait_ge(pt_ready, it * 2 * NU + 2 * u + 2)
                    for j in range(i + 2):
                        k = P if j <= i else 16
                        mm = nc.tensor.matmul(out, vcur[0:k, j, e * HD:e * HD + HD], ptS[0:k, b, j],
                                              start=(j == 0), stop=(j == i + 1))
                    mm.then_inc(pv_done, 1)

                for u in range(NU):
                    turn(u)
                    if u + 2 < NU:
                        score(it, u + 2)
                    elif not (isinstance(it, int) and it == NP4 - 1):
                        score(it + 1, u + 2 - NU)
                    values(u)

            pe.wait_ge(loaded, 16)
            pe.wait_ge(roots, NT)
            score(0, 0)
            score(0, 1)
            pe.wait_ge(v_ready, 2 * NP4)
            pairs(pe, pair)


def rwkv_inputs(nc, d, keep):
    zT, cols = keep["zT"], keep["cols"]
    L, Lx, kk, ka, bonus, g = (keep[n] for n in ("L", "Lx", "kk", "ka", "bonus", "g"))
    with ExitStack() as ctx:
        def sb(name, shape, dt=F32):
            return ctx.enter_context(nc.sbuf_tensor(name, shape, dt))

        def sem(name):
            return ctx.enter_context(nc.semaphore(name))

        tanh_w = sb("tanh_w", [HD, T])
        wa_up = sb("wa_up", [P, W5])
        g_up = sb("g_up", [P, 2, W5])
        reset = sb("reset", [P, T])
        a = sb("a_rate", [P, 2, T])
        sq = sb("r_sq", [P, 2, T])
        rk = sb("r_rk", [P, 2, T])
        rn = sb("r_rn", [P, NP4, T])
        lora_ps = ctx.enter_context(nc.psum_tensor("lora_ps", [P, 3, 2, 512], F32))
        sum_ps = ctx.enter_context(nc.psum_tensor("sum_ps", [P, 2, 512], F32))

        def squares_bank(m):
            return (sum_ps[:], lora_ps[:, 2])[m % 2][:, :, 0:TH]

        loaded = sem("r_loaded")
        squashed = sem("r_squashed")
        lora_done = sem("r_lora_done")
        lora_out = sem("r_lora_out")
        kk_raw = sem("r_kk_raw")
        squared = sem("r_squared")
        summed = sem("r_summed")
        bounded = sem("r_bounded")
        inverted = sem("r_inverted")
        rk_ready = sem("r_rk_ready")
        rk_summed = sem("r_rk_summed")
        bonus_out = sem("r_bonus_out")
        steps = sem("r_steps")
        block = ctx.enter_context(nc.Block())

        @block.sync
        def _(sp):
            sp.dma_start(wa_up[:], d["wa_up"]).then_inc(loaded, 16)
            sp.dma_start(g_up[:], d["g_up"]).then_inc(loaded, 16)
            sp.dma_start(reset[:], d["reset"]).then_inc(loaded, 16)

        @block.vector
        def _(dve):
            def col(c, m):
                return cols[:, c + m:c + m + 1]
            for m in range(NP4):
                nc.vector.tensor_scalar(kk[:, m], zT[:, ZRK + m], col(C_KK, m), None, ALU.mult).then_inc(kk_raw, 1)
            for m in range(NP4):
                dve.wait_ge(summed, m + 1)
                nc.vector.tensor_scalar(rn[:, m], squares_bank(m), 1e-24, None, ALU.max).then_inc(bounded, 1)
            link = Chain(dve, steps)
            dve.wait_ge(kk_raw, NP4)
            dve.wait_ge(inverted, NP4 + 1)
            link(nc.vector.tensor_tensor(kk[:], kk[:], rn[:], ALU.mult))

            def bonus_of(m):
                dve.wait_ge(rk_summed, m + 1)
                nc.vector.tensor_tensor(bonus[:, m], sum_ps[:, :, 0:TH], zT[:, ZRV + m], ALU.mult).then_inc(bonus_out, 1)
            dve.wait_ge(loaded, 48)
            for m in range(NP4):
                r, k, am = zT[:, ZR + m], zT[:, ZRK + m], a[:, m % 2]
                dve.wait_ge(lora_out, 3 * m + 3)
                link(nc.vector.tensor_scalar(Lx[:, m], L[:, m], -float(np.exp(-0.5)), None, ALU.mult))
                link(nc.vector.tensor_tensor_scan(L[:, m], reset[:], Lx[:, m], 0.0, ALU.mult, ALU.add))
                link(nc.vector.tensor_tensor(Lx[:, m], L[:, m], Lx[:, m], ALU.subtract))
                link(nc.vector.tensor_scalar(ka[:, m], am, 1.0, col(C_KA, m), ALU.subtract, ALU.mult))
                link(nc.vector.scalar_tensor_tensor(out=k, in0=ka[:, m], scalar=1.0, in1=k, op0=ALU.add, op1=ALU.mult))
                link(nc.vector.tensor_tensor(ka[:, m], kk[:, m], am, ALU.mult))
                nc.vector.scalar_tensor_tensor(out=rk[:, m % 2], in0=r, scalar=col(C_RK, m), in1=k, op0=ALU.mult,
                                               op1=ALU.mult).then_inc(rk_ready, 1)
                if m >= 1:
                    bonus_of(m - 1)
            bonus_of(NP4 - 1)

        @block.scalar
        def _(act):
            nc.scalar.activation(tanh_w[:], zT[0:HD, ZWA], ACT.Tanh).then_inc(squashed, 1)
            nc.scalar.activation(zT[:, ZGD], zT[:, ZGD], ACT.Sigmoid).then_inc(squashed, 1)
            nc.scalar.activation(zT[32:64, ZFG], zT[32:64, ZFG], ACT.Sigmoid).then_inc(squashed, 1)

            def square(m):
                act.wait_ge(kk_raw, m + 1)
                if m >= 2:
                    act.wait_ge(summed, m - 1)
                nc.scalar.activation(sq[:, m % 2], kk[:, m], ACT.Square).then_inc(squared, 1)
            for m in range(NP4):
                square(m)
            for m in range(NP4):
                act.wait_ge(bounded, m + 1)
                nc.scalar.activation(rn[:, m], rn[:, m], ACT.Ln).then_inc(inverted, 1)
            act.wait_ge(inverted, NP4)
            nc.scalar.activation(rn[:], rn[:], ACT.Exp, scale=-0.5).then_inc(inverted, 1)
            for m in range(NP4):
                act.wait_ge(lora_done, m + 1)
                if m >= 2:
                    act.wait_ge(rk_ready, m - 1)
                nc.scalar.activation(L[:, m], lora_ps[:, 0, :, 0:TH], ACT.Sigmoid,
                                     bias=cols[:, C_W0 + m:C_W0 + m + 1]).then_inc(lora_out, 1)
                nc.scalar.activation(a[:, m % 2], lora_ps[:, 1, :, 0:TH], ACT.Sigmoid,
                                     bias=cols[:, C_A0 + m:C_A0 + m + 1]).then_inc(lora_out, 1)
                nc.scalar.copy(g[:, m], lora_ps[:, 2, :, 0:TH]).then_inc(lora_out, 1)

        @block.tensor
        def _(pe):
            def head_sums(bank, x, done):
                for half in range(2):
                    mm = nc.tensor.matmul(bank[:, half], keep["blockones"][:], x[:, half * TH:half * TH + TH],
                                          start=True, stop=True)
                mm.then_inc(done, 1)
            for m in range(NP4):
                pe.wait_ge(squared, m + 1)
                if m >= 2:
                    pe.wait_ge(bounded, m - 1)
                head_sums(squares_bank(m), sq[:, m % 2], summed)
            pe.wait_ge(loaded, 48)
            pe.wait_ge(squashed, 3)
            pe.wait_ge(bounded, NP4)

            def lora(m):
                c = slice(m * P, m * P + P)
                if m >= 1:
                    pe.wait_ge(lora_out, 3 * m)
                for half in range(2):
                    t = slice(half * TH, half * TH + TH)
                    nc.tensor.matmul(lora_ps[:, 0, half, 0:TH], wa_up[0:HD, c], tanh_w[:, t], start=True, stop=True)
                    nc.tensor.matmul(lora_ps[:, 1, half, 0:TH], wa_up[HD:P, c], zT[HD:P, ZWA, t], start=True, stop=True)
                    nc.tensor.matmul(lora_ps[:, 2, half, 0:TH], g_up[:, 0, c], zT[:, ZGD, t], start=True, stop=False)
                    mm = nc.tensor.matmul(lora_ps[:, 2, half, 0:TH], g_up[32:64, 1, c], zT[32:64, ZFG, t], start=False,
                                          stop=True)
                mm.then_inc(lora_done, 1)
            lora(0)
            for m in range(NP4):
                if m + 1 < NP4:
                    lora(m + 1)
                pe.wait_ge(rk_ready, m + 1)
                if m >= 1:
                    pe.wait_ge(bonus_out, m)
                head_sums(sum_ps[:, :, 0:TH], rk[:, m % 2], rk_summed)


def rwkv_recurrence(nc, d, keep):
    zT, L, Lx, kk, ka, yT = (keep[n] for n in ("zT", "L", "Lx", "kk", "ka", "yT"))
    NLEV = len(LEVELS)
    R = HD + C
    HP = NP4 // 2
    with ExitStack() as ctx:
        def sb(name, shape, dt=F32):
            return ctx.enter_context(nc.sbuf_tensor(name, shape, dt))

        def sem(name):
            return ctx.enter_context(nc.semaphore(name))

        mgram = sb("mgram", [P, NP4, 2 * C])
        mlev = sb("mlev", [P, NLEV + 2, C])
        eye8 = sb("eye8", [P, 2, NP4, C])
        ex = sb("ex", [P, 2, 3, NP4, C])
        ar = sb("ar", [P, 2, NP4, 2, C])
        bt = sb("bt", [P, 2, NP4, C])
        kt = sb("kt", [P, 2, NP4, C])
        vt = sb("vt", [P, 2, NP4, C])
        mb = sb("mb", [P, 2, NP4, 2 * C])
        mk = sb("mk", [P, 2, NP4, 2 * C])
        inv = sb("inv", [P, 2, 2, NP4, C])
        off = sb("off", [P, NP4, C])
        toks = sb("toks", [P, 2, 3, NP4, HD])
        rhs = sb("rhs", [P, NP4, HD])
        nu = sb("nu", [P, NP4, HD])
        last = sb("last", [P, NP4, NCH])
        ST = sb("ST", [P, NP4, HD])
        ps = ctx.enter_context(nc.psum_tensor("r_ps", [P, 8, 512], F32))

        loaded = sem("k_loaded")
        started = sem("k_started")
        exps = sem("k_exps")
        scaled = sem("k_scaled")
        gram = sem("k_gram")
        masked = sem("k_masked")
        inv1 = sem("k_inv1")
        turned = sem("k_turned")
        tok_out = sem("k_tok_out")
        offs = sem("k_offs")
        off_out = sem("k_off_out")
        grown = sem("k_grown")
        grown_out = sem("k_grown_out")
        steps = sem("k_steps")
        passed = sem("k_passed")
        rhs_done = sem("k_rhs_done")
        rhs_out = sem("k_rhs_out")
        u_done = sem("k_u_done")
        u_out = sem("k_u_out")
        y_done = sem("k_y_done")
        y_out = sem("k_y_out")
        s_done = sem("k_s_done")
        s_add = sem("k_s_add")
        s_out = sem("k_s_out")
        block = ctx.enter_context(nc.Block())
        NSTEP = 2

        def order(scale, prepare, level, recur, eng):
            def both(c, b):
                prepare(c, b)
                for lv in range(NLEV):
                    if lv == 2 and not (isinstance(c, int) and c == NCH - 1):
                        scale(c + 1, 1 - b)
                    level(c, b, lv)
                    if not (isinstance(c, int) and c == 0):
                        recur(c - 1, 1 - b, lv)
            both(0, 0)
            both(1, 1)
            with eng.Fori(2, NCH - 2, 2) as c:
                both(c, 0)
                both(c + 1, 1)
            both(NCH - 1, 0)
            for lv in range(NLEV):
                recur(NCH - 1, 0, lv)

        def isn(c, k):
            return not isinstance(c, int) or c >= k

        def kinds(lv):
            return (0, 1) if lv < NLEV - 1 else (1,)

        @block.sync
        def _(sp):
            sp.dma_start(mgram[:], d["mgram"]).then_inc(loaded, 16)
            sp.dma_start(mlev[:], d["mlev"]).then_inc(loaded, 16)
            sp.dma_start(eye8[:], d["eye8"]).then_inc(loaded, 16)
            sp.wait_ge(loaded, 48)
            sp.dma_start(keep["wb_fox"][:], d["w_branch"][:, 0]).then_inc(loaded, 16)
            sp.wait_ge(loaded, 64)

        @block.scalar
        def _(act):
            def scale(c, b):
                t = bass.ds(c * C, C)
                if isn(c, 2):
                    act.wait_ge(scaled, 4 * c - 4)
                    act.wait_ge(turned, 3 * c - 3)
                nc.scalar.activation(ex[:, b, 0], L[:, :, t], ACT.Exp).then_inc(exps, 1)
                nc.scalar.activation(ex[:, b, 1], L[:, :, t], ACT.Exp, scale=-1.0).then_inc(exps, 1)
                nc.scalar.activation(ex[:, b, 2], Lx[:, :, t], ACT.Exp).then_inc(exps, 1)
                nc.scalar.copy(vt[:, b], zT[:, ZRV:ZRV + 4, t]).then_inc(exps, 1)

            def prepare(c, b):
                for j, bank in enumerate((6, 7, 0)):
                    act.wait_ge(turned, 3 * c + j + 1)
                    x = ps[0:C, bank].rearrange("c (p e f) -> c p e f", p=NP4, e=2)
                    for e in range(2):
                        nc.scalar.copy(toks[e * HD:e * HD + C, b, j], x[:, :, e]).then_inc(tok_out, 1)

            def level(c, b, lv):
                pass

            def recur(c, b, lv):
                if lv == 0:
                    act.wait_ge(rhs_done, c + 1)
                    nc.scalar.copy(rhs[0:R], ps[0:R, 6, 0:256]).then_inc(rhs_out, 1)
                if lv == 1:
                    act.wait_ge(u_done, c + 1)
                    nc.scalar.mul(nu[0:R], ps[0:R, 1, 0:256], -1.0).then_inc(u_out, 1)
            nc.scalar.activation(last[:], L[:, :, bass.ds(C - 1, NCH, step=C)], ACT.Exp).then_inc(started, 1)
            act.wait_ge(started, 3)
            scale(0, 0)
            order(scale, prepare, level, recur, act)

        @block.vector
        def _(dve):
            nc.vector.memset(ps[32:64], 0.0).then_inc(started, 1)
            nc.vector.memset(ST[:], 0.0).then_inc(started, 1)
            dve.wait_ge(loaded, 48)
            dve.wait_ge(started, 3)

            def scale(c, b):
                t = bass.ds(c * C, C)
                dve.wait_ge(exps, 4 * c + 4)
                if isn(c, 2):
                    dve.wait_ge(y_done, c - 1)
                nc.vector.tensor_tensor(bt[:, b], ex[:, b, 1], ka[:, :, t], ALU.mult).then_inc(scaled, 1)
                nc.vector.tensor_tensor(ar[:, b, :, 0], ex[:, b, 2], kk[:, :, t], ALU.mult).then_inc(scaled, 1)
                nc.vector.tensor_tensor(ar[:, b, :, 1], ex[:, b, 0], zT[:, ZR:ZR + 4, t], ALU.mult).then_inc(scaled, 1)
                nc.vector.tensor_tensor(kt[:, b], ex[:, b, 1], zT[:, ZRK:ZRK + 4, t], ALU.mult).then_inc(scaled, 1)

            def prepare(c, b):
                for j, m in enumerate((mb, mk)):
                    dve.wait_ge(gram, 3 * c + j + 1)
                    nc.vector.tensor_tensor(m[0:R, b], ps[0:R, j, 0:NP4 * 2 * C].rearrange("p (a b) -> p a b", a=NP4),
                                            mgram[0:R], ALU.mult).then_inc(masked, 1)
                dve.wait_ge(gram, 3 * c + 3)
                dve.wait_ge(masked, 2 * c + 1)
                link = Chain(dve, steps, c * NSTEP)
                link(nc.vector.tensor_tensor(inv[0:R, b, 0], ps[0:R, 2, 0:NP4 * C].rearrange("p (a b) -> p a b", a=NP4),
                                             mlev[0:R, NLEV:NLEV + 1].broadcast_to([R, NP4, C]), ALU.mult))
                link(nc.vector.tensor_tensor(inv[0:R, b, 1], mb[0:R, b, :, 0:C],
                                             mlev[0:R, NLEV + 1:NLEV + 2].broadcast_to([R, NP4, C]), ALU.mult))
                nc.vector.tensor_tensor(inv[0:R, b], inv[0:R, b], eye8[0:R], ALU.add).then_inc(inv1, 1)

            def level(c, b, lv):
                n = c * NLEV + lv
                for g in range(2):
                    dve.wait_ge(offs, n * 2 + g + 1)
                    nc.vector.tensor_tensor(off[0:R, g * HP:g * HP + HP],
                                            ps[0:R, 2 + g, 0:HP * C].rearrange("p (a b) -> p a b", a=HP),
                                            mlev[0:R, lv:lv + 1].broadcast_to([R, HP, C]), ALU.mult).then_inc(off_out, 1)
                if lv == NLEV - 1 and not (isinstance(c, int) and c == NCH - 1):
                    scale(c + 1, 1 - b)
                for g in range(2):
                    dve.wait_ge(grown, n * 2 + g + 1)
                    x0 = kinds(lv)[0]
                    i = inv[0:R, b, x0:2, g * HP:g * HP + HP]
                    nc.vector.tensor_tensor(i, i, ps[0:R, 4 + g, x0 * HP * C:2 * HP * C].rearrange(
                        "p (x a b) -> p x a b", x=2 - x0, a=HP), ALU.add).then_inc(grown_out, 1)

            def recur(c, b, lv):
                if lv == 3:
                    dve.wait_ge(s_done, c + 1)
                    dve.wait_ge(y_done, c + 1)
                    nc.vector.tensor_tensor(ST[:], ps[:, 7, 256:512].rearrange("p (a b) -> p a b", a=NP4),
                                            ST[:], ALU.add).then_inc(s_add, 1)
                    dve.wait_ge(s_add, c + 1)
                    nc.vector.tensor_tensor(ST[:], ST[:], last[:, :, bass.ds(c, 1)].broadcast_to([P, NP4, HD]),
                                            ALU.mult).then_inc(s_out, 1)
                    nc.vector.tensor_copy(yT[:, :, bass.ds(c * C, C)],
                                          ps[:, 7, 0:NP4 * C].rearrange("p (a b) -> p a b", a=NP4)).then_inc(y_out, 1)
            scale(0, 0)
            order(lambda c, b: None, prepare, level, recur, dve)

        @block.tensor
        def _(pe):
            pe.wait_ge(loaded, 48)
            pe.wait_ge(started, 3)

            def alone():
                pe.sem_inc(passed, 1)

            def heads(pairs=range(NP4)):
                return [(p, slice(e * HD, e * HD + HD), slice(e * HD, e * HD + C)) for p in pairs for e in range(2)]

            def prepare(c, b):
                pe.wait_ge(scaled, 4 * c + 3)
                if isn(c, 1):
                    pe.wait_ge(grown_out, c * 2 * NLEV)
                    pe.wait_ge(tok_out, 6 * c)
                if isn(c, 2):
                    pe.wait_ge(u_out, c - 1)
                alone()
                for p, f, t in heads():
                    mm = nc.tensor.matmul(ps[t, 0, p * 96:p * 96 + 96], bt[f, b, p], ar[f, b, p], start=True, stop=True)
                mm.then_inc(gram, 1)
                pe.wait_ge(scaled, 4 * c + 4)
                alone()
                for p, f, t in heads():
                    mm = nc.tensor.matmul(ps[t, 1, p * 96:p * 96 + 96], kt[f, b, p], ar[f, b, p], start=True, stop=True)
                mm.then_inc(gram, 1)
                for p, f, t in heads():
                    mm = nc.tensor.matmul(ps[t, 2, p * C:p * C + C], ar[f, b, p, 0], bt[f, b, p], start=True, stop=True)
                mm.then_inc(gram, 1)
                if isn(c, 2):
                    pe.wait_ge(rhs_out, c - 1)
                    pe.wait_ge(y_out, c - 1)
                    pe.wait_ge(s_add, c - 1)
                for j, (x, bank) in enumerate(((kt, 6), (bt, 7), (vt, 0))):
                    if j == 2:
                        pe.wait_ge(exps, 4 * c + 4)
                        pe.wait_ge(masked, 2 * c + 1)
                    alone()
                    for p in range(NP4):
                        mm = nc.tensor.transpose(ps[0:C, bank, p * P:p * P + P], x[:, b, p], keep["ident"][:])
                    mm.then_inc(turned, 1)

            def level(c, b, lv):
                n = c * NLEV + lv
                if lv == 0:
                    pe.wait_ge(inv1, c + 1)
                for g in range(2):
                    if lv >= 1:
                        pe.wait_ge(grown_out, n * 2 + g - 1)
                    alone()
                    for p, _, t in heads(range(g * HP, g * HP + HP)):
                        mm = nc.tensor.matmul(ps[t, 2 + g, p % HP * C:p % HP * C + C], mb[t, b, p, 0:C],
                                              inv[t, b, 0, p], start=True, stop=True)
                    mm.then_inc(offs, 1)
                for g in range(2):
                    pe.wait_ge(off_out, n * 2 + g + 1)
                    alone()
                    for x in kinds(lv):
                        for p, _, t in heads(range(g * HP, g * HP + HP)):
                            o = ps[t, 4 + g, (x * HP + p % HP) * C:(x * HP + p % HP) * C + C]
                            a, m = (inv[t, b, 1, p], off[t, p]) if x == 0 else (off[t, p], inv[t, b, 1, p])
                            mm = nc.tensor.matmul(o, a, m, start=True, stop=True)
                    mm.then_inc(grown, 1)

            def sums(bank, col, width, terms, rows):
                for p in range(NP4):
                    for i in range(len(terms(0, slice(0, HD), slice(0, C)))):
                        for _, f, t in heads([p]):
                            a, m = terms(p, f, t)[i]
                            mm = nc.tensor.matmul(ps[t if rows == C else f, bank, col + p * width:col + p * width + width],
                                                  a, m, start=(i == 0), stop=(i == len(terms(p, f, t)) - 1))
                return mm

            def recur(c, b, lv):
                if lv == 0:
                    if isn(c, 1):
                        pe.wait_ge(s_out, c)
                    pe.wait_ge(grown_out, (c + 1) * 2 * NLEV)
                    pe.wait_ge(tok_out, 6 * NCH if isinstance(c, int) and c == NCH - 1 else 6 * c + 12)
                    alone()
                    sums(6, 0, HD, lambda p, f, t: [(ar[f, b, p, 0], ST[f, p]), (mk[t, b, p, 0:C], toks[t, b, 2, p])],
                         C).then_inc(rhs_done, 1)
                if lv == 1:
                    pe.wait_ge(rhs_out, c + 1)
                    alone()
                    sums(1, 0, HD, lambda p, f, t: [(inv[t, b, 1, p], rhs[t, p])], C).then_inc(u_done, 1)
                if lv == 2:
                    pe.wait_ge(u_out, c + 1)
                    if isn(c, 1):
                        pe.wait_ge(y_out, c)
                    alone()
                    sums(7, 256, HD, lambda p, f, t: [(toks[t, b, 0, p], toks[t, b, 2, p]), (toks[t, b, 1, p], nu[t, p])],
                         HD).then_inc(s_done, 1)
                    sums(7, 0, C, lambda p, f, t: [(ST[f, p], ar[f, b, p, 1]), (toks[t, b, 2, p], mk[t, b, p, C:2 * C]),
                                                   (nu[t, p], mb[t, b, p, C:2 * C])], HD).then_inc(y_done, 1)

            order(lambda c, b: None, prepare, level, recur, pe)


def rwkv_output(nc, d, keep):
    cols, yT, bonus, g, yrT, zT, wbf, yfT, gated = (keep[n] for n in (
        "cols", "yT", "bonus", "g", "yrT", "zT", "wb_fox", "yfT", "gated"))
    X = slice(N_META, T)
    with ExitStack() as ctx:
        def sb(name, shape, dt=F32):
            return ctx.enter_context(nc.sbuf_tensor(name, shape, dt))

        def sem(name):
            return ctx.enter_context(nc.semaphore(name))

        yc = sb("o_yc", [P, NP4, SEQ])
        sq = sb("o_sq", [P, NP4, SEQ])
        rt = sb("o_rt", [P, NP4, SEQ])
        ps = ctx.enter_context(nc.psum_tensor("o_ps", [P, 4, 512], F32))
        b_ps = ctx.enter_context(nc.psum_tensor("ob_ps", [P, 4, 512], F32))
        mean, centred, squared, var, rooted, steps, loaded, gates, branch, gated_done = (sem("o_" + n) for n in (
            "mean", "centred", "squared", "var", "rooted", "steps", "loaded", "gates", "branch", "gated"))
        block = ctx.enter_context(nc.Block())

        @block.sync
        def _(sp):
            sp.dma_start(keep["wb_rwkv"][:], d["w_branch"][:, 1]).then_inc(loaded, 16)
            sp.wait_ge(loaded, 16)

        @block.tensor
        def _(pe):
            def fox_branch(m):
                if m >= 4:
                    pe.wait_ge(gated_done, m - 3)
                for k in range(NP4):
                    mm = nc.tensor.matmul(b_ps[:, m % 4], wbf[:, k, m * P:m * P + P], yfT[:, k],
                                          start=(k == 0), stop=(k == NP4 - 1))
                mm.then_inc(branch, 1)
            for m in range(NP4):
                nc.tensor.matmul(ps[:, m], keep["blockmean"][:], yT[:, m, X], start=True, stop=True).then_inc(mean, 1)
            for m in range(2):
                fox_branch(m)
            for m in range(NP4):
                pe.wait_ge(squared, m + 1)
                nc.tensor.matmul(ps[:, m], keep["blockmean"][:], sq[:, m], start=True, stop=True).then_inc(var, 1)
            for m in range(2, KD):
                fox_branch(m)

        @block.scalar
        def _(act):
            for m in range(KD):
                nc.scalar.activation(zT[:, ZGF + m, X], zT[:, ZGF + m, X], ACT.Sigmoid).then_inc(gates, 1)
            for m in range(NP4):
                act.wait_ge(centred, m + 1)
                nc.scalar.activation(sq[:, m], yc[:, m], ACT.Square).then_inc(squared, 1)
            for m in range(NP4):
                act.wait_ge(var, m + 1)
                nc.scalar.activation(rt[:, m], ps[:, m], ACT.Ln, bias=keep["eps"][:, 2:3]).then_inc(rooted, 1)
            for m in range(NP4):
                act.wait_ge(rooted, NP4 + m)
                nc.scalar.activation(rt[:, m], rt[:, m], ACT.Exp, scale=-0.5).then_inc(rooted, 1)
            for m in range(KD):
                nc.scalar.activation(zT[:, ZGR + m, X], zT[:, ZGR + m, X], ACT.Sigmoid).then_inc(gates, 1)

        @block.vector
        def _(dve):
            link = Chain(dve, steps)

            def gate(m):
                dve.wait_ge(gates, m + 1)
                dve.wait_ge(branch, m + 1)
                nc.vector.tensor_tensor(gated[:, m], b_ps[:, m % 4], zT[:, ZGF + m, X], ALU.mult).then_inc(gated_done, 1)
            for m in range(NP4):
                dve.wait_ge(mean, m + 1)
                nc.vector.tensor_tensor(yc[:, m], yT[:, m, X], ps[:, m], ALU.subtract).then_inc(centred, 1)
            dve.wait_ge(centred, NP4)
            for m in range(2):
                gate(m)
            for m in range(NP4):
                def col(c):
                    return cols[:, c + m:c + m + 1]
                dve.wait_ge(rooted, NP4 + m + 1)
                link(nc.vector.tensor_tensor(yc[:, m], yc[:, m], rt[:, m], ALU.mult))
                link(nc.vector.tensor_scalar(yc[:, m], yc[:, m], col(C_LG), col(C_LB), ALU.mult, ALU.add))
                link(nc.vector.tensor_tensor(yc[:, m], yc[:, m], bonus[:, m, X], ALU.add))
                link(nc.vector.tensor_tensor(yrT[:, m], yc[:, m], g[:, m, X], ALU.mult))
                gate(2 + m)
            for m in range(2 + NP4, KD):
                gate(m)


def branches_and_residual(nc, d, keep):
    wb, zT, yrT, gated, acc = (keep[n] for n in ("wb_rwkv", "zT", "yrT", "gated", "acc"))
    X = slice(N_META, T)
    with ExitStack() as ctx:
        def sb(name, shape, dt=F32):
            return ctx.enter_context(nc.sbuf_tensor(name, shape, dt))

        def sem(name):
            return ctx.enter_context(nc.semaphore(name))

        wo = sb("wo", [P, KD, D])
        part = sb("b_part", [P, 2, SEQ])
        mixed = gated
        sq = sb("b_sq", [P, 2, D])
        ps = ctx.enter_context(nc.psum_tensor("b_ps", [P, 8, 512], F32))
        loaded_o, x_loaded, branch, parts, mixed_done, wout_done, h2_done, squared = (sem("b_" + n) for n in (
            "loaded_o", "x_loaded", "branch", "parts", "mixed", "wout", "h2", "squared"))
        block = ctx.enter_context(nc.Block())

        @block.scalar
        def _(act):
            for i in range(NQ):
                act.wait_ge(h2_done, 2 * i + 2)
                if i >= 2:
                    act.wait_ge(squared, i - 1)
                nc.scalar.activation(sq[:, i % 2], acc[:, i], ACT.Square,
                                     accum_out=keep["ms"][:, 0, i:i + 1]).then_inc(squared, 1)
            act.wait_ge(squared, NQ)
            nc.scalar.activation(keep["ms"][:, 1], keep["ms"][:, 0], ACT.Sqrt, bias=keep["eps"][:, 0:1],
                                 scale=1.0 / D).then_inc(squared, 1)

        @block.sync
        def _(sp):
            sp.dma_start(wo[:], d["w_out"]).then_inc(loaded_o, 16)
            sp.dma_start(acc[:], d["x_tok"]).then_inc(x_loaded, 16)

        @block.tensor
        def _(pe):
            for m in range(KD):
                if m >= 4:
                    pe.wait_ge(parts, m - 3)
                for k in range(NP4):
                    mm = nc.tensor.matmul(ps[:, m % 4], wb[:, k, m * P:m * P + P], yrT[:, k],
                                          start=(k == 0), stop=(k == NP4 - 1))
                mm.then_inc(branch, 1)
            pe.wait_ge(loaded_o, 16)
            for i in range(NQ):
                for half in range(2):
                    n = 2 * i + half
                    if n >= 4:
                        pe.wait_ge(h2_done, n - 3)
                    for k in range(KD):
                        if n == 0:
                            pe.wait_ge(mixed_done, k + 1)
                        mm = nc.tensor.matmul(ps[:, 4 + n % 4], mixed[:, k, i * P:i * P + P],
                                              wo[:, k, half * 512:half * 512 + 512], start=(k == 0), stop=(k == KD - 1))
                    mm.then_inc(wout_done, 1)

        @block.vector
        def _(dve):
            for m in range(KD):
                dve.wait_ge(branch, m + 1)
                if m >= 2:
                    dve.wait_ge(mixed_done, m - 1)
                nc.vector.tensor_tensor(part[:, m % 2], ps[:, m % 4], zT[:, ZGR + m, X], ALU.mult).then_inc(parts, 1)
                dve.wait_ge(parts, m + 1)
                nc.vector.tensor_tensor(mixed[:, m], part[:, m % 2], gated[:, m], ALU.add).then_inc(mixed_done, 1)
            dve.wait_ge(x_loaded, 16)
            for n in range(2 * NQ):
                dve.wait_ge(wout_done, n + 1)
                o = acc[:, n // 2, n % 2 * 512:n % 2 * 512 + 512]
                nc.vector.tensor_tensor(o, ps[:, 4 + n % 4], o, ALU.add).then_inc(h2_done, 1)


def second_norm(nc, d, keep):
    cols, acc, x2h, x2l = (keep[n] for n in ("cols", "acc", "x2h", "x2l"))
    with ExitStack() as ctx:
        def sb(name, shape, dt=F32):
            return ctx.enter_context(nc.sbuf_tensor(name, shape, dt))

        def sem(name):
            return ctx.enter_context(nc.semaphore(name))

        ms = keep["ms"]
        free = keep["zT"][:].rearrange("p a t -> p (a t)")
        xn = free[:, 0:NQ * D].rearrange("p (i n) -> p i n", i=NQ)
        xT = free[:, NQ * D:NQ * D + KD * SEQ].rearrange("p (k t) -> p k t", k=KD)
        NBANK = 6
        ps = ctx.enter_context(nc.psum_tensor("n_ps", [P, NBANK, 512], F32))
        inverted, scaled, turned, gained, x_hi, x_lo, stored = (sem("n_" + n) for n in (
            "inverted", "scaled", "turned", "gained", "x_hi", "x_lo", "stored"))
        block = ctx.enter_context(nc.Block())

        @block.sync
        def _(sp):
            load = keep["hidden"][0]
            load(sp, 0, 0)
            for b in range(2):
                sp.dma_start(keep["q_wraw"][:, b], d["w_q"][b]).then_inc(keep["q_w_in"][b], 16)
            load(sp, 1, 1)
            sp.dma_start(keep["H2"], acc[:]).then_inc(stored, 16)
            sp.wait_ge(stored, 16)

        @block.scalar
        def _(act):
            for k in range(KD):
                act.wait_ge(turned, k + 1)
                nc.scalar.activation(xT[:, k], ps[:, k % NBANK], ACT.Copy, scale=cols[:, C_G2 + k:C_G2 + k + 1]).then_inc(gained, 1)

        @block.vector
        def _(dve):
            nc.vector.reciprocal(ms[:, 0], ms[:, 1]).then_inc(inverted, 1)
            dve.wait_ge(inverted, 1)
            for i in range(NQ):
                nc.vector.tensor_scalar(xn[:, i], acc[:, i], ms[:, 0, i:i + 1], None, ALU.mult).then_inc(scaled, 1)
            for k in range(KD):
                dve.wait_ge(gained, k + 1)
                nc.vector.tensor_copy(x2h[:, k], xT[:, k]).then_inc(x_hi, 1)
                dve.wait_ge(x_hi, k + 1)
                nc.vector.tensor_tensor(x2l[:, k], xT[:, k], x2h[:, k].bitcast(F32), ALU.subtract).then_inc(x_lo, 1)

        @block.tensor
        def _(pe):
            pe.wait_ge(scaled, NQ)
            for k in range(KD):
                if k >= NBANK:
                    pe.wait_ge(gained, k - NBANK + 1)
                for i in range(NQ):
                    mm = nc.tensor.transpose(ps[:, k % NBANK, i * P:i * P + P], xn[:, i, k * P:k * P + P], keep["ident"][:])
                mm.then_inc(turned, 1)


def hidden_layer(nc, d, keep, sb, sem):
    x2h, x2l, HID = (keep[n] for n in ("x2h", "x2l", "HID"))
    uraw = sb("uraw", [P, 2, KD, P])
    uh = sb("uh", [P, 2, KD, P], F32R)
    ul = sb("ul", [P, 2, KD, P], F32R)
    hid = sb("hid", [P, 2, SEQ])
    h_ps = keep["h_ps"]
    u_in = [sem(f"u_arrived{s}") for s in range(2)]
    stored = [sem(f"hid_stored{s}") for s in range(2)]
    u_hi, u_lo, u_done, hid_out = (sem(n) for n in ("u_hi", "u_lo", "u_done", "hid_out"))

    def isn(m, k):
        return not isinstance(m, int) or m >= k

    def rounds(m, s):
        return (m // 2 + 1) * 16 if isinstance(m, int) else (m + (2 - s)) * 8

    def load(sp, m, s):
        if isn(m, 2):
            sp.wait_ge(u_lo, m - 1)
        sp.dma_start(uraw[:, s], d["u"][m]).then_inc(u_in[s], 16)

    def store(sp, m, s):
        sp.wait_ge(hid_out, m + 1)
        sp.dma_start(HID[m], hid[:, s]).then_inc(stored[s], 16)

    def split_hi(act, m, s):
        act.wait_ge(u_in[s], rounds(m, s))
        if isn(m, 2):
            act.wait_ge(u_done, m - 1)
        nc.scalar.copy(uh[:, s], uraw[:, s]).then_inc(u_hi, 1)

    def gelu(act, m, s):
        act.wait_ge(u_done, m + 1)
        if isn(m, 2):
            act.wait_ge(stored[s], rounds(m - 2, s))
        nc.scalar.activation(hid[:, s], h_ps[:, s], ACT.Gelu).then_inc(hid_out, 1)

    def split_lo(pool, m, s):
        pool.wait_ge(u_hi, m + 1)
        nc.gpsimd.tensor_tensor(ul[:, s], uraw[:, s], uh[:, s].bitcast(F32), ALU.subtract).then_inc(u_lo, 1)

    def product(pe, m, s, ks=range(KD)):
        if ks[0] == 0:
            pe.wait_ge(u_lo, m + 1)
            if isn(m, 2):
                pe.wait_ge(hid_out, m - 1)
        for k in ks:
            mm = matmul3(nc, h_ps[:, s], (uh[:, s, k], ul[:, s, k]), (x2h[:, k], x2l[:, k]), k == 0, k == KD - 1)
        if ks[-1] == KD - 1:
            mm.then_inc(u_done, 1)

    def all_stored(sp):
        for s in range(2):
            sp.wait_ge(stored[s], NCHUNK // 2 * 16)
    return load, store, split_hi, gelu, split_lo, product, all_stored


def peer_retrieval(nc, d, keep):
    x2h, x2l, picksT = (keep[n] for n in ("x2h", "x2l", "picksT"))
    NV = TOPK * TOPK
    UPH = 12
    with ExitStack() as ctx:
        def sb(name, shape, dt=F32):
            return ctx.enter_context(nc.sbuf_tensor("q_" + name, shape, dt))

        def sem(name):
            return ctx.enter_context(nc.semaphore("q_" + name))

        wraw, w_in = keep["q_wraw"], keep["q_w_in"]
        wh = sb("wh", [P, 2, KD, P], F32R)
        wl = sb("wl", [P, 2, KD, P], F32R)
        subk = sb("subk", [P, 2, NK])
        iota = sb("iota16", [P, TOPK])
        qT = sb("qT", [P, 2, SEQ])
        s = sb("s", [P, 2, NQ, NK])
        rest = sb("rest", [P, NQ, NK])
        top = sb("top", [P, 2, NQ, TOPK])
        idx = sb("idx", [P, 2, NQ, TOPK], U32)
        idxf = sb("idxf", [P, 2, NQ, TOPK])
        cand = sb("cand", [P, NQ, NV])
        crest = sb("crest", [P, NQ, NV])
        ctop = sb("ctop", [P, NQ, TOPK])
        cpos = sb("cpos", [P, NQ, TOPK], U32)
        cab = sb("cab", [P, 2, NQ, TOPK], U32)
        cabf = sb("cabf", [P, 2, NQ, TOPK])
        eq = sb("eq", [P, NQ, TOPK, TOPK])
        shifted = sb("shifted", [P, NQ, TOPK])
        gates = sb("gates", [P, NQ, TOPK])
        gsum = sb("gsum", [P, 2, NQ])
        picks = sb("picks", [P, 3, NQ, PH, TOPK])
        q_ps = ctx.enter_context(nc.psum_tensor("q_ps", [P, 2, 512], F32))
        s_ps = ctx.enter_context(nc.psum_tensor("qs_ps", [P, 2, 512], F32))
        load, store, split_hi, gelu, split_lo, product, _ = keep["hidden"]

        loaded = sem("loaded")
        w_hi, w_lo, q_done, q_out, s_done, s_out, found, shift_done, exp_done, listed, turned, t_out, steps = (
            sem(n) for n in ("w_hi", "w_lo", "q_done", "q_out", "s_done", "s_out", "found", "shift_done",
                             "exp_done", "listed", "turned", "t_out", "steps"))
        block = ctx.enter_context(nc.Block())

        def heads(eng, head):
            head(0)
            with eng.Fori(1, PH - 1) as h:
                head(h)
            head(PH - 1)

        def chunks(eng, h, a, b, step):
            if isinstance(h, int) and h == 0 and a < 4:
                for m in range(a, 4):
                    step(m, m % 2)
                a = 4
            if a < b:
                with eng.Fori(a, b - 1, 2) as j:
                    for s in range(2):
                        step(h * UPH + j + s, s)

        @block.sync
        def _(sp):
            sp.dma_start(subk[:], d["subk"]).then_inc(loaded, 16)
            sp.dma_start(iota[:], d["iota16"]).then_inc(loaded, 16)

            def both(m, s):
                if not isinstance(m, int) or m >= 2:
                    load(sp, m, s)
                if not isinstance(m, int) or m >= 3:
                    store(sp, m - 3, 1 - s)

            def head(h):
                chunks(sp, h, 0, 6, both)
                if not isinstance(h, int) or h < PH - 1:
                    for b in range(2):
                        sp.wait_ge(w_lo, h * 2 + b + 1)
                        sp.dma_start(wraw[:, b], d["w_q"][h * 2 + b + 2]).then_inc(w_in[b], 16)
                chunks(sp, h, 6, UPH, both)
            heads(sp, head)
            for m in range(PH * UPH, PH * UPH + 2):
                both(m, m % 2)

        @block.scalar
        def _(act):
            def split_w(h, b):
                act.wait_ge(w_in[b], h * 16 + 16)
                if not isinstance(h, int) or h > 0:
                    act.wait_ge(q_done, h * 2)
                nc.scalar.copy(wh[:, b], wraw[:, b]).then_inc(w_hi, 1)

            def head(h):
                for b in range(2):
                    act.wait_ge(q_done, h * 2 + b + 1)
                    if not isinstance(h, int) or h > 0:
                        act.wait_ge(s_done, h * 2)
                    nc.scalar.copy(qT[:, b], q_ps[:, b]).then_inc(q_out, 1)
                for b in range(2):
                    act.wait_ge(s_done, h * 2 + b + 1)
                    if not isinstance(h, int) or h > 0:
                        act.wait_ge(found, h * 2)
                    nc.scalar.copy(s[:, b], s_ps[:, b]).then_inc(s_out, 1)

                def step(m, sl):
                    split_hi(act, m + 1, 1 - sl)
                    if not isinstance(m, int) or m >= 1:
                        gelu(act, m - 1, 1 - sl)
                chunks(act, h, 0, 4, step)
                if not isinstance(h, int) or h < PH - 1:
                    split_w(h + 1, 0)
                chunks(act, h, 4, 8, step)
                if not isinstance(h, int) or h < PH - 1:
                    split_w(h + 1, 1)
                chunks(act, h, 8, 10, step)
                act.wait_ge(shift_done, h + 1)
                nc.scalar.activation(gates[:], shifted[:], ACT.Exp).then_inc(exp_done, 1)
                chunks(act, h, 10, UPH, step)
            for b in range(2):
                split_w(0, b)
            split_hi(act, 0, 0)
            heads(act, head)
            gelu(act, PH * UPH - 1, 1)
            act.wait_ge(turned, 3)
            for j, bank in enumerate((q_ps[:, 0], q_ps[:, 1], s_ps[:, 0])):
                nc.scalar.copy(picksT[:, j], bank).then_inc(t_out, 1)

        @block.gpsimd
        def _(pool):
            def split_w(h, b):
                pool.wait_ge(w_hi, h * 2 + b + 1)
                nc.gpsimd.tensor_tensor(wl[:, b], wraw[:, b], wh[:, b].bitcast(F32), ALU.subtract).then_inc(w_lo, 1)

            def head(h):
                def step(m, sl):
                    split_lo(pool, m + 1, 1 - sl)
                chunks(pool, h, 0, 4, step)
                if not isinstance(h, int) or h < PH - 1:
                    split_w(h + 1, 0)
                chunks(pool, h, 4, 8, step)
                if not isinstance(h, int) or h < PH - 1:
                    split_w(h + 1, 1)
                chunks(pool, h, 8, UPH, step)
            for b in range(2):
                split_w(0, b)
            split_lo(pool, 0, 0)
            heads(pool, head)

        @block.vector
        def _(dve):
            link = Chain(dve, steps)
            for h in range(PH):
                for b in range(2):
                    dve.wait_ge(s_out, h * 2 + b + 1)
                    for i in range(NQ):
                        link(nc.vector.max(top[:, b, i, 0:8], s[:, b, i]))
                        link(nc.vector.match_replace(rest[:, i], top[:, b, i, 0:8], s[:, b, i], -3.0e38))
                        nc.vector.max_index(idx[:, b, i, 0:8], top[:, b, i, 0:8], s[:, b, i])
                        link(nc.vector.max(top[:, b, i, 8:16], rest[:, i]))
                        link(nc.vector.max_index(idx[:, b, i, 8:16], top[:, b, i, 8:16], rest[:, i]))
                    nc.vector.tensor_copy(idxf[:, b], idx[:, b]).then_inc(found, 1)
                    dve.wait_ge(found, h * 2 + b + 1)
                link(nc.vector.tensor_tensor(
                    cand[:].rearrange("p q (a b) -> p q a b", a=TOPK),
                    top[:, 0].unsqueeze(3).broadcast_to([P, NQ, TOPK, TOPK]),
                    top[:, 1].unsqueeze(2).broadcast_to([P, NQ, TOPK, TOPK]), ALU.add))
                for i in range(NQ):
                    link(nc.vector.max(ctop[:, i, 0:8], cand[:, i]))
                    link(nc.vector.match_replace(crest[:, i], ctop[:, i, 0:8], cand[:, i], -3.0e38))
                    nc.vector.max_index(cpos[:, i, 0:8], ctop[:, i, 0:8], cand[:, i])
                    link(nc.vector.max(ctop[:, i, 8:16], crest[:, i]))
                    link(nc.vector.max_index(cpos[:, i, 8:16], ctop[:, i, 8:16], crest[:, i]))
                nc.vector.tensor_tensor(shifted[:], ctop[:], ctop[:, :, 0:1].broadcast_to([P, NQ, TOPK]),
                                        ALU.subtract).then_inc(shift_done, 1)
                link(nc.vector.tensor_scalar(cab[:, 0], cpos[:], 4, None, ALU.logical_shift_right))
                link(nc.vector.tensor_scalar(cab[:, 1], cpos[:], 15, None, ALU.bitwise_and))
                link(nc.vector.tensor_copy(cabf[:], cab[:]))
                for j in range(2):
                    link(nc.vector.tensor_tensor(
                        eq[:], cabf[:, j].unsqueeze(3).broadcast_to([P, NQ, TOPK, TOPK]),
                        iota[:].unsqueeze(1).unsqueeze(1).broadcast_to([P, NQ, TOPK, TOPK]), ALU.is_equal))
                    link(nc.vector.tensor_tensor(eq[:], eq[:], idxf[:, j].unsqueeze(2).broadcast_to([P, NQ, TOPK, TOPK]),
                                                 ALU.mult))
                    link(nc.vector.reduce_sum(picks[:, j, :, h], eq[:], AX.X))
                dve.wait_ge(exp_done, h + 1)
                link(nc.vector.reduce_sum(gsum[:, 0], gates[:], AX.X))
                link(nc.vector.reciprocal(gsum[:, 1], gsum[:, 0]))
                nc.vector.tensor_tensor(picks[:, 2, :, h], gates[:],
                                        gsum[:, 1].unsqueeze(2).broadcast_to([P, NQ, TOPK]), ALU.mult).then_inc(listed, 1)
                dve.wait_ge(listed, h + 1)

        @block.tensor
        def _(pe):
            pe.wait_ge(loaded, 32)

            def head(h):
                later = not isinstance(h, int) or h > 0
                for b in range(2):
                    pe.wait_ge(w_lo, h * 2 + b + 1)
                    if later:
                        pe.wait_ge(q_out, h * 2)
                    for k in range(KD):
                        mm = matmul3(nc, q_ps[:, b], (wh[:, b, k], wl[:, b, k]), (x2h[:, k], x2l[:, k]), k == 0, k == KD - 1)
                    mm.then_inc(q_done, 1)
                for b in range(2):
                    pe.wait_ge(q_out, h * 2 + b + 1)
                    if later:
                        pe.wait_ge(s_out, h * 2)
                    for i in range(NQ):
                        mm = nc.tensor.matmul(s_ps[:, b, i * NK:i * NK + NK], qT[:, b, i * P:i * P + P], subk[:, b],
                                              start=True, stop=True)
                    mm.then_inc(s_done, 1)
                chunks(pe, h, 0, UPH, lambda m, sl: product(pe, m, sl))
            heads(pe, head)
            pe.wait_ge(listed, PH)
            for j, bank in enumerate((q_ps[:, 0], q_ps[:, 1], s_ps[:, 0])):
                for i in range(NQ):
                    mm = nc.tensor.transpose(bank[:, i * P:i * P + P],
                                             picks[:, j, i].rearrange("p h k -> p (h k)"), keep["ident"][:])
                mm.then_inc(turned, 1)


def gate_matrix(nc, d, keep):
    picksT, G = keep["picksT"], keep["G"]
    TB = 4
    NS = P // TB
    PER = 8
    NT = NQ * NS // PER
    COUNT = 2 * NT
    with ExitStack() as ctx:
        def sb(name, shape, dt=F32):
            return ctx.enter_context(nc.sbuf_tensor("g_" + name, shape, dt))

        def sem(name):
            return ctx.enter_context(nc.semaphore("g_" + name))

        iota = sb("iota128", [P, NK])
        hot1 = sb("hot1", [P, 2, TB, NK])
        hot2 = sb("hot2", [P, 2, TB, NK])
        stage = sb("stage", [P, 2, NK, P])
        ps = ctx.enter_context(nc.psum_tensor("g_ps", [P, 2, TB, NK], F32))
        load, store, split_hi, gelu, split_lo, product, all_stored = keep["hidden"]
        FIRST = NCHUNK - COUNT
        loaded, hot1_made, hot2_made, placed, staged = (sem(n) for n in ("loaded", "hot1_made", "hot2_made", "placed",
                                                                         "staged"))
        g_stored = [sem(f"stage_stored{b}") for b in range(2)]
        TAIL = NCHUNK - 4
        QA = NK // 4
        block = ctx.enter_context(nc.Block())

        def turns(eng, turn):
            turn(0)
            turn(1)
            with eng.Fori(2, NT - 2) as t:
                turn(t)
            turn(NT - 2)
            turn(NT - 1)

        def beside(t):
            return not isinstance(t, int) or FIRST + 2 * t < TAIL

        def later(n, k):
            return not isinstance(n, int) or n >= k

        @block.sync
        def _(sp):
            sp.dma_start(iota[:], d["iota128"]).then_inc(loaded, 16)

            def store_quarter(tile, r):
                sp.wait_ge(staged, NS * (tile + 1))
                a = slice(r * QA, (r + 1) * QA)
                sp.dma_start(G[a, :, tile * P:tile * P + P].rearrange("a b t -> b a t"),
                             stage[:, tile % 2, a]).then_inc(g_stored[tile % 2], 16)

            for t in range(NT):
                tile, r = t // 4, t % 4
                for s in range(2):
                    m = FIRST + 2 * t + s
                    if m + 2 < NCHUNK:
                        load(sp, m + 2, s)
                    if m - 1 < TAIL:
                        store(sp, m - 1, 1 - s)
                if tile >= 1:
                    store_quarter(tile - 1, r)
            for r in range(4):
                store_quarter(NQ - 1, r)
                store(sp, TAIL + r, r % 2)
            all_stored(sp)
            for b in range(2):
                sp.wait_ge(g_stored[b], NQ // 2 * 4 * 16)

        @block.gpsimd
        def _(pool):
            def turn(t):
                for s in range(2):
                    if beside(t):
                        split_lo(pool, t * 2 + (FIRST + s + 1), 1 - s)
            turns(pool, turn)
            for m in range(TAIL + 1, NCHUNK):
                split_lo(pool, m, m % 2)

        @block.vector
        def _(dve):
            dve.wait_ge(loaded, 16)

            def step(n, b):
                if later(n, 2):
                    dve.wait_ge(placed, n - 1)
                nc.vector.tensor_tensor(hot2[:, b], iota[:].unsqueeze(1).broadcast_to([P, TB, NK]),
                                        picksT[:, 1, bass.ds(n * TB, TB)].unsqueeze(2).broadcast_to([P, TB, NK]),
                                        ALU.is_equal).then_inc(hot2_made, 1)
                for t in range(TB):
                    t1 = bass.ds(n * TB + t, 1)
                    nc.vector.tensor_scalar(hot1[:, b, t], iota[:], picksT[:, 0, t1], picksT[:, 2, t1],
                                            ALU.is_equal, ALU.mult).then_inc(hot1_made, 1)
            for n in range(2):
                step(n, n)
            with dve.Fori(2, NQ * NS - 1, 2) as n:
                for b in range(2):
                    step(n + b, b)

        @block.tensor
        def _(pe):
            def turn(t):
                for s in range(2):
                    for i in range(PER // 2):
                        if beside(t):
                            product(pe, t * 2 + (FIRST + s), s, range(i * KD // (PER // 2), (i + 1) * KD // (PER // 2)))
                        n, b = t * PER + s * (PER // 2) + i, i % 2
                        pe.wait_ge(hot1_made, (n + 1) * TB)
                        pe.wait_ge(hot2_made, n + 1)
                        if later(n, 2):
                            pe.wait_ge(staged, n - 1)
                        for j in range(TB):
                            mm = nc.tensor.matmul(ps[:, b, j], hot2[:, b, j], hot1[:, b, j], start=True, stop=True)
                        mm.then_inc(placed, 1)
            turns(pe, turn)
            for m in range(TAIL, NCHUNK):
                product(pe, m, m % 2)

        @block.scalar
        def _(act):
            def turn(t, tile, r):
                for s in range(2):
                    m = t * 2 + (FIRST + s)
                    if beside(t) or (isinstance(m, int) and m == TAIL):
                        split_hi(act, m + 1, 1 - s)
                    if later(m, FIRST + 1) and not (isinstance(m, int) and m > TAIL):
                        gelu(act, m - 1, 1 - s)
                    for i in range(PER // 2):
                        n, b = s * (PER // 2) + i, i % 2
                        act.wait_ge(placed, t * PER + n + 1)
                        nc.scalar.copy(stage[:, tile % 2, :, bass.ds((r * PER + n) * TB, TB)].rearrange("p a t -> p t a"),
                                       ps[:, b]).then_inc(staged, 1)
            for tile in range(NQ):
                t0 = tile * NT // NQ
                if tile >= 2:
                    act.wait_ge(g_stored[tile % 2], 4 * 16 * (tile // 2))
                turn(t0, tile, 0)
                if tile in (0, NQ - 1):
                    turn(t0 + 1, tile, 1)
                if tile == NQ - 1:
                    turn(t0 + 2, tile, 2)
                else:
                    with act.Fori(2 if tile == 0 else 1, 3) as r:
                        turn(t0 + r, tile, r)
                turn(t0 + 3, tile, 3)
            for m in range(TAIL, NCHUNK):
                if TAIL + 1 < m + 1 < NCHUNK:
                    split_hi(act, m + 1, (m + 1) % 2)
                if m > TAIL:
                    gelu(act, m - 1, (m - 1) % 2)
            gelu(act, NCHUNK - 1, (NCHUNK - 1) % 2)


def experts(nc, d, keep):
    acc, G, HID = (keep[n] for n in ("acc", "G", "HID"))
    NG = NCHUNK // GROUP
    NB = 2 * NQ
    with ExitStack() as ctx:
        def sb(name, shape, dt=F32):
            return ctx.enter_context(nc.sbuf_tensor(name, shape, dt))

        def sem(name):
            return ctx.enter_context(nc.semaphore(name))

        vraw = sb("vraw", [P, GROUP, D])
        vh = sb("vh", [P, 2, GROUP, D], F32R)
        vl = sb("vl", [P, 2, GROUP, D], F32R)
        h2 = sb("e_h2", [P, NQ, D])
        gm = sb("gm", [P, GROUP, SEQ])
        hid = sb("e_hid", [P, GROUP, SEQ])
        wh = sb("e_wh", [P, 2, GROUP, SEQ], F32R)
        wl = sb("e_wl", [P, 2, GROUP, SEQ], F32R)
        o_ps = ctx.enter_context(nc.psum_tensor("eo_ps", [P, 8, 512], F32))
        v_in = [sem(f"e_v_arrived{s}") for s in range(GROUP)]
        g_in = [sem(f"e_g_arrived{s}") for s in range(GROUP)]
        acc_moved, v_hi, v_lo, w_done, w_hi, w_lo, v_done, added, added_h2 = (sem("e_" + n) for n in (
            "acc_moved", "v_hi", "v_lo", "w_done", "w_hi", "w_lo", "v_done", "added", "added_h2"))
        block = ctx.enter_context(nc.Block())

        def groups(eng, group):
            group(0, 0)
            group(1, 1)
            with eng.Fori(2, NG - 3, 2) as g:
                group(g, 0)
                group(g + 1, 1)
            group(NG - 2, 0)
            group(NG - 1, 1)

        def isn(g, k):
            return not isinstance(g, int) or g >= k

        @block.sync
        def _(sp):
            def group(g, b):
                for s in range(GROUP):
                    n = g * GROUP + s
                    if isn(g, 1):
                        sp.wait_ge(v_lo, (g - 1) * GROUP + s + 1)
                        sp.wait_ge(w_lo, (g - 1) * GROUP + s + 1)
                    sp.dma_start(vraw[:, s], d["v"][n]).then_inc(v_in[s], 16)
                    sp.dma_start(gm[:, s], G[n]).then_inc(g_in[s], 16)
                    sp.dma_start(hid[:, s], HID[n]).then_inc(g_in[s], 16)
                if isinstance(g, int) and g == 1:
                    sp.dma_start(h2[:], keep["H2"]).then_inc(acc_moved, 16)
            groups(sp, group)
            for i in range(NQ):
                sp.wait_ge(added, (NG - 1) * NB + 2 * i + 2)
                sp.dma_start(d["out"][i * P:i * P + P], acc[:, i]).then_inc(acc_moved, 16)
            sp.wait_ge(acc_moved, 16 + 16 * NQ)

        @block.scalar
        def _(act):
            def group(g, b):
                for s in range(GROUP):
                    n = g * GROUP + s
                    act.wait_ge(v_in[s], (g + 1) * 16)
                    if isn(g, 2):
                        act.wait_ge(v_done, (g - 1) * NB)
                    nc.scalar.copy(vh[:, b, s], vraw[:, s]).then_inc(v_hi, 1)
                    act.wait_ge(w_done, n + 1)
                    nc.scalar.copy(wh[:, b, s], hid[:, s]).then_inc(w_hi, 1)
            groups(act, group)

        @block.gpsimd
        def _(pool):
            def group(g, b):
                for s in range(GROUP):
                    pool.wait_ge(v_hi, g * GROUP + s + 1)
                    nc.gpsimd.tensor_tensor(vl[:, b, s], vraw[:, s], vh[:, b, s].bitcast(F32), ALU.subtract).then_inc(v_lo, 1)
            groups(pool, group)

        @block.vector
        def _(dve):
            def add(g, o):
                dve.wait_ge(v_done, g * NB + o + 1)
                a = acc[:, o // 2, o % 2 * 512:o % 2 * 512 + 512]
                if isinstance(g, int) and g == 0:
                    nc.vector.tensor_copy(a, o_ps[:, o]).then_inc(added, 1)
                else:
                    nc.vector.tensor_tensor(a, o_ps[:, o], a, ALU.add).then_inc(added, 1)

            def group(g, b):
                for s in range(GROUP):
                    n = g * GROUP + s
                    dve.wait_ge(g_in[s], (g + 1) * 32)
                    nc.vector.tensor_tensor(hid[:, s], hid[:, s], gm[:, s], ALU.mult).then_inc(w_done, 1)
                    dve.wait_ge(w_hi, n + 1)
                    nc.vector.tensor_tensor(wl[:, b, s], hid[:, s], wh[:, b, s].bitcast(F32), ALU.subtract).then_inc(w_lo, 1)
                    if isn(g, 2):
                        for o in range(s * NB // GROUP, (s + 1) * NB // GROUP):
                            add(g - 1, o)
                if isinstance(g, int) and g == 1:
                    for o in range(NB):
                        add(0, o)
            groups(dve, group)
            dve.wait_ge(acc_moved, 16)
            dve.wait_ge(added, (NG - 1) * NB)
            for i in range(NQ):
                nc.vector.tensor_tensor(acc[:, i], acc[:, i], h2[:, i], ALU.add).then_inc(added_h2, 1)
            for o in range(NB):
                dve.wait_ge(added_h2, o // 2 + 1)
                add(NG - 1, o)

        @block.tensor
        def _(pe):
            def product(b, s, o):
                i, h = slice(o // 2 * P, o // 2 * P + P), slice(o % 2 * 512, o % 2 * 512 + 512)
                return matmul3(nc, o_ps[:, o], (wh[:, b, s, i], wl[:, b, s, i]), (vh[:, b, s, h], vl[:, b, s, h]),
                               s == 0, s == GROUP - 1)

            def group(g, b):
                if isinstance(g, int) and g == 0:
                    for s in range(GROUP):
                        pe.wait_ge(w_lo, s + 1)
                        pe.wait_ge(v_lo, s + 1)
                        for o in range(NB):
                            mm = product(b, s, o)
                            if s == GROUP - 1:
                                mm.then_inc(v_done, 1)
                    return
                pe.wait_ge(w_lo, (g + 1) * GROUP)
                pe.wait_ge(v_lo, (g + 1) * GROUP)
                for o in range(NB):
                    pe.wait_ge(added, (g - 1) * NB + (o + 1))
                    for s in range(GROUP):
                        mm = product(b, s, o)
                    mm.then_inc(v_done, 1)
            groups(pe, group)


def build(nc, d):
    with ExitStack() as ctx:
        def sb(name, shape, dt=F32):
            return ctx.enter_context(nc.sbuf_tensor(name, shape, dt))
        keep = {}
        for name in CONSTS:
            keep[name] = sb(name, [P, P])
        keep["cols"] = sb("cols", [P, NC_COLS])
        keep["eps"] = sb("eps", [P, 8])
        keep["ms"] = sb("ms", [P, 2, NQ])
        EPS_COLS = [EPS, HD * EPS, GN_EPS, 0.0]
        with nc.Block() as block:
            @block.gpsimd
            def _(pool):
                for i, e in enumerate(EPS_COLS):
                    nc.gpsimd.memset(keep["eps"][:, i:i + 1], e)
        keep["G"] = nc.dram_tensor("G_scratch", (NK, NK, SEQ), F32, kind="Internal").ap()
        keep["HID"] = nc.dram_tensor("HID_scratch", (NCHUNK, P, SEQ), F32, kind="Internal").ap()
        keep["H2"] = nc.dram_tensor("H2_scratch", (P, NQ, D), F32, kind="Internal").ap()
        early = ctx.enter_context(ExitStack())
        keep["zT"] = early.enter_context(nc.sbuf_tensor("zT", [P, NZ, T], F32, side="right"))
        keep["yfT"] = early.enter_context(nc.sbuf_tensor("yfT", [P, NP4, SEQ], F32, side="right"))
        norm_and_project(nc, d, keep)
        fox_attention(nc, d, keep)
        branch = ctx.enter_context(ExitStack())
        with ExitStack() as rwkv:
            for name in ("bonus", "g"):
                keep[name] = rwkv.enter_context(nc.sbuf_tensor("r_" + name, [P, NP4, T], F32, side="right"))
            with ExitStack() as recurrence:
                for name in ("L", "Lx", "kk", "ka"):
                    keep[name] = recurrence.enter_context(nc.sbuf_tensor("r_" + name, [P, NP4, T], F32, side="right"))
                rwkv_inputs(nc, d, keep)
                keep["wb_fox"] = branch.enter_context(nc.sbuf_tensor("wb_fox", [P, NP4, D], F32))
                keep["yT"] = keep["zT"][:, ZQ:ZQ + NP4]
                rwkv_recurrence(nc, d, keep)
            keep["wb_rwkv"] = branch.enter_context(nc.sbuf_tensor("wb_rwkv", [P, NP4, D], F32))
            keep["gated"] = branch.enter_context(nc.sbuf_tensor("gated", [P, KD, SEQ], F32))
            keep["yrT"] = keep["zT"][:, ZK:ZK + NP4, 0:SEQ]
            rwkv_output(nc, d, keep)
        keep["acc"] = early.enter_context(nc.sbuf_tensor("acc", [P, NQ, D], F32, side="right"))
        branches_and_residual(nc, d, keep)
        branch.close()
        with ExitStack() as mid:
            keep["picksT"] = mid.enter_context(nc.sbuf_tensor("picksT", [P, 3, SEQ], F32))
            for name in ("x2h", "x2l"):
                keep[name] = mid.enter_context(nc.sbuf_tensor(name, [P, KD, SEQ], F32R))
            keep["h_ps"] = mid.enter_context(nc.psum_tensor("h_ps", [P, 2, 512], F32))
            keep["hidden"] = hidden_layer(
                nc, d, keep, lambda name, shape, dt=F32: mid.enter_context(nc.sbuf_tensor("h_" + name, shape, dt)),
                lambda name: mid.enter_context(nc.semaphore("h_" + name)))
            queries = mid.enter_context(ExitStack())
            keep["q_wraw"] = queries.enter_context(nc.sbuf_tensor("q_wraw", [P, 2, KD, P], F32))
            keep["q_w_in"] = [mid.enter_context(nc.semaphore(f"q_w_arrived{b}")) for b in range(2)]
            second_norm(nc, d, keep)
            early.close()
            peer_retrieval(nc, d, keep)
            queries.close()
            gate_matrix(nc, d, keep)
        keep["acc"] = sb("acc2", [P, NQ, D])
        experts(nc, d, keep)


def _columns(vectors):
    return np.concatenate([v.reshape(-1, P).T for v in vectors], axis=1)


def layout(x, meta_tokens, norm1_g, w_in, fox_q_norm, fox_k_norm, fox_f_bias,
           rwkv_mu, rwkv_w0, rwkv_w_up, rwkv_a0, rwkv_a_up, rwkv_g_up, rwkv_k_k,
           rwkv_k_a, rwkv_r_k, rwkv_ln_g, rwkv_ln_b, w_branch_fox, w_branch_rwkv,
           w_out, norm2_g, peer_w_q, peer_sub_k1, peer_sub_k2, peer_u, peer_v):
    f = lambda a: np.asarray(a)
    x, meta = f(x)[0], f(meta_tokens)
    z = lambda *s: np.zeros(s, np.float32)
    d = {}
    h = np.concatenate([meta, x], axis=0)
    d["hT"] = h.T.reshape(KD, P, T).transpose(1, 0, 2)
    d["x_tok"] = x.reshape(NQ, P, D).transpose(1, 0, 2)
    w = f(w_in)[0]
    fox, rwkv, gates = w[:, :1544], w[:, 1544:1544 + 1824], w[:, 3368:]
    pad = lambda n: z(D, n)
    wz = np.concatenate([fox[:, :1536], rwkv[:, :1536], rwkv[:, 1536:1664], rwkv[:, 1664:1792],
                         fox[:, 1536:1544], pad(24), rwkv[:, 1792:1824], pad(64), gates], axis=1)
    d["w_z"] = wz.reshape(KD, P, NZ, P).transpose(2, 1, 0, 3)
    mu = f(rwkv_mu)[0]
    mu = np.concatenate([mu[:1792], z(32), mu[1792:1824], z(64)])
    fb = np.concatenate([f(fox_f_bias)[0], z(P - NH)])
    d["cols"] = _columns([f(a)[0].reshape(-1) for a in (
        fox_q_norm, fox_k_norm, rwkv_w0, rwkv_a0, rwkv_k_k, rwkv_k_a, rwkv_r_k, rwkv_ln_g,
        rwkv_ln_b)] + [mu, fb, f(norm1_g)[0], f(norm2_g)[0]])
    d["ident"] = np.eye(P, dtype=np.float32)
    d["blockones"] = np.kron(np.eye(2), np.ones((HD, HD))).astype(np.float32)
    d["ones"] = np.ones((P, P), np.float32)
    d["mask"] = np.where(np.tril(np.ones((P, P), bool)), 0.0, MASKED).astype(np.float32)
    d["wa_up"] = np.concatenate([f(rwkv_w_up)[0], f(rwkv_a_up)[0]])
    gu = f(rwkv_g_up)[0]
    d["g_up"] = np.stack([gu[:P], np.concatenate([z(32, W5), gu[P:], z(64, W5)])], axis=1)
    d["blockmean"] = d["blockones"] / HD
    d["reset"] = np.broadcast_to((np.arange(T) % C != 0).astype(np.float32), (P, T))
    s_, t_ = np.arange(C)[:, None], np.arange(C)[None, :]
    gram = np.concatenate([s_ < t_, s_ <= t_], axis=1).astype(np.float32)
    def both_parities(m):
        o = np.zeros((P,) + m.shape[1:], np.float32)
        o[0:C], o[HD:HD + C] = m, m
        return o
    d["mgram"] = both_parities(np.repeat(gram[:, None], NP4, axis=1))
    lev = [-((s_ // m % 2 == 1) & (t_ // m == s_ // m - 1)).astype(np.float32) for m in LEVELS + [1]]
    d["mlev"] = both_parities(np.stack(lev + [lev[-1].T], axis=1))
    d["eye8"] = both_parities(np.broadcast_to(np.eye(C, dtype=np.float32)[:, None, None], (C, 2, NP4, C)))
    wb = np.stack([f(w_branch_fox)[0], f(w_branch_rwkv)[0]])
    d["w_branch"] = wb.reshape(2, NP4, P, D).transpose(2, 0, 1, 3)
    d["w_out"] = f(w_out)[0].reshape(KD, P, D).transpose(1, 0, 2)
    d["w_q"] = f(peer_w_q)[0].reshape(KD, P, 2 * PH, P).transpose(2, 1, 0, 3)
    d["subk"] = np.stack([f(peer_sub_k1)[0].T, f(peer_sub_k2)[0].T], axis=1)
    d["iota16"] = np.broadcast_to(np.arange(TOPK, dtype=np.float32), (P, TOPK))
    d["iota128"] = np.broadcast_to(np.arange(NK, dtype=np.float32), (P, NK))
    d["u"] = f(peer_u)[0].reshape(NCHUNK, P, KD, P).transpose(0, 3, 2, 1)
    d["v"] = f(peer_v)[0].reshape(NCHUNK, P, D)
    return {k: np.ascontiguousarray(v) for k, v in d.items()}


def kernel(**inputs):
    import concourse.bacc as bacc
    from concourse.bass_utils import run_bass_kernel_spmd as run

    arrays = layout(**inputs)
    nc = bacc.Bacc("TRN2", target_bir_lowering=False, num_devices=1)
    d = {k: nc.dram_tensor(f"in_{k}", v.shape, mybir.dt.from_np(v.dtype), kind="ExternalInput").ap()
         for k, v in arrays.items()}
    d["out"] = nc.dram_tensor("out", (SEQ, D), F32, kind="ExternalOutput").ap()
    build(nc, d)
    r = run(nc, [{f"in_{k}": v for k, v in arrays.items()}], core_ids=[0])
    return r.results[0]["out"].reshape(1, SEQ, D)
```
